# Optimizing a Trainium2 kernel written in Bass

```python
import math
import jax, jax.numpy as jnp
from jax import lax
import numpy as np

D_MODEL = 2048
BATCH = 1
SEQ = 256
DEPTH = 2

HEAD_DIM = 128
N_HEADS_SB = 4
N_HEADS_DIL = 4
D_SB = N_HEADS_SB * HEAD_DIM
D_DIL = N_HEADS_DIL * HEAD_DIM
D_MIX = D_SB + D_DIL
D_IN = 3 * D_MIX
DILATED_CONFIGS = ((128, 1), (512, 4), (2048, 16))
SB_BLOCK = 128
D_FF = 5632
D_FF_EXPERT = 1408
N_EXPERTS = 8
TOP_K = 2
ROPE_THETA = 10000.0
EPS = 1e-6
NEG_INF = -1e30
N_DENSE = (DEPTH + 1) // 2
N_MOE = DEPTH // 2

kernel_name = "hymba_stickbreak_dilated_moe_trunk"

def rmsnorm(x, g):
    x32 = x.astype(jnp.float32)
    y = x32 * lax.rsqrt(jnp.mean(x32 * x32, axis=-1, keepdims=True) + EPS)
    return (y * g.astype(jnp.float32)).astype(x.dtype)

def rope_tables(positions):
    inv = ROPE_THETA ** (-jnp.arange(0, HEAD_DIM, 2, dtype=jnp.float32) / HEAD_DIM)
    ang = positions.astype(jnp.float32)[..., None] * inv
    cos = jnp.concatenate([jnp.cos(ang), jnp.cos(ang)], -1)[:, :, None, :]
    sin = jnp.concatenate([jnp.sin(ang), jnp.sin(ang)], -1)[:, :, None, :]
    return cos, sin

def apply_rope(x, cos, sin):
    x32 = x.astype(jnp.float32)
    x1, x2 = jnp.split(x32, 2, axis=-1)
    rot = jnp.concatenate([-x2, x1], axis=-1)
    return (x32 * cos + rot * sin).astype(x.dtype)

def stick_breaking(q, k, v):
    B, S, H, dh = q.shape
    C = SB_BLOCK
    nb = S // C
    scale = 1.0 / math.sqrt(dh)
    qt = q.astype(jnp.float32).transpose(0, 2, 1, 3) * scale
    kt = k.astype(jnp.float32).transpose(0, 2, 1, 3)
    vt = v.astype(jnp.float32).transpose(0, 2, 1, 3)
    ar = jnp.arange(C)
    incl = (ar[:, None] >= ar[None, :]).astype(jnp.float32)
    strict = ar[:, None] > ar[None, :]
    outs = []
    for n in range(nb):
        qn = qt[:, :, n * C:(n + 1) * C]
        z_d = jnp.einsum('bhtd,bhsd->bhts', qn, kt[:, :, n * C:(n + 1) * C])
        sp_d = jnp.where(strict, jnp.log1p(jnp.exp(z_d)), 0.0)
        r_d = jnp.einsum('bhtj,js->bhts', sp_d, incl)
        a_d = jnp.where(strict, jnp.exp(z_d - r_d), 0.0)
        o = jnp.einsum('bhts,bhsd->bhtd', a_d, vt[:, :, n * C:(n + 1) * C])
        if n > 0:
            ko = kt[:, :, :n * C].reshape(B, H, n, C, dh)
            vo = vt[:, :, :n * C].reshape(B, H, n, C, dh)
            z_o = jnp.einsum('bhtd,bhcsd->bhtcs', qn, ko)
            sp_o = jnp.log1p(jnp.exp(z_o))
            r_o = jnp.einsum('bhtcj,js->bhtcs', sp_o, incl)
            tot = r_o[..., 0]
            later = lax.cumsum(tot, axis=3, reverse=True) - tot + r_d[..., :1]
            a_o = jnp.exp(z_o - r_o - later[..., None])
            o = o + jnp.einsum('bhtcs,bhcsd->bhtd', a_o, vo)
        outs.append(o)
    o = jnp.concatenate(outs, axis=2)
    return o.transpose(0, 2, 1, 3).reshape(B, S, H * dh).astype(q.dtype)

def dilated_branch(q, k, v, steps, dil):
    B, S, H, dh = q.shape
    span = steps * dil
    Sp = -(-S // span) * span
    pad = [(0, 0), (0, Sp - S), (0, 0), (0, 0)]
    L = Sp // dil
    nb = L // steps
    scale = 1.0 / math.sqrt(dh)

    def regroup(t):
        t = jnp.pad(t.astype(jnp.float32), pad)
        return t.reshape(B, L, dil, H, dh).transpose(0, 2, 1, 3, 4).reshape(B, dil, nb, steps, H, dh)

    def with_prev(t):
        prev = jnp.concatenate([jnp.zeros_like(t[:, :, :1]), t[:, :, :-1]], axis=2)
        return jnp.concatenate([prev, t], axis=3)

    qs = regroup(q)
    kk = with_prev(regroup(k))
    vv = with_prev(regroup(v))
    s = jnp.einsum('brnqhd,brnkhd->brnhqk', qs, kk) * scale
    qi = jnp.arange(steps)[:, None]
    ki = jnp.arange(2 * steps)[None, :]
    dist = qi + steps - ki
    band = (dist >= 0) & (dist <= steps)
    has_prev = (jnp.arange(nb)[:, None, None] > 0) | (ki[None] >= steps)
    mask = (band[None] & has_prev)[:, None]
    s = jnp.where(mask, s, NEG_INF)
    m = jnp.max(s, axis=-1, keepdims=True)
    p = jnp.exp(s - m)
    den = jnp.sum(p, axis=-1, keepdims=True)
    o = jnp.einsum('brnhqk,brnkhd->brnqhd', p / den, vv)
    lse = (m + jnp.log(den))[..., 0]
    o = o.reshape(B, dil, L, H, dh).transpose(0, 2, 1, 3, 4).reshape(B, Sp, H, dh)[:, :S]
    lse = lse.transpose(0, 1, 2, 4, 3).reshape(B, dil, L, H).transpose(0, 2, 1, 3).reshape(B, Sp, H)[:, :S]
    return o, lse

def dilated_attention(q, k, v):
    B, S, H, dh = q.shape
    outs, lses = [], []
    for window, dil in DILATED_CONFIGS:
        o, l = dilated_branch(q, k, v, window // dil, dil)
        outs.append(o)
        lses.append(l)
    alpha = jax.nn.softmax(jnp.stack(lses, 0), axis=0)
    o = jnp.einsum('gbsh,gbshd->bshd', alpha, jnp.stack(outs, 0))
    return o.reshape(B, S, H * dh).astype(q.dtype)

def mixer_layer(x, cos, sin, g_norm, w_in, q_norm_sb, k_norm_sb, q_norm_dil, k_norm_dil,
                g_out_sb, g_out_dil, w_out):
    B, S, _ = x.shape
    h = rmsnorm(x, g_norm) @ w_in
    qa, ka, va, qb, kb, vb = jnp.split(
        h, [D_SB, 2 * D_SB, 3 * D_SB, 3 * D_SB + D_DIL, 3 * D_SB + 2 * D_DIL], axis=-1)
    heads = lambda t: t.reshape(B, S, -1, HEAD_DIM)
    o_sb = stick_breaking(rmsnorm(heads(qa), q_norm_sb), rmsnorm(heads(ka), k_norm_sb),
                          heads(va))
    qb = apply_rope(rmsnorm(heads(qb), q_norm_dil), cos, sin)
    kb = apply_rope(rmsnorm(heads(kb), k_norm_dil), cos, sin)
    o_dil = dilated_attention(qb, kb, heads(vb))
    o = jnp.concatenate([rmsnorm(o_sb, g_out_sb), rmsnorm(o_dil, g_out_dil)], axis=-1)
    return x + o @ w_out

def swiglu(x, wg, wu, wd):
    return (jax.nn.silu(x @ wg) * (x @ wu)) @ wd

def moe(xn, w_router, wg, wu, wd):
    B, S, D = xn.shape
    t = xn.reshape(-1, D)
    logits = (t @ w_router).astype(jnp.float32)
    top_vals, top_idx = lax.top_k(logits, TOP_K)
    gates = jax.nn.softmax(top_vals, axis=-1)
    comb = jnp.einsum('nk,nke->ne', gates, jax.nn.one_hot(top_idx, N_EXPERTS, dtype=jnp.float32))
    y = jnp.zeros_like(t)
    for e in range(N_EXPERTS):
        y = y + comb[:, e:e + 1].astype(t.dtype) * swiglu(t, wg[e], wu[e], wd[e])
    return y.reshape(B, S, D)

def setup_inputs(seed: int = 0) -> dict:
    key = jax.random.key(seed)
    ks = jax.random.split(key, 20)
    f32 = jnp.float32
    nrm = lambda k, shape, fan_in: jax.random.normal(k, shape, f32) * fan_in ** -0.5
    gain = lambda k, shape: 1.0 + 0.02 * jax.random.normal(k, shape, f32)
    x = jax.random.normal(ks[0], (BATCH, SEQ, D_MODEL), f32)
    positions = jnp.broadcast_to(jnp.arange(SEQ, dtype=jnp.int32)[None, :], (BATCH, SEQ))
    return {
        "x": x,
        "positions": positions,
        "norm_mix": gain(ks[1], (DEPTH, D_MODEL)),
        "w_in": nrm(ks[2], (DEPTH, D_MODEL, D_IN), D_MODEL),
        "q_norm_sb": gain(ks[3], (DEPTH, HEAD_DIM)),
        "k_norm_sb": gain(ks[4], (DEPTH, HEAD_DIM)),
        "q_norm_dil": gain(ks[5], (DEPTH, HEAD_DIM)),
        "k_norm_dil": gain(ks[6], (DEPTH, HEAD_DIM)),
        "out_norm_sb": gain(ks[7], (DEPTH, D_SB)),
        "out_norm_dil": gain(ks[8], (DEPTH, D_DIL)),
        "w_out": nrm(ks[9], (DEPTH, D_MIX, D_MODEL), D_MIX),
        "norm_ffn": gain(ks[10], (DEPTH, D_MODEL)),
        "w_gate_dense": nrm(ks[11], (N_DENSE, D_MODEL, D_FF), D_MODEL),
        "w_up_dense": nrm(ks[12], (N_DENSE, D_MODEL, D_FF), D_MODEL),
        "w_down_dense": nrm(ks[13], (N_DENSE, D_FF, D_MODEL), D_FF),
        "w_router": nrm(ks[14], (N_MOE, D_MODEL, N_EXPERTS), D_MODEL),
        "w_gate_moe": nrm(ks[15], (N_MOE, N_EXPERTS, D_MODEL, D_FF_EXPERT), D_MODEL),
        "w_up_moe": nrm(ks[16], (N_MOE, N_EXPERTS, D_MODEL, D_FF_EXPERT), D_MODEL),
        "w_down_moe": nrm(ks[17], (N_MOE, N_EXPERTS, D_FF_EXPERT, D_MODEL), D_FF_EXPERT),
    }

def reference(x, positions, norm_mix, w_in, q_norm_sb, k_norm_sb, q_norm_dil, k_norm_dil,
              out_norm_sb, out_norm_dil, w_out, norm_ffn, w_gate_dense, w_up_dense, w_down_dense,
              w_router, w_gate_moe, w_up_moe, w_down_moe):
    cos, sin = rope_tables(positions)
    for i in range(DEPTH):
        x = mixer_layer(x, cos, sin, norm_mix[i], w_in[i], q_norm_sb[i], k_norm_sb[i],
                        q_norm_dil[i], k_norm_dil[i], out_norm_sb[i], out_norm_dil[i], w_out[i])
        xn = rmsnorm(x, norm_ffn[i])
        j = i // 2
        if i % 2 == 0:
            x = x + swiglu(xn, w_gate_dense[j], w_up_dense[j], w_down_dense[j])
        else:
            x = x + moe(xn, w_router[j], w_gate_moe[j], w_up_moe[j], w_down_moe[j])
    return x


_drawn_inputs = setup_inputs


def setup_inputs(seed=0):
    import zlib

    import numpy as np

    out = dict(_drawn_inputs(seed))
    spreads = {}
    factors = {'q_norm_sb': 4.029, 'k_norm_sb': 4.703, 'q_norm_dil': 2.816}
    for name, (base, spread) in spreads.items():
        noise = np.random.default_rng([zlib.crc32(name.encode()), seed]).standard_normal(out[name].shape)
        drawn = base * np.exp(spread * noise) if base else spread * noise
        out[name] = __import__('jax').numpy.asarray(drawn.astype(out[name].dtype))
    for name, factor in factors.items():
        out[name] = (out[name] * factor).astype(out[name].dtype)
    return out
```

```python
from contextlib import ExitStack

import numpy as np
import concourse.bass as bass
from concourse import mybir

F32 = mybir.dt.float32
F32R = mybir.dt.float32r
I32 = mybir.dt.int32
ALU = mybir.AluOpType
ACT = mybir.ActivationFunctionType
AX = mybir.AxisListType

P = 128
SEQ = 256
TILES = SEQ // P
D = 2048
KD = D // P
HEADS = 4
DH = 128
D_MIX = 2 * HEADS * DH
D_IN = 3 * D_MIX
LAYERS = 2
N_EXP = 8
FE = 1408
FC = FE // P
DENSE_SLICES = 4
EPS = 1e-6
BIG = 1e30
EXP_OVERFLOW = 88.72283
SCALE = DH ** -0.5
ROPE_THETA = 10000.0

GB = 352
GBLOCKS = FE // GB
NB = 512
GU_W = 2 * 2 * GB
NB_W = 2 * NB
DN_PIECES = (FC + 1) // 2
RAW = 4
RING = 8

IN_BLOCKS, OUT_BLOCKS, DBLOCKS = D_IN // NB, D // NB, D // NB
IN_PIECES, OUT_PIECES, GU_PIECES = KD // 2, D_MIX // P // 2, KD // 2
SLICE_PIECES = GBLOCKS * GU_PIECES + DBLOCKS * DN_PIECES
SLICE_USED = GBLOCKS * (GU_PIECES - 1) + DBLOCKS * (DN_PIECES - 1)
T_AFTER = [(0, 2), (2, 5), (5, 8), (8, 11)]

TWO_PI_PARTS = (6.28125, 0.0019350051879882812, 3.019916e-07)
ROUND = 12582912.0


def down_width(j):
    return min(2, FC - 2 * j) * NB


def trunk(nc, x, positions, norm_mix, w_in, q_norm_sb, k_norm_sb, q_norm_dil, k_norm_dil, out_norm_sb,
          out_norm_dil, w_out, norm_ffn, gu_dense, down_dense, w_router, gu_moe, down_moe, inv_freq, out):
    FFN = [dict(slices=DENSE_SLICES), dict(slices=N_EXP)]
    n_piece = n_gu = n_dn = n_tp = n_used = 0
    MIX = []
    for layer in range(LAYERS):
        MIX.append(dict(p_in=n_piece, p_out=n_piece + IN_BLOCKS * IN_PIECES, gu=n_gu, dn=n_dn,
                        tp_x=n_tp, tp_o=n_tp + 8, used_in=n_used, used_out=n_used + IN_BLOCKS * (IN_PIECES - 1)))
        n_used += IN_BLOCKS * (IN_PIECES - 1) + OUT_BLOCKS * (OUT_PIECES - 1)
        n_piece += IN_BLOCKS * IN_PIECES + OUT_BLOCKS * OUT_PIECES
        n_gu += IN_BLOCKS * TILES
        n_dn += OUT_BLOCKS * TILES
        n_tp += 12
        f = FFN[layer]
        f.update(piece=n_piece, gu=n_gu, dn=n_dn, tp_x=n_tp, tp=n_tp + 8, used=n_used)
        n_used += f["slices"] * SLICE_USED
        n_piece += f["slices"] * SLICE_PIECES
        n_gu += f["slices"] * GBLOCKS * TILES
        n_dn += f["slices"] * DBLOCKS * TILES
        n_tp += 8 + f["slices"] * GBLOCKS * TILES
    N_PIECES = n_piece

    with ExitStack() as ctx:
        def sb(name, shape, dt=F32, where=ctx):
            return where.enter_context(nc.sbuf_tensor(name, shape, dt))

        def sem(name):
            return ctx.enter_context(nc.semaphore(name))

        RAWS = sb("raw_pieces", [P, RAW, GU_W])
        WH = sb("w_high", [P, RING, GU_W], F32R)
        WL = sb("w_low", [P, RING, GU_W], F32R)
        X = sb("x_resid", [P, TILES, D])
        TOK = sb("token_major", [P, TILES * D_IN])
        HTH = sb("hT_high", [P, FC, SEQ], F32R)
        HTL = sb("hT_low", [P, FC, SEQ], F32R)
        SG = sb("silu_gate", [P, TILES, GB])
        IDN = sb("identity", [P, P])
        INCL = sb("incl", [P, P])
        ONES = sb("ones", [P, P])
        NEGZ = sb("neg_not_strict", [P, P])
        KEEPZ = sb("keep_strict", [P, P])
        CNT = sb("branch_count", [P, 3 * P])
        NEGU = sb("neg_union", [P, 3 * P])
        COS = sb("rope_cos", [P, TILES, DH // 2])
        SIN = sb("rope_sin", [P, TILES, DH // 2])
        WRH = sb("router_high", [P, KD, N_EXP], F32R)
        WRL = sb("router_low", [P, KD, N_EXP], F32R)
        COMB = sb("expert_gates", [P, TILES, N_EXP])
        SMALL = sb("small", [P, 64])
        XN = TOK[:, 0:TILES * D].rearrange("p (t n) -> p t n", t=TILES)
        GAIN = TOK[:, TILES * D:TILES * D + D]
        QKV = TOK[:, :].rearrange("p (t n) -> p t n", t=TILES)
        H = TOK[:, 0:TILES * FE].rearrange("p (t n) -> p t n", t=TILES)
        with ExitStack() as scratch:
            ATT = sb("mixer_scratch", [P, 2 * KD * SEQ], F32, scratch)
        XTH = sb("xT_high", [P, KD, SEQ], F32R)
        XTL = sb("xT_low", [P, KD, SEQ], F32R)

        at = [0]

        def part(n):
            at[0] += n
            return ATT[:, at[0] - n:at[0]]

        ROPE_C = part(2 * TILES * DH).rearrange("p (t q d) -> p t q d", t=TILES, q=2)
        ROPE_S = part(2 * TILES * DH).rearrange("p (t q d) -> p t q d", t=TILES, q=2)
        DIL_G = part(2 * DH).rearrange("p (q d) -> p q d", q=2)
        heads_at = at[0]
        QKT = [[part(4 * P) for _ in range(2)] for _ in range(2)]
        ZS, SPL, SP, AZ, WD, WDT = ([part(3 * P) for _ in range(2)] for _ in range(6))
        at[0] = heads_at
        SQ = part(TILES * D_MIX).rearrange("p (t n) -> p t n", t=TILES)
        RT1, RT2 = part(HEADS * DH), part(HEADS * DH)
        GOUT = ATT[:, 0:D_MIX]
        ANG, TURN, RED = (ATT[:, i * P:(i + 1) * P].rearrange("p (t d) -> p t d", t=TILES) for i in range(3))
        INV = ATT[:, 3 * P:3 * P + DH // 2]
        POS_I = ATT[:, 4 * P:4 * P + TILES].bitcast(I32)
        POS = ATT[:, 4 * P + 4:4 * P + 4 + TILES]
        DIST = ATT[:, 5 * P:8 * P].bitcast(I32)
        DMOD = ATT[:, 8 * P:11 * P].bitcast(I32)
        DF, C1 = ATT[:, 11 * P:14 * P], ATT[:, 14 * P:17 * P]
        SS, RSTD = SMALL[:, 0:2], SMALL[:, 2:4]
        SB_GAIN = SMALL[:, 4:6]
        O_SS, O_RSTD = SMALL[:, 6:10], SMALL[:, 10:14]
        HSS = SMALL[:, 14:46]
        MX, NMX, DEN, RDEN = (SMALL[:, 46 + 4 * i:50 + 4 * i] for i in range(4))
        HSSR = sb("head_rstd", [P, 32])
        LG = sb("logits", [P, TILES, N_EXP])
        RK = sb("rank_terms", [P, 2, N_EXP, N_EXP])
        BEFORE = sb("earlier_expert", [P, N_EXP, N_EXP])
        R1 = sb("router_rows", [P, 4, TILES, N_EXP])

        def bank(name):
            return ctx.enter_context(nc.psum_tensor(name, [P, 512], F32))
        G = [bank("gate0"), bank("gate1")]
        U = [bank("up0"), bank("up1")]
        DN = [bank("down0"), bank("down1")]
        TP = [bank("transpose0"), bank("transpose1")]

        raw_full = [sem(f"raw_full{i}") for i in range(RAW)]
        high_done = sem("high_done")
        low_done = sem("low_done")
        used = sem("piece_used")
        gu_ready = sem("gu_ready")
        gu_free = sem("gu_free")
        silu_done = sem("silu_done")
        dn_ready = sem("dn_ready")
        dn_free = sem("dn_free")
        tp_ready = sem("tp_ready")
        tp_high = sem("tp_high")
        tp_free = sem("tp_free")
        x_in = sem("x_in")
        small_in = sem("small_in")
        gain_in = sem("gain_in")
        gain_used = sem("gain_used")
        router_in = sem("router_in")
        const_done = sem("const_done")
        tables_done = sem("tables_done")
        masks_done = sem("masks_done")
        pool_chain = sem("pool_chain")
        dve_chain = sem("dve_chain")
        act_chain = sem("act_chain")
        rope_red = sem("rope_reduced")
        sq_done = sem("sq_done")
        ms_done = sem("mean_square_done")
        root_done = sem("root_done")
        xn_done = sem("xn_done")
        dilg_in, gout_in, sbg_in = sem("dilg_in"), sem("gout_in"), sem("sbg_in")
        rope_done = sem("rope_done")
        sbg_done = sem("sbg_done")
        qk_t = sem("qk_transposed")
        qk_ev = sem("qk_evacuated")
        z_ready, z_copied, spl_done = sem("z_ready"), sem("z_copied"), sem("spl_done")
        sp_done, r_ready, az_done, a_done = sem("sp_done"), sem("r_ready"), sem("az_done"), sem("a_done")
        osb_ready, osb_done = sem("osb_ready"), sem("osb_done")
        s_ready, s_max, e_done = sem("s_ready"), sem("s_max"), sem("e_done")
        w_done, wt_ready, wt_done = sem("w_done"), sem("wt_ready"), sem("wt_done")
        odil_ready, odil_done = sem("odil_ready"), sem("odil_done")
        osq_done, on_done = sem("osq_done"), sem("on_done")
        wr_high, wr_done = sem("wr_high"), sem("wr_done")
        lg_ready, lg_done, pexp_done, comb_done = sem("lg_ready"), sem("lg_done"), sem("pexp_done"), sem("comb_done")
        stored = sem("stored")

        block = ctx.enter_context(nc.Block())

        def slice_pieces():
            return ([("gu", b, j, GU_W) for b in range(GBLOCKS) for j in range(GU_PIECES)]
                    + [("dn", d, j, down_width(j)) for d in range(DBLOCKS) for j in range(DN_PIECES)])

        WIDTHS = [w for _, _, _, w in slice_pieces()]

        @block.sync
        def _(sp):
            def load(slot, width, src, piece):
                if isinstance(piece, int):
                    if piece >= RAW:
                        sp.wait_ge(low_done, piece - RAW + 1)
                else:
                    sp.wait_ge(low_done, piece - (RAW - 1))
                sp.dma_start(RAWS[:, slot, 0:width], src).then_inc(raw_full[slot], 16)

            sp.dma_start(X[:, :, :], x.rearrange("(t p) n -> p t n", p=P)).then_inc(x_in, 16)
            for layer in range(LAYERS):
                m, f = MIX[layer], FFN[layer]
                for c in range(IN_BLOCKS):
                    for j in range(IN_PIECES):
                        n = m["p_in"] + c * IN_PIECES + j
                        load(n % RAW, NB_W, w_in[layer, c, j], n)
                for d in range(OUT_BLOCKS):
                    for j in range(OUT_PIECES):
                        n = m["p_out"] + d * OUT_PIECES + j
                        load(n % RAW, NB_W, w_out[layer, d, j], n)
                gu, down = (gu_dense, down_dense) if layer == 0 else (gu_moe, down_moe)
                with sp.Fori(0, f["slices"]) as e:
                    for i, (kind, b, j, width) in enumerate(slice_pieces()):
                        if kind == "gu":
                            src = gu[bass.ds(e, 1), b, j].rearrange("o p n -> (o p) n")
                        else:
                            src = down[bass.ds(e, 1), b, :, j * NB_W:j * NB_W + width].rearrange("o p n -> (o p) n")
                        load(i % RAW, width, src, e * SLICE_PIECES + (f["piece"] + i))
            total = 2 + n_dn
            for d in range(DBLOCKS):
                for t in range(TILES):
                    sp.wait_ge(dn_free, total - DBLOCKS * TILES + d * TILES + t + 1)
                    sp.dma_start(out[t * P:(t + 1) * P, d * NB:(d + 1) * NB], X[:, t, d * NB:(d + 1) * NB]).then_inc(stored, 16)
            sp.wait_ge(stored, 16 * DBLOCKS * TILES)

        @block.gpsimd
        def _(pool):
            n = [0]

            def link(ins):
                n[0] += 1
                ins.then_inc(pool_chain, 1)
                pool.wait_ge(pool_chain, n[0])

            pool.dma_start(GAIN, norm_mix[0].partition_broadcast(P)).then_inc(gain_in, 16)
            pool.dma_start(INV, inv_freq.partition_broadcast(P)).then_inc(small_in, 16)
            pool.dma_start(POS_I, positions).then_inc(small_in, 16)
            link(pool.memset(IDN[:, :], 0.0))
            link(pool.affine_select(out=IDN[:, :], in_=IDN[:, :], compare_op=ALU.not_equal, fill=1.0, base=0,
                                    pattern=[[-1, P]], channel_multiplier=1))
            link(pool.memset(ONES[:, :], 1.0))
            link(pool.affine_select(out=INCL[:, :], in_=ONES[:, :], compare_op=ALU.is_ge, fill=0.0, base=0,
                                    pattern=[[-1, P]], channel_multiplier=1))
            link(pool.affine_select(out=KEEPZ[:, :], in_=ONES[:, :], compare_op=ALU.is_gt, fill=0.0, base=0,
                                    pattern=[[1, P]], channel_multiplier=-1))
            link(pool.memset(NEGZ[:, :], 0.0))
            link(pool.affine_select(out=NEGZ[:, :], in_=NEGZ[:, :], compare_op=ALU.is_gt, fill=-BIG, base=0,
                                    pattern=[[1, P]], channel_multiplier=-1))
            link(pool.iota(DIST[:, 0:P], [[-1, P]], base=0, channel_multiplier=1))
            link(pool.iota(DIST[:, P:3 * P], [[-1, 2 * P]], base=P, channel_multiplier=1))
            link(pool.memset(BEFORE[:, :, :], 1.0))
            pool.affine_select(out=BEFORE[:, :, :], in_=BEFORE[:, :, :], compare_op=ALU.is_gt, fill=0.0, base=0,
                               pattern=[[1, N_EXP], [-1, N_EXP]], channel_multiplier=0).then_inc(const_done, 1)
            for layer in range(LAYERS):
                m = MIX[layer]
                pool.wait_ge(gu_ready, m["gu"] + IN_BLOCKS * TILES)
                pool.dma_start(DIL_G[:, 0, :], q_norm_dil[layer].partition_broadcast(P)).then_inc(dilg_in, 16)
                pool.dma_start(DIL_G[:, 1, :], k_norm_dil[layer].partition_broadcast(P)).then_inc(dilg_in, 16)
                if layer:
                    pool.wait_ge(qk_ev, 2 * HEADS * layer)
                pool.dma_start(SB_GAIN[:, 0:1], q_norm_sb[layer].rearrange("(p o) -> p o", o=1)).then_inc(sbg_in, 16)
                pool.dma_start(SB_GAIN[:, 1:2], k_norm_sb[layer].rearrange("(p o) -> p o", o=1)).then_inc(sbg_in, 16)
                pool.wait_ge(rope_done, layer + 1)
                pool.dma_start(GOUT[:, 0:HEADS * DH], out_norm_sb[layer].partition_broadcast(P)).then_inc(gout_in, 16)
                pool.dma_start(GOUT[:, HEADS * DH:], out_norm_dil[layer].partition_broadcast(P)).then_inc(gout_in, 16)
                pool.wait_ge(tp_ready, m["tp_o"] + 4)
                pool.dma_start(GAIN, norm_ffn[layer].partition_broadcast(P)).then_inc(gain_in, 16)
                if layer + 1 < LAYERS:
                    pool.wait_ge(xn_done, TILES * (2 * layer + 2))
                    pool.dma_start(GAIN, norm_mix[layer + 1].partition_broadcast(P)).then_inc(gain_in, 16)
            pool.wait_ge(xn_done, TILES * 2 * LAYERS)
            pool.dma_start(GAIN[:, 0:KD * N_EXP], w_router).then_inc(router_in, 16)
            for s, v in ((gain_in, 16 * 2 * LAYERS), (small_in, 32), (router_in, 16)):
                pool.wait_ge(s, v)

        @block.tensor
        def _(pe):
            def three(out_ap, left, ls, right, rs, first, last):
                (lh, ll), (rh, rl) = left, right
                pe.matmul(out_ap, lh[ls], rh[rs], start=first, stop=False)
                pe.matmul(out_ap, lh[ls], rl[rs], start=False, stop=False)
                return pe.matmul(out_ap, ll[ls], rh[rs], start=False, stop=last)

            def transposes(k, src, chunks):
                for i, c in enumerate(chunks):
                    ins = pe.transpose(TP[k % 2][:, i * P:(i + 1) * P], src[:, c * P:(c + 1) * P], IDN[:, :])
                ins.then_inc(tp_ready, 1)

            def x_transposes(norm, tp):
                for t in range(TILES):
                    pe.wait_ge(xn_done, TILES * norm + t + 1)
                    for q in range(4):
                        k = tp + 4 * t + q
                        if k >= 2:
                            pe.wait_ge(tp_free, k - 1)
                        transposes(k, XN[:, t, :], range(4 * q, 4 * q + 4))

            def project(t, slot0, pieces, chunks, piece0, banks, act, last_tile, shift=0):
                for j in range(pieces):
                    slot = (slot0 + j) % RING
                    if t == 0:
                        pe.wait_ge(low_done, piece0 + (j + 1))
                    k2 = min(2, chunks - 2 * j)
                    for i in range(k2):
                        k = 2 * j + i
                        first, last = k == 0, k == chunks - 1
                        left = [a[:, k, t * P:(t + 1) * P] for a in act]
                        for half in range(2):
                            for n, (b, lo, hi) in enumerate(banks):
                                right = [w[:, slot, i * (GU_W // 2 if len(banks) == 2 else NB) + lo:
                                           i * (GU_W // 2 if len(banks) == 2 else NB) + hi] for w in (WH, WL)]
                                if half == 0:
                                    pe.matmul(b, left[0], right[0], start=first, stop=False)
                                    ins = pe.matmul(b, left[0], right[1], start=False, stop=False)
                                else:
                                    ins = pe.matmul(b, left[1], right[0], start=False, stop=last)
                    if last_tile and j < pieces - 1:
                        ins.then_inc(used, 1)
                return ins

            pe.wait_ge(const_done, 1)
            for layer in range(LAYERS):
                m, f = MIX[layer], FFN[layer]
                x_transposes(2 * layer, m["tp_x"])
                pe.wait_ge(tp_free, m["tp_x"] + 8)
                with pe.Fori(0, IN_BLOCKS) as c:
                    for t in range(TILES):
                        pe.wait_ge(gu_free, c * TILES + (m["gu"] + t + 1))
                        ins = project(t, 0, IN_PIECES, KD, c * IN_PIECES + m["p_in"], [(G[t][:, :], 0, NB)],
                                      (XTH, XTL), t == TILES - 1)
                        ins.then_inc(gu_ready, 1)
                pe.wait_ge(rope_done, layer + 1)
                for h in range(HEADS):
                    n = HEADS * layer + h
                    b = h % 2
                    for kind in range(2):
                        col = 3 * HEADS * DH * kind + h * DH
                        if n:
                            pe.wait_ge(qk_ev, 2 * (n - 1) + kind + 1)
                        for qk in range(2):
                            for t in range(TILES):
                                ins = pe.transpose(TP[kind][:, (2 * qk + t) * P:(2 * qk + t + 1) * P],
                                                   QKV[:, t, col + qk * HEADS * DH:col + qk * HEADS * DH + DH], IDN[:, :])
                        ins.then_inc(qk_t, 1)
                    qs, ks = QKT[0][b][:, 0:2 * P], QKT[0][b][:, 2 * P:4 * P]
                    qd, kd = QKT[1][b][:, 0:2 * P], QKT[1][b][:, 2 * P:4 * P]
                    pe.wait_ge(qk_ev, 2 * n + 1)
                    if n:
                        pe.wait_ge(z_copied, n)
                    pe.matmul(G[0][:, 0:2 * P], ks[:, 0:P], qs, start=True, stop=True)
                    pe.matmul(G[0][:, 2 * P:3 * P], ks[:, P:2 * P], qs[:, P:2 * P], start=True, stop=True).then_inc(z_ready, 1)
                    pe.wait_ge(qk_ev, 2 * n + 2)
                    if n:
                        pe.wait_ge(s_max, n)
                    pe.matmul(U[0][:, 0:P], qd[:, 0:P], kd[:, 0:P], start=True, stop=True)
                    pe.matmul(U[0][:, P:3 * P], qd[:, P:2 * P], kd, start=True, stop=True).then_inc(s_ready, 1)
                    pe.wait_ge(sp_done, n + 1)
                    if n:
                        pe.wait_ge(az_done, n)
                    sp_b = SP[b]
                    pe.matmul(G[1][:, 0:2 * P], INCL[:, :], sp_b[:, 0:2 * P], start=True, stop=False)
                    pe.matmul(G[1][:, P:2 * P], ONES[:, :], sp_b[:, 2 * P:3 * P], start=False, stop=True)
                    pe.matmul(G[1][:, 2 * P:3 * P], INCL[:, :], sp_b[:, 2 * P:3 * P], start=True, stop=True).then_inc(r_ready, 1)
                    pe.wait_ge(w_done, n + 1)
                    if n:
                        pe.wait_ge(wt_done, n)
                    for i in range(3):
                        ins = pe.transpose(U[1][:, i * P:(i + 1) * P], WD[b][:, i * P:(i + 1) * P], IDN[:, :])
                    ins.then_inc(wt_ready, 1)
                    for w, bnk, done, free, ready, kind in ((AZ[b], DN[0], a_done, osb_done, osb_ready, 0),
                                                            (WDT[b], DN[1], wt_done, odil_done, odil_ready, 1)):
                        v = 3 * HEADS * DH * kind + 2 * HEADS * DH + h * DH
                        pe.wait_ge(done, n + 1)
                        if n:
                            pe.wait_ge(free, n)
                        pe.matmul(bnk[:, 0:P], w[:, 0:P], QKV[:, 0, v:v + DH], start=True, stop=True)
                        pe.matmul(bnk[:, P:2 * P], w[:, P:2 * P], QKV[:, 0, v:v + DH], start=True, stop=False)
                        pe.matmul(bnk[:, P:2 * P], w[:, 2 * P:3 * P], QKV[:, 1, v:v + DH], start=False, stop=True).then_inc(ready, 1)
                for t in range(TILES):
                    for kind in range(2):
                        k = m["tp_o"] + 2 * t + kind
                        pe.wait_ge(on_done, 2 * TILES * layer + 2 * t + kind + 1)
                        pe.wait_ge(tp_free, k - 1)
                        transposes(k, QKV[:, t, 3 * HEADS * DH * kind:], range(HEADS))
                pe.wait_ge(tp_free, m["tp_o"] + 4)
                for d in range(OUT_BLOCKS):
                    for t in range(TILES):
                        n = m["dn"] + TILES * d + t
                        pe.wait_ge(dn_free, n + 1)
                        ins = project(t, d * OUT_PIECES, OUT_PIECES, D_MIX // P, m["p_out"] + d * OUT_PIECES,
                                      [(DN[t][:, :], 0, NB)], (HTH, HTL), t == TILES - 1)
                        ins.then_inc(dn_ready, 1)
                x_transposes(2 * layer + 1, f["tp_x"])
                pe.wait_ge(tp_free, f["tp_x"] + 8)
                if layer == 1:
                    pe.wait_ge(wr_done, 1)
                    for t in range(TILES):
                        for k in range(KD):
                            ts = (slice(None), k, slice(t * P, (t + 1) * P))
                            ins = three(DN[0][:, t * N_EXP:(t + 1) * N_EXP], (XTH, XTL), ts, (WRH, WRL),
                                        (slice(None), k, slice(None)), k == 0, k == KD - 1)
                    ins.then_inc(lg_ready, 1)
                    pe.wait_ge(lg_done, 1)

                def ffn_slice(e):
                    def gate_up(b, t):
                        pe.wait_ge(gu_free, e * (GBLOCKS * TILES) + (f["gu"] + b * TILES + t + 1))
                        ins = project(t, b * GU_PIECES, GU_PIECES, KD, e * SLICE_PIECES + (f["piece"] + b * GU_PIECES),
                                      [(G[t][:, 0:GB], 0, GB), (U[t][:, 0:GB], GB, 2 * GB)], (XTH, XTL), t == TILES - 1)
                        ins.then_inc(gu_ready, 1)

                    def h_transposes(b, t):
                        k = b * TILES + t
                        pe.wait_ge(gu_free, e * (GBLOCKS * TILES) + (f["gu"] + k + 3))
                        pe.wait_ge(tp_free, e * (GBLOCKS * TILES) + (f["tp"] + k - 1))
                        transposes(f["tp"] + k, H[:, t, :], range(*T_AFTER[b]))

                    def down(d, t):
                        k = e * (DBLOCKS * TILES) + (f["dn"] + d * TILES + t)
                        pe.wait_ge(dn_free, k + 1)
                        if d == 0:
                            pe.wait_ge(tp_free, e * (GBLOCKS * TILES) + (f["tp"] + (GBLOCKS - 1) * TILES + t + 1))
                        ins = project(t, GBLOCKS * GU_PIECES + d * DN_PIECES, DN_PIECES, FC,
                                      e * SLICE_PIECES + (f["piece"] + GBLOCKS * GU_PIECES + d * DN_PIECES),
                                      [(DN[t][:, :], 0, NB)], (HTH, HTL), t == TILES - 1)
                        ins.then_inc(dn_ready, 1)

                    for b in range(GBLOCKS):
                        gate_up(b, 0)
                        if b:
                            h_transposes(b - 1, 1)
                        gate_up(b, 1)
                        h_transposes(b, 0)
                    down(0, 0)
                    h_transposes(GBLOCKS - 1, 1)
                    for d in range(DBLOCKS):
                        if d:
                            down(d, 0)
                        down(d, 1)

                with pe.Fori(0, f["slices"]) as e:
                    ffn_slice(e)

        @block.scalar
        def _(act):
            n_link = [0]

            def link(ins):
                n_link[0] += 1
                ins.then_inc(act_chain, 1)
                act.wait_ge(act_chain, n_link[0])

            def high_ahead(i, width, piece, shift=0):
                act.wait_ge(raw_full[i % RAW], shift * (16 // RAW) + 16 * (piece // RAW + 1))
                act.activation(WH[:, i % RING, 0:width], RAWS[:, i % RAW, 0:width], ACT.Copy).then_inc(high_done, 1)

            def squares(norm):
                for t in range(TILES):
                    act.activation(XN[:, t, :], X[:, t, :], ACT.Square, accum_out=SS[:, t:t + 1]).then_inc(sq_done, 1)

            def x_high(k, t, q):
                act.wait_ge(tp_ready, k + 1)
                act.activation(XTH[:, 4 * q:4 * q + 4, t * P:(t + 1) * P], TP[k % 2][:, :].rearrange("p (c n) -> p c n", c=4),
                               ACT.Copy).then_inc(tp_high, 1)

            def roots(which, n):
                act.wait_ge(ms_done, n + 1)
                act.activation(which, which, ACT.Sqrt).then_inc(root_done, 1)

            act.sem_inc(gu_free, 2)
            act.sem_inc(dn_free, 2)
            act.wait_ge(x_in, 16)
            act.wait_ge(gain_in, 16)
            squares(0)
            roots(RSTD, 0)
            act.wait_ge(rope_red, 1)
            act.activation(SIN[:, :, :], RED, ACT.Sin).then_inc(tables_done, 1)
            act.wait_ge(rope_red, 2)
            act.activation(COS[:, :, :], TURN, ACT.Sin).then_inc(tables_done, 1)
            act.wait_ge(tables_done, 2)
            act.wait_ge(masks_done, 1)
            for layer in range(LAYERS):
                m, f = MIX[layer], FFN[layer]
                for k in range(8):
                    x_high(m["tp_x"] + k, k // 4, k % 4)
                    if layer == 0:
                        high_ahead(k, NB_W, k)
                with act.Fori(0, IN_BLOCKS) as c:
                    for t in range(TILES):
                        if t == TILES - 1:
                            for j in range(IN_PIECES - 1):
                                act.wait_ge(used, c * (IN_PIECES - 1) + (m["used_in"] + j + 1))
                                high_ahead(j, NB_W, m["p_in"] + j + RING, c * IN_PIECES)
                        act.wait_ge(gu_ready, c * TILES + (m["gu"] + t + 1))
                        if t == TILES - 1:
                            high_ahead(IN_PIECES - 1, NB_W, m["p_in"] + IN_PIECES - 1 + RING, c * IN_PIECES)
                        act.activation(TOK[:, bass.ds(c * NB + t * D_IN, NB)], G[t][:, :], ACT.Copy).then_inc(gu_free, 1)
                roots(HSSR[:, :], 4 * layer + 1)
                act.wait_ge(sbg_done, layer + 1)
                for h in range(HEADS):
                    n = HEADS * layer + h
                    b = h % 2
                    act.wait_ge(qk_t, 2 * n + 1)
                    if h >= 2:
                        act.wait_ge(z_ready, n - 1)
                        act.wait_ge(s_ready, n - 1)
                    act.activation(QKT[0][b][:, 0:2 * P], TP[0][:, 0:2 * P], ACT.Copy, scale=SB_GAIN[:, 0:1])
                    act.activation(QKT[0][b][:, 2 * P:4 * P], TP[0][:, 2 * P:4 * P], ACT.Copy,
                                   scale=SB_GAIN[:, 1:2]).then_inc(qk_ev, 1)
                    act.wait_ge(qk_t, 2 * n + 2)
                    act.activation(QKT[1][b], TP[1][:, :], ACT.Copy).then_inc(qk_ev, 1)
                    act.wait_ge(z_ready, n + 1)
                    if h >= 2:
                        act.wait_ge(az_done, n - 1)
                    act.activation(ZS[b], G[0][:, 0:3 * P], ACT.Copy).then_inc(z_copied, 1)
                    link(act.activation(SPL[b], G[0][:, 0:3 * P], ACT.Abs))
                    link(act.activation(SPL[b], SPL[b], ACT.Exp, scale=-1.0))
                    act.activation(SPL[b], SPL[b], ACT.Ln, bias=1.0).then_inc(spl_done, 1)
                    act.wait_ge(s_max, n + 1)
                    act.activation(WD[b][:, 0:P], WD[b][:, 0:P], ACT.Exp, bias=NMX[:, 2 * b:2 * b + 1], scale=SCALE)
                    act.activation(WD[b][:, P:3 * P], WD[b][:, P:3 * P], ACT.Exp, bias=NMX[:, 2 * b + 1:2 * b + 2],
                                   scale=SCALE).then_inc(e_done, 1)
                    act.wait_ge(az_done, n + 1)
                    act.activation(AZ[b], AZ[b], ACT.Exp).then_inc(a_done, 1)
                    act.wait_ge(wt_ready, n + 1)
                    if h >= 2:
                        act.wait_ge(odil_ready, n - 1)
                    act.activation(WDT[b], U[1][:, 0:3 * P], ACT.Copy).then_inc(wt_done, 1)
                    act.wait_ge(osb_ready, n + 1)
                    act.activation(QKV[:, :, h * DH:(h + 1) * DH], DN[0][:, 0:2 * P].rearrange("p (t d) -> p t d", t=TILES),
                                   ACT.Copy).then_inc(osb_done, 1)
                    act.wait_ge(odil_ready, n + 1)
                    for t in range(TILES):
                        ins = act.activation(QKV[:, t, 3 * HEADS * DH + h * DH:3 * HEADS * DH + (h + 1) * DH],
                                             DN[1][:, t * P:(t + 1) * P], ACT.Copy, scale=RDEN[:, 2 * b + t:2 * b + t + 1])
                    ins.then_inc(odil_done, 1)
                act.wait_ge(odil_done, HEADS * (layer + 1))
                act.wait_ge(osb_done, HEADS * (layer + 1))
                for t in range(TILES):
                    for kind in range(2):
                        act.activation(ATT[:, heads_at:heads_at + HEADS * DH], QKV[:, t, 3 * HEADS * DH * kind:3 * HEADS * DH * kind + HEADS * DH],
                                       ACT.Square, accum_out=O_SS[:, 2 * t + kind:2 * t + kind + 1]).then_inc(osq_done, 1)
                        act.wait_ge(osq_done, 2 * TILES * layer + 2 * t + kind + 1)
                roots(O_RSTD, 4 * layer + 2)
                for t in range(TILES):
                    for kind in range(2):
                        k = m["tp_o"] + 2 * t + kind
                        act.wait_ge(tp_ready, k + 1)
                        act.activation(HTH[:, HEADS * kind:HEADS * (kind + 1), t * P:(t + 1) * P],
                                       TP[k % 2][:, :].rearrange("p (c n) -> p c n", c=4), ACT.Copy).then_inc(tp_high, 1)
                for d in range(OUT_BLOCKS):
                    for j in range(OUT_PIECES):
                        i = d * OUT_PIECES + j
                        if j < OUT_PIECES - 1:
                            act.wait_ge(used, m["used_out"] + d * (OUT_PIECES - 1) + j + 1)
                        else:
                            act.wait_ge(dn_ready, m["dn"] + TILES * (d + 1))
                        high_ahead(i, NB_W if i + RING < OUT_BLOCKS * OUT_PIECES else GU_W, m["p_out"] + i + RING)
                act.wait_ge(dn_free, 2 + m["dn"] + OUT_BLOCKS * TILES)
                act.wait_ge(gain_in, 16 * (2 * layer + 2))
                squares(2 * layer + 1)
                roots(RSTD, 4 * layer + 3)
                if layer == 1:
                    act.wait_ge(router_in, 16)
                    act.activation(WRH[:, :, :], GAIN[:, 0:KD * N_EXP].rearrange("p (k e) -> p k e", k=KD), ACT.Copy).then_inc(wr_high, 1)
                for k in range(8):
                    x_high(f["tp_x"] + k, k // 4, k % 4)
                if layer == 1:
                    act.wait_ge(lg_done, 2)
                    for t in range(TILES):
                        ins = act.activation(R1[:, 0, t, :], R1[:, 1, t, :], ACT.Exp)
                    ins.then_inc(pexp_done, 1)

                def ffn_slice(e, last):
                    def ahead(i, semaphore, count):
                        k = i + RING
                        if k >= SLICE_PIECES and last:
                            return
                        act.wait_ge(semaphore, count)
                        high_ahead(i, WIDTHS[k % SLICE_PIECES], f["piece"] + k, e * SLICE_PIECES)

                    def gate_up(b, t):
                        if t == TILES - 1:
                            for j in range(GU_PIECES - 1):
                                ahead(b * GU_PIECES + j, used, e * SLICE_USED + (f["used"] + b * (GU_PIECES - 1) + j + 1))
                        act.wait_ge(gu_ready, e * (GBLOCKS * TILES) + (f["gu"] + b * TILES + t + 1))
                        act.activation(SG[:, t, :], G[t][:, 0:GB], ACT.Silu).then_inc(silu_done, 1)
                        if t == TILES - 1:
                            ahead(b * GU_PIECES + GU_PIECES - 1, gu_ready,
                                  e * (GBLOCKS * TILES) + (f["gu"] + b * TILES + t + 1))

                    def h_high(b, t):
                        k = b * TILES + t
                        c0, c1 = T_AFTER[b]
                        act.wait_ge(tp_ready, e * (GBLOCKS * TILES) + (f["tp"] + k + 1))
                        act.activation(HTH[:, c0:c1, t * P:(t + 1) * P],
                                       TP[(f["tp"] + k) % 2][:, 0:(c1 - c0) * P].rearrange("p (c n) -> p c n", n=P),
                                       ACT.Copy).then_inc(tp_high, 1)

                    for b in range(GBLOCKS):
                        gate_up(b, 0)
                        if b:
                            h_high(b - 1, 1)
                        gate_up(b, 1)
                        h_high(b, 0)
                    h_high(GBLOCKS - 1, 1)
                    for d in range(DBLOCKS):
                        for j in range(DN_PIECES - 1):
                            ahead(GBLOCKS * GU_PIECES + d * DN_PIECES + j, used,
                                  e * SLICE_USED + (f["used"] + GBLOCKS * (GU_PIECES - 1) + d * (DN_PIECES - 1) + j + 1))
                        ahead(GBLOCKS * GU_PIECES + (d + 1) * DN_PIECES - 1, dn_ready,
                              e * (DBLOCKS * TILES) + (f["dn"] + TILES * (d + 1)))

                if layer + 1 < LAYERS:
                    with act.Fori(0, f["slices"]) as e:
                        ffn_slice(e, False)
                    act.wait_ge(dn_free, 2 + f["dn"] + f["slices"] * DBLOCKS * TILES)
                    act.wait_ge(tp_ready, f["tp"] + f["slices"] * GBLOCKS * TILES)
                    squares(2 * layer + 2)
                    roots(RSTD, 4 * layer + 4)
                else:
                    with act.Fori(0, f["slices"] - 1) as e:
                        ffn_slice(e, False)
                    ffn_slice(f["slices"] - 1, True)

        @block.vector
        def _(dve):
            n_link = [0]

            def link(ins):
                n_link[0] += 1
                ins.then_inc(dve_chain, 1)
                dve.wait_ge(dve_chain, n_link[0])

            def low(i, width, piece, shift=None):
                dve.wait_ge(high_done, piece + 1 if shift is None else shift + (piece + 1))
                dve.tensor_tensor(WL[:, i % RING, 0:width], RAWS[:, i % RAW, 0:width], WH[:, i % RING, 0:width],
                                  ALU.subtract).then_inc(low_done, 1)

            def inverse_roots(dst, sums, count, n):
                dve.tensor_scalar(dst, sums, 1.0 / count, EPS, ALU.mult, ALU.add).then_inc(ms_done, 1)
                dve.wait_ge(root_done, n + 1)
                link(dve.reciprocal(dst, dst))

            def normalise(norm):
                dve.wait_ge(sq_done, TILES * (norm + 1))
                dve.wait_ge(gain_in, 16 * (norm + 1))
                inverse_roots(RSTD, SS, D, 4 * (norm // 2) + 3 * (norm % 2))
                for t in range(TILES):
                    dve.scalar_tensor_tensor(out=XN[:, t, :], in0=X[:, t, :], scalar=RSTD[:, t:t + 1], in1=GAIN,
                                             op0=ALU.mult, op1=ALU.mult).then_inc(xn_done, 1)

            def x_low(k, t, q):
                dve.wait_ge(tp_high, k + 1)
                dst = (slice(None), slice(4 * q, 4 * q + 4), slice(t * P, (t + 1) * P))
                dve.tensor_tensor(XTL[dst], TP[k % 2][:, :].rearrange("p (c n) -> p c n", c=4), XTH[dst],
                                  ALU.subtract).then_inc(tp_free, 1)

            normalise(0)
            dve.wait_ge(small_in, 32)
            link(dve.tensor_copy(POS, POS_I))
            for t in range(TILES):
                link(dve.tensor_scalar(ANG[:, t, :], INV, POS[:, t:t + 1], None, ALU.mult))
            link(dve.tensor_scalar(TURN, ANG, 1.0 / (2.0 * np.pi), ROUND, ALU.mult, ALU.add))
            link(dve.tensor_scalar(TURN, TURN, -ROUND, None, ALU.add))
            link(dve.scalar_tensor_tensor(out=RED, in0=TURN, scalar=-TWO_PI_PARTS[0], in1=ANG, op0=ALU.mult, op1=ALU.add))
            link(dve.scalar_tensor_tensor(out=RED, in0=TURN, scalar=-TWO_PI_PARTS[1], in1=RED, op0=ALU.mult, op1=ALU.add))
            link(dve.scalar_tensor_tensor(out=RED, in0=TURN, scalar=-TWO_PI_PARTS[2], in1=RED, op0=ALU.mult, op1=ALU.add))
            link(dve.tensor_scalar(RED, RED, 3.1415925, -3.1415925, ALU.min, ALU.max))
            link(dve.scalar_tensor_tensor(out=TURN, in0=RED, scalar=-1.0, in1=RED, op0=ALU.mult, op1=ALU.max))
            dve.sem_inc(rope_red, 1)
            dve.tensor_scalar(TURN, TURN, -1.0, np.pi / 2, ALU.mult, ALU.add).then_inc(rope_red, 1)
            dve.wait_ge(const_done, 1)
            link(dve.tensor_copy(DF, DIST))
            link(dve.tensor_scalar(CNT[:, :], DF, 128.5, None, ALU.is_lt))
            for dil in (4, 16):
                link(dve.tensor_scalar(DMOD, DIST, dil - 1, None, ALU.bitwise_and))
                link(dve.tensor_scalar(C1, DMOD, 0, None, ALU.is_equal))
                link(dve.tensor_tensor(CNT[:, :], CNT[:, :], C1, ALU.add))
            link(dve.scalar_tensor_tensor(out=CNT[:, :], in0=DF, scalar=-0.5, in1=CNT[:, :], op0=ALU.is_gt, op1=ALU.mult))
            dve.tensor_scalar(NEGU[:, :], CNT[:, :], 0.5, -BIG, ALU.is_lt, ALU.mult).then_inc(masks_done, 1)
            dve.wait_ge(tables_done, 2)

            for layer in range(LAYERS):
                m, f = MIX[layer], FFN[layer]
                for k in range(8):
                    x_low(m["tp_x"] + k, k // 4, k % 4)
                    if layer == 0:
                        low(k, NB_W, k)
                with dve.Fori(0, IN_BLOCKS) as c:
                    for j in range(IN_PIECES):
                        low(j, NB_W, m["p_in"] + j + RING, c * IN_PIECES)
                dve.wait_ge(gu_free, 2 + m["gu"] + IN_BLOCKS * TILES)
                dve.wait_ge(dilg_in, 32 * (layer + 1))
                for qk in range(2):
                    for t in range(TILES):
                        lo, hi = slice(0, DH // 2), slice(DH // 2, DH)
                        g = DIL_G[:, qk, :]
                        dve.tensor_tensor(ROPE_C[:, t, qk, lo], g[:, lo], COS[:, t, :], ALU.mult)
                        dve.tensor_tensor(ROPE_C[:, t, qk, hi], g[:, hi], COS[:, t, :], ALU.mult)
                        dve.scalar_tensor_tensor(out=ROPE_S[:, t, qk, lo], in0=g[:, hi], scalar=-1.0, in1=SIN[:, t, :],
                                                 op0=ALU.mult, op1=ALU.mult)
                        link(dve.tensor_tensor(ROPE_S[:, t, qk, hi], g[:, lo], SIN[:, t, :], ALU.mult))
                dve.wait_ge(sbg_in, 32 * (layer + 1))
                dve.tensor_scalar(SB_GAIN[:, 0:1], SB_GAIN[:, 0:1], SCALE, None, ALU.mult).then_inc(sbg_done, 1)
                for kind in range(2):
                    c0 = 3 * HEADS * DH * kind
                    qk_cols = QKV[:, :, c0:c0 + 2 * HEADS * DH]
                    link(dve.tensor_tensor(SQ, qk_cols, qk_cols, ALU.mult))
                    link(dve.tensor_reduce(HSS[:, 16 * kind:16 * kind + 16], SQ.rearrange("p t (h d) -> p (t h) d", d=DH),
                                           AX.X, ALU.add))
                inverse_roots(HSSR[:, :], HSS, DH, 4 * layer + 1)
                for kind in range(2):
                    c0 = 3 * HEADS * DH * kind
                    rs = HSSR[:, 16 * kind:16 * kind + 16]
                    for t in range(TILES):
                        v = QKV[:, t, c0:c0 + 2 * HEADS * DH].rearrange("p (h d) -> p h d", d=DH)
                        link(dve.tensor_tensor(v, v, rs[:, 8 * t:8 * t + 8].unsqueeze(2).to_broadcast([P, 8, DH]), ALU.mult))
                for t in range(TILES):
                    for qk in range(2):
                        c0 = 3 * HEADS * DH + qk * HEADS * DH
                        v = QKV[:, t, c0:c0 + HEADS * DH].rearrange("p (h d) -> p h d", d=DH)
                        t1 = RT1.rearrange("p (h d) -> p h d", d=DH)
                        t2 = RT2.rearrange("p (h d) -> p h d", d=DH)
                        half = DH // 2
                        bc = [P, HEADS, half]
                        dve.tensor_tensor(t1, v, ROPE_C[:, t, qk, :].unsqueeze(1).to_broadcast([P, HEADS, DH]), ALU.mult)
                        dve.tensor_tensor(t2[:, :, 0:half], v[:, :, half:DH],
                                          ROPE_S[:, t, qk, 0:half].unsqueeze(1).to_broadcast(bc), ALU.mult)
                        link(dve.tensor_tensor(t2[:, :, half:DH], v[:, :, 0:half],
                                               ROPE_S[:, t, qk, half:DH].unsqueeze(1).to_broadcast(bc), ALU.mult))
                        link(dve.tensor_tensor(v, t1, t2, ALU.add))
                dve.sem_inc(rope_done, 1)
                for h in range(HEADS):
                    n = HEADS * layer + h
                    b = h % 2
                    dve.wait_ge(s_ready, n + 1)
                    link(dve.tensor_tensor(WD[b], U[0][:, 0:3 * P], NEGU[:, :], ALU.add))
                    dve.tensor_reduce(MX[:, 2 * b:2 * b + 1], WD[b][:, 0:P], AX.X, ALU.max)
                    link(dve.tensor_reduce(MX[:, 2 * b + 1:2 * b + 2], WD[b][:, P:3 * P], AX.X, ALU.max))
                    dve.tensor_scalar(NMX[:, 2 * b:2 * b + 2], MX[:, 2 * b:2 * b + 2], -SCALE, None, ALU.mult).then_inc(s_max, 1)
                    dve.wait_ge(spl_done, n + 1)
                    link(dve.scalar_tensor_tensor(out=SP[b], in0=ZS[b], scalar=0.0, in1=SPL[b], op0=ALU.max, op1=ALU.add))
                    link(dve.tensor_scalar(AZ[b], ZS[b], EXP_OVERFLOW, BIG, ALU.is_gt, ALU.mult))
                    link(dve.tensor_tensor(SP[b], SP[b], AZ[b], ALU.add))
                    dve.tensor_tensor(SP[b][:, 0:P], SP[b][:, 0:P], KEEPZ[:, :], ALU.mult)
                    dve.tensor_tensor(SP[b][:, 2 * P:3 * P], SP[b][:, 2 * P:3 * P], KEEPZ[:, :], ALU.mult).then_inc(sp_done, 1)
                    dve.wait_ge(e_done, n + 1)
                    dve.tensor_tensor(WD[b][:, 0:3 * P], WD[b][:, 0:3 * P], CNT[:, :], ALU.mult).then_inc(w_done, 1)
                    dve.wait_ge(w_done, n + 1)
                    dve.tensor_reduce(DEN[:, 2 * b:2 * b + 1], WD[b][:, 0:P], AX.X, ALU.add)
                    link(dve.tensor_reduce(DEN[:, 2 * b + 1:2 * b + 2], WD[b][:, P:3 * P], AX.X, ALU.add))
                    link(dve.reciprocal(RDEN[:, 2 * b:2 * b + 2], DEN[:, 2 * b:2 * b + 2]))
                    dve.wait_ge(r_ready, n + 1)
                    link(dve.tensor_tensor(AZ[b], ZS[b], G[1][:, 0:3 * P], ALU.subtract))
                    dve.tensor_tensor(AZ[b][:, 0:P], AZ[b][:, 0:P], NEGZ[:, :], ALU.add)
                    dve.tensor_tensor(AZ[b][:, 2 * P:3 * P], AZ[b][:, 2 * P:3 * P], NEGZ[:, :], ALU.add).then_inc(az_done, 1)
                dve.wait_ge(osq_done, 2 * TILES * (layer + 1))
                dve.wait_ge(gout_in, 32 * (layer + 1))
                inverse_roots(O_RSTD, O_SS, HEADS * DH, 4 * layer + 2)
                for t in range(TILES):
                    for kind in range(2):
                        o = QKV[:, t, 3 * HEADS * DH * kind:3 * HEADS * DH * kind + HEADS * DH]
                        dve.scalar_tensor_tensor(out=o, in0=o, scalar=O_RSTD[:, 2 * t + kind:2 * t + kind + 1],
                                                 in1=GOUT[:, kind * HEADS * DH:(kind + 1) * HEADS * DH],
                                                 op0=ALU.mult, op1=ALU.mult).then_inc(on_done, 1)
                for t in range(TILES):
                    for kind in range(2):
                        k = m["tp_o"] + 2 * t + kind
                        dve.wait_ge(tp_high, k + 1)
                        dst = (slice(None), slice(HEADS * kind, HEADS * (kind + 1)), slice(t * P, (t + 1) * P))
                        dve.tensor_tensor(HTL[dst], TP[k % 2][:, :].rearrange("p (c n) -> p c n", c=4), HTH[dst],
                                          ALU.subtract).then_inc(tp_free, 1)

                def add_down(d, t, k, gate):
                    dve.wait_ge(dn_ready, k + 1)
                    xs = X[:, t, d * NB:(d + 1) * NB]
                    if gate is None:
                        dve.tensor_tensor(xs, DN[t][:, :], xs, ALU.add).then_inc(dn_free, 1)
                    else:
                        dve.scalar_tensor_tensor(out=xs, in0=DN[t][:, :], scalar=gate, in1=xs, op0=ALU.mult,
                                                 op1=ALU.add).then_inc(dn_free, 1)

                for d in range(OUT_BLOCKS):
                    add_down(d, 0, m["dn"] + TILES * d, None)
                    for j in range(OUT_PIECES):
                        i = d * OUT_PIECES + j
                        low(i, NB_W if i + RING < OUT_BLOCKS * OUT_PIECES else GU_W, m["p_out"] + i + RING)
                    add_down(d, 1, m["dn"] + TILES * d + 1, None)
                normalise(2 * layer + 1)
                if layer == 1:
                    dve.wait_ge(wr_high, 1)
                    dve.tensor_tensor(WRL[:, :, :], GAIN[:, 0:KD * N_EXP].rearrange("p (k e) -> p k e", k=KD), WRH[:, :, :],
                                      ALU.subtract).then_inc(wr_done, 1)
                for k in range(8):
                    x_low(f["tp_x"] + k, k // 4, k % 4)
                if layer == 1:
                    dve.wait_ge(lg_ready, 1)
                    dve.tensor_copy(LG[:, :, :], DN[0][:, 0:TILES * N_EXP].rearrange("p (t e) -> p t e", t=TILES)).then_inc(lg_done, 1)
                    dve.wait_ge(lg_done, 1)
                    top, sel, rank = R1[:, 2, 0, 0:TILES], R1[:, 3, :, :], R1[:, 2, :, :]
                    link(dve.tensor_reduce(MX[:, 0:TILES], LG[:, :, :], AX.X, ALU.max))
                    for t in range(TILES):
                        ins = dve.tensor_scalar(R1[:, 1, t, :], LG[:, t, :], MX[:, t:t + 1], None, ALU.subtract)
                    ins.then_inc(lg_done, 1)
                    for t in range(TILES):
                        mine = LG[:, t, :].unsqueeze(2).to_broadcast([P, N_EXP, N_EXP])
                        other = LG[:, t, :].unsqueeze(1).to_broadcast([P, N_EXP, N_EXP])
                        dve.tensor_tensor(RK[:, 0], mine, other, ALU.is_lt)
                        link(dve.tensor_tensor(RK[:, 1], mine, other, ALU.is_equal))
                        link(dve.tensor_tensor(RK[:, 1], RK[:, 1], BEFORE[:, :, :], ALU.mult))
                        link(dve.tensor_tensor(RK[:, 0], RK[:, 0], RK[:, 1], ALU.add))
                        link(dve.tensor_reduce(rank[:, t, :], RK[:, 0], AX.X, ALU.add))
                    link(dve.tensor_scalar(sel, rank, 1.5, None, ALU.is_lt))
                    dve.wait_ge(pexp_done, 1)
                    link(dve.tensor_tensor(sel, sel, R1[:, 0, :, :], ALU.mult))
                    link(dve.tensor_reduce(MX[:, 0:TILES], sel, AX.X, ALU.add))
                    link(dve.reciprocal(MX[:, 0:TILES], MX[:, 0:TILES]))
                    for t in range(TILES):
                        link(dve.tensor_scalar(COMB[:, t, :], sel[:, t, :], MX[:, t:t + 1], None, ALU.mult))

                def ffn_slice(e, last):
                    def ahead(i):
                        k = i + RING
                        if k >= SLICE_PIECES and last:
                            return
                        low(i, WIDTHS[k % SLICE_PIECES], f["piece"] + k, e * SLICE_PIECES)

                    def gate_up(b, t):
                        if t == TILES - 1:
                            for j in range(GU_PIECES - 1):
                                ahead(b * GU_PIECES + j)
                        dve.wait_ge(silu_done, e * (GBLOCKS * TILES) + (f["gu"] - (IN_BLOCKS * TILES) * (layer + 1) + b * TILES + t + 1))
                        dve.tensor_tensor(H[:, t, b * GB:(b + 1) * GB], U[t][:, 0:GB], SG[:, t, :], ALU.mult).then_inc(gu_free, 1)
                        if t == TILES - 1:
                            ahead(b * GU_PIECES + GU_PIECES - 1)

                    def h_low(b, t):
                        k = b * TILES + t
                        c0, c1 = T_AFTER[b]
                        dve.wait_ge(tp_high, e * (GBLOCKS * TILES) + (f["tp"] + k + 1))
                        dst = (slice(None), slice(c0, c1), slice(t * P, (t + 1) * P))
                        dve.tensor_tensor(HTL[dst], TP[(f["tp"] + k) % 2][:, 0:(c1 - c0) * P].rearrange("p (c n) -> p c n", n=P),
                                          HTH[dst], ALU.subtract).then_inc(tp_free, 1)

                    for b in range(GBLOCKS):
                        gate_up(b, 0)
                        if b:
                            h_low(b - 1, 1)
                        gate_up(b, 1)
                        h_low(b, 0)
                    for d in range(DBLOCKS):
                        for t in range(TILES):
                            if d == 0 and t == 0:
                                h_low(GBLOCKS - 1, 1)
                            if t == TILES - 1:
                                for j in range(DN_PIECES):
                                    ahead(GBLOCKS * GU_PIECES + d * DN_PIECES + j)
                            gate = None
                            if layer == 1:
                                gate = COMB[:, t, bass.ds(e, 1)] if not last else COMB[:, t, e:e + 1]
                            add_down(d, t, e * (DBLOCKS * TILES) + (f["dn"] + d * TILES + t), gate)

                if layer + 1 < LAYERS:
                    with dve.Fori(0, f["slices"]) as e:
                        ffn_slice(e, False)
                    normalise(2 * layer + 2)
                else:
                    with dve.Fori(0, f["slices"] - 1) as e:
                        ffn_slice(e, False)
                    ffn_slice(f["slices"] - 1, True)


def pieces_by_column_block(w, width):
    *lead, k, n = w.shape
    w = w.reshape(*lead, k // (2 * P), 2, P, n // width, width)
    a = len(lead)
    w = w.transpose(*range(a), a + 3, a, a + 2, a + 1, a + 4)
    return np.ascontiguousarray(w.reshape(*lead, n // width, k // (2 * P), P, 2 * width))


def gate_up_pieces(gate, up):
    s = gate.shape[0]
    w = np.stack([gate, up], 1).reshape(s, 2, KD // 2, 2, P, GBLOCKS, GB)
    return np.ascontiguousarray(w.transpose(0, 5, 2, 4, 3, 1, 6).reshape(s, GBLOCKS, KD // 2, P, GU_W))


def down_pieces(down):
    s = down.shape[0]
    w = down.reshape(s, FC, P, DBLOCKS, NB).transpose(0, 3, 2, 1, 4)
    return np.ascontiguousarray(w.reshape(s, DBLOCKS, P, FC * NB))


def kernel(**inputs):
    import concourse.bacc as _bacc
    from concourse.bass_utils import run_bass_kernel_spmd as _run

    a = {k: np.asarray(v) for k, v in inputs.items()}
    by_slice = lambda w: w[0].reshape(D, DENSE_SLICES, FE).transpose(1, 0, 2)
    laid = {
        "x": a["x"][0],
        "positions": a["positions"].reshape(TILES, P).T,
        "norm_mix": a["norm_mix"],
        "w_in": pieces_by_column_block(a["w_in"], NB),
        "q_norm_sb": a["q_norm_sb"], "k_norm_sb": a["k_norm_sb"],
        "q_norm_dil": a["q_norm_dil"], "k_norm_dil": a["k_norm_dil"],
        "out_norm_sb": a["out_norm_sb"], "out_norm_dil": a["out_norm_dil"],
        "w_out": pieces_by_column_block(a["w_out"], NB),
        "norm_ffn": a["norm_ffn"],
        "gu_dense": gate_up_pieces(by_slice(a["w_gate_dense"]), by_slice(a["w_up_dense"])),
        "down_dense": down_pieces(a["w_down_dense"][0].reshape(DENSE_SLICES, FE, D)),
        "w_router": a["w_router"][0].reshape(KD, P, N_EXP).transpose(1, 0, 2).reshape(P, KD * N_EXP),
        "gu_moe": gate_up_pieces(a["w_gate_moe"][0], a["w_up_moe"][0]),
        "down_moe": down_pieces(a["w_down_moe"][0]),
        "inv_freq": (ROPE_THETA ** (-np.arange(0, DH, 2, dtype=np.float32) / np.float32(DH))).astype(np.float32),
    }
    nc = _bacc.Bacc("TRN2", target_bir_lowering=False, num_devices=1, dynamic_dma_scratch_size=4096)
    arrays, args = {}, {}
    for name, v in laid.items():
        v = np.ascontiguousarray(v)
        arrays[f"in_{name}"] = v
        args[name] = nc.dram_tensor(f"in_{name}", v.shape, mybir.dt.from_np(v.dtype), kind="ExternalInput").ap()
    args["out"] = nc.dram_tensor("out_x", (SEQ, D), F32, kind="ExternalOutput").ap()
    trunk(nc, **args)
    r = _run(nc, [arrays], core_ids=[0])
    return r.results[0]["out_x"].reshape(1, SEQ, D)
```

```python
from contextlib import ExitStack

import numpy as np
import concourse.bass as bass
from concourse import mybir

F32 = mybir.dt.float32
F32R = mybir.dt.float32r
I32 = mybir.dt.int32
ALU = mybir.AluOpType
ACT = mybir.ActivationFunctionType
AX = mybir.AxisListType

P = 128
SEQ = 256
TILES = SEQ // P
D = 2048
KD = D // P
HEADS = 4
DH = 128
D_MIX = 2 * HEADS * DH
D_IN = 3 * D_MIX
LAYERS = 2
N_EXP = 8
FE = 1408
FC = FE // P
DENSE_SLICES = 4
EPS = 1e-6
BIG = 1e30
EXP_OVERFLOW = 88.72283
SCALE = DH ** -0.5
ROPE_THETA = 10000.0

GB = 352
GBLOCKS = FE // GB
NB = 512
GU_W = 2 * 2 * GB
NB_W = 2 * NB
DN_PIECES = (FC + 1) // 2
RAW = 4
RING = 8

IN_BLOCKS, OUT_BLOCKS, DBLOCKS = D_IN // NB, D // NB, D // NB
IN_PIECES, OUT_PIECES, GU_PIECES = KD // 2, D_MIX // P // 2, KD // 2
SLICE_PIECES = GBLOCKS * GU_PIECES + DBLOCKS * DN_PIECES
SLICE_USED = GBLOCKS * (GU_PIECES - 1) + DBLOCKS * (DN_PIECES - 1)
T_AFTER = [(0, 2), (2, 5), (5, 8), (8, 11)]

SLOTS = P
PASSES = SEQ // SLOTS

TWO_PI_PARTS = (6.28125, 0.0019350051879882812, 3.019916e-07)
ROUND = 12582912.0


def expert_steps(more):
    order = [("gu", 1), ("t", 0), ("gu", 2), ("t", 1), ("gu", 3), ("t", 2), ("gather", 0), ("t", 3), ("dn", 0), ("dn", 1),
             ("sc", 0), ("dn", 2), ("sc", 1), ("dn", 3), ("sc", 2), ("gu", GBLOCKS), ("sc", 3), ("st", 0)]
    uses = {"t": 1, "gather": KD // 4, "sc": TILES, "st": TILES}
    tp = high = 0
    steps = []
    for name, i in order:
        if not more and (name in ("gather", "st") or (name, i) == ("gu", GBLOCKS)):
            continue
        steps.append((name, i, tp, high))
        tp += uses.get(name, 0)
        high += uses[name] if name in ("t", "gather") else 0
    return steps, tp, high


def down_width(j):
    return min(2, FC - 2 * j) * NB


def trunk(nc, x, positions, norm_mix, w_in, q_norm_sb, k_norm_sb, q_norm_dil, k_norm_dil, out_norm_sb,
          out_norm_dil, w_out, norm_ffn, gu_dense, down_dense, w_router, gu_moe, down_moe, inv_freq, out):
    FFN = [dict(), dict()]
    n_piece = n_gu = n_dn = n_tp = n_used = 0
    MIX = []
    for layer in range(LAYERS):
        MIX.append(dict(p_in=n_piece, p_out=n_piece + IN_BLOCKS * IN_PIECES, gu=n_gu, dn=n_dn,
                        tp_x=n_tp, tp_o=n_tp + 8, used_in=n_used, used_out=n_used + IN_BLOCKS * (IN_PIECES - 1)))
        n_used += IN_BLOCKS * (IN_PIECES - 1) + OUT_BLOCKS * (OUT_PIECES - 1)
        n_piece += IN_BLOCKS * IN_PIECES + OUT_BLOCKS * OUT_PIECES
        n_gu += IN_BLOCKS * TILES
        n_dn += OUT_BLOCKS * TILES
        n_tp += 12
        f = FFN[layer]
        f.update(piece=n_piece, gu=n_gu, dn=n_dn, tp_x=n_tp, tp=n_tp + 8, used=n_used)
        if layer == 0:
            n_piece += DENSE_SLICES * SLICE_PIECES
            n_used += DENSE_SLICES * SLICE_USED
            n_gu += DENSE_SLICES * GBLOCKS * TILES
            n_dn += DENSE_SLICES * DBLOCKS * TILES
            n_tp += 8 + DENSE_SLICES * GBLOCKS * TILES
    TP_MORE, HIGH_MORE = expert_steps(True)[1:]
    TP_LAST, HIGH_LAST = expert_steps(False)[1:]
    n_tp += 8
    n_high, n_silu = n_tp, DENSE_SLICES * GBLOCKS * TILES
    PASS = []
    for _ in range(PASSES):
        PASS.append(dict(piece=n_piece, used=n_used, gu=n_gu, dn=n_dn, tp0=n_tp, tp=n_tp + KD // 4 + TILES,
                         high0=n_high, high=n_high + KD // 4, silu=n_silu))
        n_piece += N_EXP * SLICE_PIECES
        n_used += N_EXP * SLICE_USED
        n_gu += N_EXP * GBLOCKS
        n_dn += N_EXP * DBLOCKS
        n_silu += N_EXP * GBLOCKS
        n_tp += KD // 4 + TILES + (N_EXP - 1) * TP_MORE + TP_LAST
        n_high += KD // 4 + (N_EXP - 1) * HIGH_MORE + HIGH_LAST

    with ExitStack() as ctx:
        def sb(name, shape, dt=F32, where=ctx):
            return where.enter_context(nc.sbuf_tensor(name, shape, dt))

        def sem(name):
            return ctx.enter_context(nc.semaphore(name))

        RAWS = sb("raw_pieces", [P, RAW, GU_W])
        WH = sb("w_high", [P, RING, GU_W], F32R)
        WL = sb("w_low", [P, RING, GU_W], F32R)
        X = sb("x_resid", [P, TILES, D])
        TOK = sb("token_major", [P, TILES * D_IN])
        HTH = sb("hT_high", [P, FC, SEQ], F32R)
        HTL = sb("hT_low", [P, FC, SEQ], F32R)
        SG = sb("silu_gate", [P, TILES, GB])
        IDN = sb("identity", [P, P])
        INCL = sb("incl", [P, P])
        ONES = sb("ones", [P, P])
        NEGZ = sb("neg_not_strict", [P, P])
        KEEPZ = sb("keep_strict", [P, P])
        CNT = sb("branch_count", [P, 3 * P])
        NEGU = sb("neg_union", [P, 3 * P])
        COS = sb("rope_cos", [P, TILES, DH // 2])
        SIN = sb("rope_sin", [P, TILES, DH // 2])
        WRH = sb("router_high", [P, KD, N_EXP], F32R)
        WRL = sb("router_low", [P, KD, N_EXP], F32R)
        COMB = sb("expert_gates", [P, TILES, N_EXP])
        SMALL = sb("small", [P, 64])
        XN = TOK[:, 0:TILES * D].rearrange("p (t n) -> p t n", t=TILES)
        GAIN = TOK[:, TILES * D:TILES * D + D]
        QKV = TOK[:, :].rearrange("p (t n) -> p t n", t=TILES)
        H = TOK[:, 0:TILES * FE].rearrange("p (t n) -> p t n", t=TILES)
        HM = GAIN[:, 0:FE]
        with ExitStack() as scratch:
            ATT = sb("mixer_scratch", [P, 2 * KD * SEQ], F32, scratch)
        XTH = sb("xT_high", [P, KD, SEQ], F32R)
        XTL = sb("xT_low", [P, KD, SEQ], F32R)

        at = [0]

        def part(n):
            at[0] += n
            return ATT[:, at[0] - n:at[0]]

        ROPE_C = part(2 * TILES * DH).rearrange("p (t q d) -> p t q d", t=TILES, q=2)
        ROPE_S = part(2 * TILES * DH).rearrange("p (t q d) -> p t q d", t=TILES, q=2)
        DIL_G = part(2 * DH).rearrange("p (q d) -> p q d", q=2)
        heads_at = at[0]
        QKT = [[part(4 * P) for _ in range(2)] for _ in range(2)]
        ZS, SPL, SP, AZ, WD, WDT = ([part(3 * P) for _ in range(2)] for _ in range(6))
        at[0] = heads_at
        SQ = part(TILES * D_MIX).rearrange("p (t n) -> p t n", t=TILES)
        RT1, RT2 = part(HEADS * DH), part(HEADS * DH)
        GOUT = ATT[:, 0:D_MIX]
        ANG, TURN, RED = (ATT[:, i * P:(i + 1) * P].rearrange("p (t d) -> p t d", t=TILES) for i in range(3))
        INV = ATT[:, 3 * P:3 * P + DH // 2]
        POS_I = ATT[:, 4 * P:4 * P + TILES].bitcast(I32)
        POS = ATT[:, 4 * P + 4:4 * P + 4 + TILES]
        DIST = ATT[:, 5 * P:8 * P].bitcast(I32)
        IOTA_I = ATT[:, 17 * P:18 * P].bitcast(I32)
        DMOD = ATT[:, 8 * P:11 * P].bitcast(I32)
        DF, C1 = ATT[:, 11 * P:14 * P], ATT[:, 14 * P:17 * P]
        SS, RSTD = SMALL[:, 0:2], SMALL[:, 2:4]
        SB_GAIN = SMALL[:, 4:6]
        O_SS, O_RSTD = SMALL[:, 6:10], SMALL[:, 10:14]
        HSS = SMALL[:, 14:46]
        MX, NMX, DEN, RDEN = (SMALL[:, 46 + 4 * i:50 + 4 * i] for i in range(4))
        HSSR = sb("head_rstd", [P, 32])
        LG = sb("logits", [P, TILES, N_EXP])
        RK = sb("rank_terms", [P, 2, N_EXP, N_EXP])
        BEFORE = sb("earlier_expert", [P, N_EXP, N_EXP])
        R1 = sb("router_rows", [P, 4, TILES, N_EXP])
        CHOSEN = sb("chosen", [P, TILES, N_EXP])
        SLOT = sb("slot", [P, TILES, N_EXP])
        IOTA = sb("iota_slots", [P, SLOTS])
        SEL = sb("selection", [P, TILES, SLOTS])
        SELT = sb("selection_T", [P, SEQ], F32R)
        FLAG = sb("another_pass", [P, 1], I32)
        YH = [HTH[:, 4 * i:4 * i + 4, P:2 * P] for i in range(2)]
        YL = [HTL[:, 4 * i:4 * i + 4, P:2 * P] for i in range(2)]

        def bank(name):
            return ctx.enter_context(nc.psum_tensor(name, [P, 512], F32))
        G = [bank("gate0"), bank("gate1")]
        U = [bank("up0"), bank("up1")]
        DN = [bank("down0"), bank("down1")]
        TP = [bank("transpose0"), bank("transpose1")]

        raw_full = [sem(f"raw_full{i}") for i in range(RAW)]
        high_done = sem("high_done")
        low_done = sem("low_done")
        used = sem("piece_used")
        gu_ready = sem("gu_ready")
        gu_free = sem("gu_free")
        silu_done = sem("silu_done")
        dn_ready = sem("dn_ready")
        dn_free = sem("dn_free")
        tp_ready = sem("tp_ready")
        tp_high = sem("tp_high")
        tp_free = sem("tp_free")
        x_in = sem("x_in")
        small_in = sem("small_in")
        gain_in = sem("gain_in")
        gain_used = sem("gain_used")
        router_in = sem("router_in")
        const_done = sem("const_done")
        tables_done = sem("tables_done")
        masks_done = sem("masks_done")
        pool_chain = sem("pool_chain")
        dve_chain = sem("dve_chain")
        act_chain = sem("act_chain")
        rope_red = sem("rope_reduced")
        sq_done = sem("sq_done")
        ms_done = sem("mean_square_done")
        root_done = sem("root_done")
        xn_done = sem("xn_done")
        dilg_in, gout_in, sbg_in = sem("dilg_in"), sem("gout_in"), sem("sbg_in")
        rope_done = sem("rope_done")
        sbg_done = sem("sbg_done")
        qk_t = sem("qk_transposed")
        qk_ev = sem("qk_evacuated")
        z_ready, z_copied, spl_done = sem("z_ready"), sem("z_copied"), sem("spl_done")
        sp_done, r_ready, az_done, a_done = sem("sp_done"), sem("r_ready"), sem("az_done"), sem("a_done")
        osb_ready, osb_done = sem("osb_ready"), sem("osb_done")
        s_ready, s_max, e_done = sem("s_ready"), sem("s_max"), sem("e_done")
        w_done, wt_ready, wt_done = sem("w_done"), sem("wt_ready"), sem("wt_done")
        odil_ready, odil_done = sem("odil_ready"), sem("odil_done")
        osq_done, on_done = sem("osq_done"), sem("on_done")
        wr_high, wr_done = sem("wr_high"), sem("wr_done")
        lg_ready, lg_done, pexp_done, comb_done = sem("lg_ready"), sem("lg_done"), sem("pexp_done"), sem("comb_done")
        chosen_done, pos_ready, slot_done = sem("chosen_done"), sem("pos_ready"), sem("slot_done")
        flag_done = sem("flag_done")
        sel_done = sem("sel_done")
        y_high = sem("y_high")
        stored = sem("stored")

        block = ctx.enter_context(nc.Block())

        def slice_pieces():
            return ([("gu", b, j, GU_W) for b in range(GBLOCKS) for j in range(GU_PIECES)]
                    + [("dn", d, j, down_width(j)) for d in range(DBLOCKS) for j in range(DN_PIECES)])

        def piece_at(piece0, b):
            return piece0 + (b * GU_PIECES if b < GBLOCKS else SLICE_PIECES)

        def used_at(used0, b):
            return used0 + (b * (GU_PIECES - 1) if b < GBLOCKS else SLICE_USED)

        WIDTHS = [w for _, _, _, w in slice_pieces()]

        @block.sync
        def _(sp):
            def load(slot, width, src, piece):
                if isinstance(piece, int):
                    if piece >= RAW:
                        sp.wait_ge(low_done, piece - RAW + 1)
                else:
                    sp.wait_ge(low_done, piece - (RAW - 1))
                sp.dma_start(RAWS[:, slot, 0:width], src).then_inc(raw_full[slot], 16)

            def stream_slice(gu, down, e, piece0):
                for i, (kind, b, j, width) in enumerate(slice_pieces()):
                    if kind == "gu":
                        src = gu[bass.ds(e, 1), b, j].rearrange("o p n -> (o p) n")
                    else:
                        src = down[bass.ds(e, 1), b, :, j * NB_W:j * NB_W + width].rearrange("o p n -> (o p) n")
                    load(i % RAW, width, src, e * SLICE_PIECES + (piece0 + i))

            sp.dma_start(X[:, :, :], x.rearrange("(t p) n -> p t n", p=P)).then_inc(x_in, 16)
            for layer in range(LAYERS):
                m, f = MIX[layer], FFN[layer]
                for c in range(IN_BLOCKS):
                    for j in range(IN_PIECES):
                        n = m["p_in"] + c * IN_PIECES + j
                        load(n % RAW, NB_W, w_in[layer, c, j], n)
                for d in range(OUT_BLOCKS):
                    for j in range(OUT_PIECES):
                        n = m["p_out"] + d * OUT_PIECES + j
                        load(n % RAW, NB_W, w_out[layer, d, j], n)
                if layer == 0:
                    with sp.Fori(0, DENSE_SLICES) as e:
                        stream_slice(gu_dense, down_dense, e, f["piece"])
            with sp.Fori(0, N_EXP) as e:
                stream_slice(gu_moe, down_moe, e, PASS[0]["piece"])
            sp.wait_ge(flag_done, 1)
            with sp.If(sp.value_load(FLAG[0:1, 0:1], min_val=0, max_val=1) > 0):
                with sp.Fori(0, N_EXP) as e:
                    stream_slice(gu_moe, down_moe, e, PASS[1]["piece"])
                sp.wait_ge(tp_free, n_tp)
            last = PASS[0]["tp"] + (N_EXP - 1) * TP_MORE
            for name, d, tp, _ in expert_steps(False)[0]:
                if name == "sc":
                    for t in range(TILES):
                        sp.wait_ge(tp_free, last + tp + t + 1)
                        sp.dma_start(out[t * P:(t + 1) * P, d * NB:(d + 1) * NB],
                                     X[:, t, d * NB:(d + 1) * NB]).then_inc(stored, 16)
            sp.wait_ge(stored, 16 * DBLOCKS * TILES)

        @block.gpsimd
        def _(pool):
            n = [0]

            def link(ins):
                n[0] += 1
                ins.then_inc(pool_chain, 1)
                pool.wait_ge(pool_chain, n[0])

            pool.dma_start(GAIN, norm_mix[0].partition_broadcast(P)).then_inc(gain_in, 16)
            pool.dma_start(INV, inv_freq.partition_broadcast(P)).then_inc(small_in, 16)
            pool.dma_start(POS_I, positions).then_inc(small_in, 16)
            link(pool.memset(IDN[:, :], 0.0))
            link(pool.affine_select(out=IDN[:, :], in_=IDN[:, :], compare_op=ALU.not_equal, fill=1.0, base=0,
                                    pattern=[[-1, P]], channel_multiplier=1))
            link(pool.memset(ONES[:, :], 1.0))
            link(pool.affine_select(out=INCL[:, :], in_=ONES[:, :], compare_op=ALU.is_ge, fill=0.0, base=0,
                                    pattern=[[-1, P]], channel_multiplier=1))
            link(pool.affine_select(out=KEEPZ[:, :], in_=ONES[:, :], compare_op=ALU.is_gt, fill=0.0, base=0,
                                    pattern=[[1, P]], channel_multiplier=-1))
            link(pool.memset(NEGZ[:, :], 0.0))
            link(pool.affine_select(out=NEGZ[:, :], in_=NEGZ[:, :], compare_op=ALU.is_gt, fill=-BIG, base=0,
                                    pattern=[[1, P]], channel_multiplier=-1))
            link(pool.iota(DIST[:, 0:P], [[-1, P]], base=0, channel_multiplier=1))
            link(pool.iota(DIST[:, P:3 * P], [[-1, 2 * P]], base=P, channel_multiplier=1))
            link(pool.iota(IOTA_I, [[1, SLOTS]], base=0, channel_multiplier=0))
            link(pool.memset(BEFORE[:, :, :], 1.0))
            pool.affine_select(out=BEFORE[:, :, :], in_=BEFORE[:, :, :], compare_op=ALU.is_gt, fill=0.0, base=0,
                               pattern=[[1, N_EXP], [-1, N_EXP]], channel_multiplier=0).then_inc(const_done, 1)
            for layer in range(LAYERS):
                m = MIX[layer]
                pool.wait_ge(gu_ready, m["gu"] + IN_BLOCKS * TILES)
                pool.dma_start(DIL_G[:, 0, :], q_norm_dil[layer].partition_broadcast(P)).then_inc(dilg_in, 16)
                pool.dma_start(DIL_G[:, 1, :], k_norm_dil[layer].partition_broadcast(P)).then_inc(dilg_in, 16)
                if layer:
                    pool.wait_ge(qk_ev, 2 * HEADS * layer)
                pool.dma_start(SB_GAIN[:, 0:1], q_norm_sb[layer].rearrange("(p o) -> p o", o=1)).then_inc(sbg_in, 16)
                pool.dma_start(SB_GAIN[:, 1:2], k_norm_sb[layer].rearrange("(p o) -> p o", o=1)).then_inc(sbg_in, 16)
                pool.wait_ge(rope_done, layer + 1)
                pool.dma_start(GOUT[:, 0:HEADS * DH], out_norm_sb[layer].partition_broadcast(P)).then_inc(gout_in, 16)
                pool.dma_start(GOUT[:, HEADS * DH:], out_norm_dil[layer].partition_broadcast(P)).then_inc(gout_in, 16)
                pool.wait_ge(tp_ready, m["tp_o"] + 4)
                pool.dma_start(GAIN, norm_ffn[layer].partition_broadcast(P)).then_inc(gain_in, 16)
                if layer + 1 < LAYERS:
                    pool.wait_ge(xn_done, TILES * (2 * layer + 2))
                    pool.dma_start(GAIN, norm_mix[layer + 1].partition_broadcast(P)).then_inc(gain_in, 16)
            pool.wait_ge(xn_done, TILES * 2 * LAYERS)
            pool.dma_start(GAIN[:, 0:KD * N_EXP], w_router).then_inc(router_in, 16)
            for s, v in ((gain_in, 16 * 2 * LAYERS), (small_in, 32), (router_in, 16)):
                pool.wait_ge(s, v)

        @block.tensor
        def _(pe):
            def three(out_ap, left, ls, right, rs, first, last):
                (lh, ll), (rh, rl) = left, right
                pe.matmul(out_ap, lh[ls], rh[rs], start=first, stop=False)
                pe.matmul(out_ap, lh[ls], rl[rs], start=False, stop=False)
                return pe.matmul(out_ap, ll[ls], rh[rs], start=False, stop=last)

            def transposes(k, src, chunks):
                for i, c in enumerate(chunks):
                    ins = pe.transpose(TP[k % 2][:, i * P:(i + 1) * P], src[:, c * P:(c + 1) * P], IDN[:, :])
                ins.then_inc(tp_ready, 1)

            def x_transposes(norm, tp):
                for t in range(TILES):
                    pe.wait_ge(xn_done, TILES * norm + t + 1)
                    for q in range(4):
                        k = tp + 4 * t + q
                        if k >= 2:
                            pe.wait_ge(tp_free, k - 1)
                        transposes(k, XN[:, t, :], range(4 * q, 4 * q + 4))

            def project(t, slot0, pieces, chunks, piece0, banks, act, last_tile, shift=0):
                for j in range(pieces):
                    slot = (slot0 + j) % RING
                    if t == 0:
                        pe.wait_ge(low_done, piece0 + (j + 1))
                    k2 = min(2, chunks - 2 * j)
                    for i in range(k2):
                        k = 2 * j + i
                        first, last = k == 0, k == chunks - 1
                        left = [a[:, k, t * P:(t + 1) * P] for a in act]
                        for half in range(2):
                            for n, (b, lo, hi) in enumerate(banks):
                                right = [w[:, slot, i * (GU_W // 2 if len(banks) == 2 else NB) + lo:
                                           i * (GU_W // 2 if len(banks) == 2 else NB) + hi] for w in (WH, WL)]
                                if half == 0:
                                    pe.matmul(b, left[0], right[0], start=first, stop=False)
                                    ins = pe.matmul(b, left[0], right[1], start=False, stop=False)
                                else:
                                    ins = pe.matmul(b, left[1], right[0], start=False, stop=last)
                    if last_tile and j < pieces - 1:
                        ins.then_inc(used, 1)
                return ins

            pe.wait_ge(const_done, 1)
            for layer in range(LAYERS):
                m, f = MIX[layer], FFN[layer]
                x_transposes(2 * layer, m["tp_x"])
                pe.wait_ge(tp_free, m["tp_x"] + 8)
                with pe.Fori(0, IN_BLOCKS) as c:
                    for t in range(TILES):
                        pe.wait_ge(gu_free, c * TILES + (m["gu"] + t + 1))
                        ins = project(t, 0, IN_PIECES, KD, c * IN_PIECES + m["p_in"], [(G[t][:, :], 0, NB)],
                                      (XTH, XTL), t == TILES - 1)
                        ins.then_inc(gu_ready, 1)
                pe.wait_ge(rope_done, layer + 1)
                for h in range(HEADS):
                    n = HEADS * layer + h
                    b = h % 2
                    for kind in range(2):
                        col = 3 * HEADS * DH * kind + h * DH
                        if n:
                            pe.wait_ge(qk_ev, 2 * (n - 1) + kind + 1)
                        for qk in range(2):
                            for t in range(TILES):
                                ins = pe.transpose(TP[kind][:, (2 * qk + t) * P:(2 * qk + t + 1) * P],
                                                   QKV[:, t, col + qk * HEADS * DH:col + qk * HEADS * DH + DH], IDN[:, :])
                        ins.then_inc(qk_t, 1)
                    qs, ks = QKT[0][b][:, 0:2 * P], QKT[0][b][:, 2 * P:4 * P]
                    qd, kd = QKT[1][b][:, 0:2 * P], QKT[1][b][:, 2 * P:4 * P]
                    pe.wait_ge(qk_ev, 2 * n + 1)
                    if n:
                        pe.wait_ge(z_copied, n)
                    pe.matmul(G[0][:, 0:2 * P], ks[:, 0:P], qs, start=True, stop=True)
                    pe.matmul(G[0][:, 2 * P:3 * P], ks[:, P:2 * P], qs[:, P:2 * P], start=True, stop=True).then_inc(z_ready, 1)
                    pe.wait_ge(qk_ev, 2 * n + 2)
                    if n:
                        pe.wait_ge(s_max, n)
                    pe.matmul(U[0][:, 0:P], qd[:, 0:P], kd[:, 0:P], start=True, stop=True)
                    pe.matmul(U[0][:, P:3 * P], qd[:, P:2 * P], kd, start=True, stop=True).then_inc(s_ready, 1)
                    pe.wait_ge(sp_done, n + 1)
                    if n:
                        pe.wait_ge(az_done, n)
                    sp_b = SP[b]
                    pe.matmul(G[1][:, 0:2 * P], INCL[:, :], sp_b[:, 0:2 * P], start=True, stop=False)
                    pe.matmul(G[1][:, P:2 * P], ONES[:, :], sp_b[:, 2 * P:3 * P], start=False, stop=True)
                    pe.matmul(G[1][:, 2 * P:3 * P], INCL[:, :], sp_b[:, 2 * P:3 * P], start=True, stop=True).then_inc(r_ready, 1)
                    pe.wait_ge(w_done, n + 1)
                    if n:
                        pe.wait_ge(wt_done, n)
                    for i in range(3):
                        ins = pe.transpose(U[1][:, i * P:(i + 1) * P], WD[b][:, i * P:(i + 1) * P], IDN[:, :])
                    ins.then_inc(wt_ready, 1)
                    for w, bnk, done, free, ready, kind in ((AZ[b], DN[0], a_done, osb_done, osb_ready, 0),
                                                            (WDT[b], DN[1], wt_done, odil_done, odil_ready, 1)):
                        v = 3 * HEADS * DH * kind + 2 * HEADS * DH + h * DH
                        pe.wait_ge(done, n + 1)
                        if n:
                            pe.wait_ge(free, n)
                        pe.matmul(bnk[:, 0:P], w[:, 0:P], QKV[:, 0, v:v + DH], start=True, stop=True)
                        pe.matmul(bnk[:, P:2 * P], w[:, P:2 * P], QKV[:, 0, v:v + DH], start=True, stop=False)
                        pe.matmul(bnk[:, P:2 * P], w[:, 2 * P:3 * P], QKV[:, 1, v:v + DH], start=False, stop=True).then_inc(ready, 1)
                for t in range(TILES):
                    for kind in range(2):
                        k = m["tp_o"] + 2 * t + kind
                        pe.wait_ge(on_done, 2 * TILES * layer + 2 * t + kind + 1)
                        pe.wait_ge(tp_free, k - 1)
                        transposes(k, QKV[:, t, 3 * HEADS * DH * kind:], range(HEADS))
                pe.wait_ge(tp_free, m["tp_o"] + 4)
                for d in range(OUT_BLOCKS):
                    for t in range(TILES):
                        n = m["dn"] + TILES * d + t
                        pe.wait_ge(dn_free, n + 1)
                        ins = project(t, d * OUT_PIECES, OUT_PIECES, D_MIX // P, m["p_out"] + d * OUT_PIECES,
                                      [(DN[t][:, :], 0, NB)], (HTH, HTL), t == TILES - 1)
                        ins.then_inc(dn_ready, 1)
                x_transposes(2 * layer + 1, f["tp_x"])
                pe.wait_ge(tp_free, f["tp_x"] + 8)
                if layer == 1:
                    pe.wait_ge(wr_done, 1)
                    for t in range(TILES):
                        for k in range(KD):
                            ts = (slice(None), k, slice(t * P, (t + 1) * P))
                            ins = three(DN[0][:, t * N_EXP:(t + 1) * N_EXP], (XTH, XTL), ts, (WRH, WRL),
                                        (slice(None), k, slice(None)), k == 0, k == KD - 1)
                    ins.then_inc(lg_ready, 1)
                    pe.wait_ge(lg_done, 1)

                def ffn_slice(e):
                    def gate_up(b, t):
                        pe.wait_ge(gu_free, e * (GBLOCKS * TILES) + (f["gu"] + b * TILES + t + 1))
                        ins = project(t, b * GU_PIECES, GU_PIECES, KD, e * SLICE_PIECES + (f["piece"] + b * GU_PIECES),
                                      [(G[t][:, 0:GB], 0, GB), (U[t][:, 0:GB], GB, 2 * GB)], (XTH, XTL), t == TILES - 1)
                        ins.then_inc(gu_ready, 1)

                    def h_transposes(b, t):
                        k = b * TILES + t
                        pe.wait_ge(gu_free, e * (GBLOCKS * TILES) + (f["gu"] + k + 3))
                        pe.wait_ge(tp_free, e * (GBLOCKS * TILES) + (f["tp"] + k - 1))
                        transposes(f["tp"] + k, H[:, t, :], range(*T_AFTER[b]))

                    def down(d, t):
                        k = e * (DBLOCKS * TILES) + (f["dn"] + d * TILES + t)
                        pe.wait_ge(dn_free, k + 1)
                        if d == 0:
                            pe.wait_ge(tp_free, e * (GBLOCKS * TILES) + (f["tp"] + (GBLOCKS - 1) * TILES + t + 1))
                        ins = project(t, GBLOCKS * GU_PIECES + d * DN_PIECES, DN_PIECES, FC,
                                      e * SLICE_PIECES + (f["piece"] + GBLOCKS * GU_PIECES + d * DN_PIECES),
                                      [(DN[t][:, :], 0, NB)], (HTH, HTL), t == TILES - 1)
                        ins.then_inc(dn_ready, 1)

                    for b in range(GBLOCKS):
                        gate_up(b, 0)
                        if b:
                            h_transposes(b - 1, 1)
                        gate_up(b, 1)
                        h_transposes(b, 0)
                    down(0, 0)
                    h_transposes(GBLOCKS - 1, 1)
                    for d in range(DBLOCKS):
                        if d:
                            down(d, 0)
                        down(d, 1)

                if layer == 0:
                    with pe.Fori(0, DENSE_SLICES) as e:
                        ffn_slice(e)

            pe.wait_ge(chosen_done, 1)
            pe.matmul(DN[1][:, 0:N_EXP], KEEPZ[:, :], CHOSEN[:, 0, :], start=True, stop=True)
            pe.matmul(DN[1][:, N_EXP:2 * N_EXP], ONES[:, :], CHOSEN[:, 0, :], start=True, stop=False)
            pe.matmul(DN[1][:, N_EXP:2 * N_EXP], KEEPZ[:, :], CHOSEN[:, 1, :], start=False, stop=True)
            pe.matmul(DN[1][:, 2 * N_EXP:3 * N_EXP], ONES[:, :], CHOSEN[:, 0, :], start=True, stop=False)
            pe.matmul(DN[1][:, 2 * N_EXP:3 * N_EXP], ONES[:, :], CHOSEN[:, 1, :], start=False, stop=True).then_inc(pos_ready, 1)
            pe.wait_ge(slot_done, 1)

            def moe_pass(n_pass):
                s = PASS[n_pass]

                def gathered(e, b):
                    if b == 0:
                        return s["tp0"] + KD // 4
                    at_ = next(tp for name, _, tp, _ in expert_steps(True)[0] if name == "gather")
                    return e * TP_MORE + (s["tp"] + at_ + KD // 4)

                def gate_up(e, b):
                    pe.wait_ge(gu_free, e * GBLOCKS + (s["gu"] + b + 1))
                    if b % GBLOCKS == 0:
                        pe.wait_ge(tp_free, gathered(e, b))
                    n = b % 2
                    project(0, (b % GBLOCKS) * GU_PIECES, GU_PIECES, KD, e * SLICE_PIECES + piece_at(s["piece"], b),
                            [(G[n][:, 0:GB], 0, GB), (U[n][:, 0:GB], GB, 2 * GB)], (XTH, XTL), True).then_inc(gu_ready, 1)

                def gather(count, k0, n_sel):
                    pe.wait_ge(sel_done, n_sel)
                    for q in range(KD // 4):
                        pe.wait_ge(tp_free, count + (q - 1))
                        for i in range(4):
                            c = 4 * q + i
                            for t in range(TILES):
                                ins = pe.matmul(TP[(k0 + q) % 2][:, i * P:(i + 1) * P], XN[:, t, c * P:(c + 1) * P],
                                                SEL[:, t, :], start=t == 0, stop=t == TILES - 1)
                        ins.then_inc(tp_ready, 1)

                def selection_transposed(count, k0):
                    for t in range(TILES):
                        pe.wait_ge(tp_free, count + (t - 1))
                        pe.transpose(TP[(k0 + t) % 2][:, 0:P], SEL[:, t, :], IDN[:, :]).then_inc(tp_ready, 1)

                def expert(e, more):
                    steps = expert_steps(more)[0]
                    last_t = next(tp for name, i, tp, _ in steps if (name, i) == ("t", GBLOCKS - 1))
                    for name, i, tp, _ in steps:
                        count = e * TP_MORE + (s["tp"] + tp)
                        k0 = s["tp"] + tp
                        if name == "gu":
                            gate_up(e, i)
                        elif name == "t":
                            pe.wait_ge(gu_free, e * GBLOCKS + (s["gu"] + i + 3))
                            pe.wait_ge(tp_free, count - 1)
                            transposes(k0, HM, range(*T_AFTER[i]))
                        elif name == "gather":
                            gather(count, k0, e + (N_EXP * n_pass + 2))
                        elif name == "dn":
                            pe.wait_ge(dn_free, e * DBLOCKS + (s["dn"] + i + 1))
                            if i == 0:
                                pe.wait_ge(tp_free, e * TP_MORE + (s["tp"] + last_t + 1))
                            project(0, GBLOCKS * GU_PIECES + i * DN_PIECES, DN_PIECES, FC,
                                    e * SLICE_PIECES + (s["piece"] + GBLOCKS * GU_PIECES + i * DN_PIECES),
                                    [(DN[i % 2][:, :], 0, NB)], (HTH, HTL), True).then_inc(dn_ready, 1)
                        elif name == "sc":
                            pe.wait_ge(dn_free, e * DBLOCKS + (s["dn"] + i + 3))
                            for t in range(TILES):
                                pe.wait_ge(tp_free, count + (t - 1))
                                bnk = TP[(k0 + t) % 2][:, :]
                                pe.matmul(bnk, SELT[:, t * P:(t + 1) * P], YH[i % 2], start=True, stop=False)
                                pe.matmul(bnk, SELT[:, t * P:(t + 1) * P], YL[i % 2], start=False, stop=True).then_inc(tp_ready, 1)
                        else:
                            selection_transposed(count, k0)

                gather(s["tp0"], s["tp0"], N_EXP * n_pass + 1)
                gate_up(0, 0)
                selection_transposed(s["tp0"] + KD // 4, s["tp0"] + KD // 4)
                with pe.Fori(0, N_EXP - 1) as e:
                    expert(e, True)
                expert(N_EXP - 1, False)

            moe_pass(0)
            pe.wait_ge(flag_done, 1)
            with pe.If(pe.value_load(FLAG[0:1, 0:1], min_val=0, max_val=1) > 0):
                moe_pass(1)

        @block.scalar
        def _(act):
            n_link = [0]

            def link(ins):
                n_link[0] += 1
                ins.then_inc(act_chain, 1)
                act.wait_ge(act_chain, n_link[0])

            def high_ahead(i, width, piece, shift=0):
                act.wait_ge(raw_full[i % RAW], shift * (16 // RAW) + 16 * (piece // RAW + 1))
                act.activation(WH[:, i % RING, 0:width], RAWS[:, i % RAW, 0:width], ACT.Copy).then_inc(high_done, 1)

            def squares(norm):
                for t in range(TILES):
                    act.activation(XN[:, t, :], X[:, t, :], ACT.Square, accum_out=SS[:, t:t + 1]).then_inc(sq_done, 1)

            def x_high(k, t, q):
                act.wait_ge(tp_ready, k + 1)
                act.activation(XTH[:, 4 * q:4 * q + 4, t * P:(t + 1) * P], TP[k % 2][:, :].rearrange("p (c n) -> p c n", c=4),
                               ACT.Copy).then_inc(tp_high, 1)

            def roots(which, n):
                act.wait_ge(ms_done, n + 1)
                act.activation(which, which, ACT.Sqrt).then_inc(root_done, 1)

            act.sem_inc(gu_free, 2)
            act.sem_inc(dn_free, 2)
            act.wait_ge(x_in, 16)
            act.wait_ge(gain_in, 16)
            squares(0)
            roots(RSTD, 0)
            act.wait_ge(rope_red, 1)
            act.activation(SIN[:, :, :], RED, ACT.Sin).then_inc(tables_done, 1)
            act.wait_ge(rope_red, 2)
            act.activation(COS[:, :, :], TURN, ACT.Sin).then_inc(tables_done, 1)
            act.wait_ge(tables_done, 2)
            act.wait_ge(masks_done, 1)
            for layer in range(LAYERS):
                m, f = MIX[layer], FFN[layer]
                for k in range(8):
                    x_high(m["tp_x"] + k, k // 4, k % 4)
                    if layer == 0:
                        high_ahead(k, NB_W, k)
                with act.Fori(0, IN_BLOCKS) as c:
                    for t in range(TILES):
                        if t == TILES - 1:
                            for j in range(IN_PIECES - 1):
                                act.wait_ge(used, c * (IN_PIECES - 1) + (m["used_in"] + j + 1))
                                high_ahead(j, NB_W, m["p_in"] + j + RING, c * IN_PIECES)
                        act.wait_ge(gu_ready, c * TILES + (m["gu"] + t + 1))
                        if t == TILES - 1:
                            high_ahead(IN_PIECES - 1, NB_W, m["p_in"] + IN_PIECES - 1 + RING, c * IN_PIECES)
                        act.activation(TOK[:, bass.ds(c * NB + t * D_IN, NB)], G[t][:, :], ACT.Copy).then_inc(gu_free, 1)
                roots(HSSR[:, :], 4 * layer + 1)
                act.wait_ge(sbg_done, layer + 1)
                for h in range(HEADS):
                    n = HEADS * layer + h
                    b = h % 2
                    act.wait_ge(qk_t, 2 * n + 1)
                    if h >= 2:
                        act.wait_ge(z_ready, n - 1)
                        act.wait_ge(s_ready, n - 1)
                    act.activation(QKT[0][b][:, 0:2 * P], TP[0][:, 0:2 * P], ACT.Copy, scale=SB_GAIN[:, 0:1])
                    act.activation(QKT[0][b][:, 2 * P:4 * P], TP[0][:, 2 * P:4 * P], ACT.Copy,
                                   scale=SB_GAIN[:, 1:2]).then_inc(qk_ev, 1)
                    act.wait_ge(qk_t, 2 * n + 2)
                    act.activation(QKT[1][b], TP[1][:, :], ACT.Copy).then_inc(qk_ev, 1)
                    act.wait_ge(z_ready, n + 1)
                    if h >= 2:
                        act.wait_ge(az_done, n - 1)
                    act.activation(ZS[b], G[0][:, 0:3 * P], ACT.Copy).then_inc(z_copied, 1)
                    link(act.activation(SPL[b], G[0][:, 0:3 * P], ACT.Abs))
                    link(act.activation(SPL[b], SPL[b], ACT.Exp, scale=-1.0))
                    act.activation(SPL[b], SPL[b], ACT.Ln, bias=1.0).then_inc(spl_done, 1)
                    act.wait_ge(s_max, n + 1)
                    act.activation(WD[b][:, 0:P], WD[b][:, 0:P], ACT.Exp, bias=NMX[:, 2 * b:2 * b + 1], scale=SCALE)
                    act.activation(WD[b][:, P:3 * P], WD[b][:, P:3 * P], ACT.Exp, bias=NMX[:, 2 * b + 1:2 * b + 2],
                                   scale=SCALE).then_inc(e_done, 1)
                    act.wait_ge(az_done, n + 1)
                    act.activation(AZ[b], AZ[b], ACT.Exp).then_inc(a_done, 1)
                    act.wait_ge(wt_ready, n + 1)
                    if h >= 2:
                        act.wait_ge(odil_ready, n - 1)
                    act.activation(WDT[b], U[1][:, 0:3 * P], ACT.Copy).then_inc(wt_done, 1)
                    act.wait_ge(osb_ready, n + 1)
                    act.activation(QKV[:, :, h * DH:(h + 1) * DH], DN[0][:, 0:2 * P].rearrange("p (t d) -> p t d", t=TILES),
                                   ACT.Copy).then_inc(osb_done, 1)
                    act.wait_ge(odil_ready, n + 1)
                    for t in range(TILES):
                        ins = act.activation(QKV[:, t, 3 * HEADS * DH + h * DH:3 * HEADS * DH + (h + 1) * DH],
                                             DN[1][:, t * P:(t + 1) * P], ACT.Copy, scale=RDEN[:, 2 * b + t:2 * b + t + 1])
                    ins.then_inc(odil_done, 1)
                act.wait_ge(odil_done, HEADS * (layer + 1))
                act.wait_ge(osb_done, HEADS * (layer + 1))
                for t in range(TILES):
                    for kind in range(2):
                        act.activation(ATT[:, heads_at:heads_at + HEADS * DH], QKV[:, t, 3 * HEADS * DH * kind:3 * HEADS * DH * kind + HEADS * DH],
                                       ACT.Square, accum_out=O_SS[:, 2 * t + kind:2 * t + kind + 1]).then_inc(osq_done, 1)
                        act.wait_ge(osq_done, 2 * TILES * layer + 2 * t + kind + 1)
                roots(O_RSTD, 4 * layer + 2)
                for t in range(TILES):
                    for kind in range(2):
                        k = m["tp_o"] + 2 * t + kind
                        act.wait_ge(tp_ready, k + 1)
                        act.activation(HTH[:, HEADS * kind:HEADS * (kind + 1), t * P:(t + 1) * P],
                                       TP[k % 2][:, :].rearrange("p (c n) -> p c n", c=4), ACT.Copy).then_inc(tp_high, 1)
                for d in range(OUT_BLOCKS):
                    for j in range(OUT_PIECES):
                        i = d * OUT_PIECES + j
                        if j < OUT_PIECES - 1:
                            act.wait_ge(used, m["used_out"] + d * (OUT_PIECES - 1) + j + 1)
                        else:
                            act.wait_ge(dn_ready, m["dn"] + TILES * (d + 1))
                        high_ahead(i, NB_W if i + RING < OUT_BLOCKS * OUT_PIECES else GU_W, m["p_out"] + i + RING)
                act.wait_ge(dn_free, 2 + m["dn"] + OUT_BLOCKS * TILES)
                act.wait_ge(gain_in, 16 * (2 * layer + 2))
                squares(2 * layer + 1)
                roots(RSTD, 4 * layer + 3)
                if layer == 1:
                    act.wait_ge(router_in, 16)
                    act.activation(WRH[:, :, :], GAIN[:, 0:KD * N_EXP].rearrange("p (k e) -> p k e", k=KD), ACT.Copy).then_inc(wr_high, 1)
                for k in range(8):
                    x_high(f["tp_x"] + k, k // 4, k % 4)
                if layer == 1:
                    act.wait_ge(lg_done, 2)
                    for t in range(TILES):
                        ins = act.activation(R1[:, 0, t, :], R1[:, 1, t, :], ACT.Exp)
                    ins.then_inc(pexp_done, 1)

                def ffn_slice(e):
                    def ahead(i, semaphore, count):
                        act.wait_ge(semaphore, count)
                        high_ahead(i, WIDTHS[(i + RING) % SLICE_PIECES], f["piece"] + i + RING, e * SLICE_PIECES)

                    def gate_up(b, t):
                        if t == TILES - 1:
                            for j in range(GU_PIECES - 1):
                                ahead(b * GU_PIECES + j, used, e * SLICE_USED + (f["used"] + b * (GU_PIECES - 1) + j + 1))
                        act.wait_ge(gu_ready, e * (GBLOCKS * TILES) + (f["gu"] + b * TILES + t + 1))
                        act.activation(SG[:, t, :], G[t][:, 0:GB], ACT.Silu).then_inc(silu_done, 1)
                        if t == TILES - 1:
                            ahead(b * GU_PIECES + GU_PIECES - 1, gu_ready,
                                  e * (GBLOCKS * TILES) + (f["gu"] + b * TILES + t + 1))

                    def h_high(b, t):
                        k = b * TILES + t
                        c0, c1 = T_AFTER[b]
                        act.wait_ge(tp_ready, e * (GBLOCKS * TILES) + (f["tp"] + k + 1))
                        act.activation(HTH[:, c0:c1, t * P:(t + 1) * P],
                                       TP[(f["tp"] + k) % 2][:, 0:(c1 - c0) * P].rearrange("p (c n) -> p c n", n=P),
                                       ACT.Copy).then_inc(tp_high, 1)

                    for b in range(GBLOCKS):
                        gate_up(b, 0)
                        if b:
                            h_high(b - 1, 1)
                        gate_up(b, 1)
                        h_high(b, 0)
                    h_high(GBLOCKS - 1, 1)
                    for d in range(DBLOCKS):
                        for j in range(DN_PIECES - 1):
                            ahead(GBLOCKS * GU_PIECES + d * DN_PIECES + j, used,
                                  e * SLICE_USED + (f["used"] + GBLOCKS * (GU_PIECES - 1) + d * (DN_PIECES - 1) + j + 1))
                        ahead(GBLOCKS * GU_PIECES + (d + 1) * DN_PIECES - 1, dn_ready,
                              e * (DBLOCKS * TILES) + (f["dn"] + TILES * (d + 1)))

                if layer == 0:
                    with act.Fori(0, DENSE_SLICES) as e:
                        ffn_slice(e)
                    act.wait_ge(dn_free, 2 + f["dn"] + DENSE_SLICES * DBLOCKS * TILES)
                    act.wait_ge(tp_ready, f["tp"] + DENSE_SLICES * GBLOCKS * TILES)
                    squares(2)
                    roots(RSTD, 4)

            def moe_pass(n_pass):
                s = PASS[n_pass]

                def ahead(e, i, semaphore, count, more):
                    if i % SLICE_PIECES + RING < SLICE_PIECES or more:
                        act.wait_ge(semaphore, count)
                        high_ahead(i, WIDTHS[(i + RING) % SLICE_PIECES], s["piece"] + i + RING, e * SLICE_PIECES)

                def gate_up(e, b, more=True):
                    i0 = piece_at(0, b)
                    for j in range(GU_PIECES - 1):
                        ahead(e, i0 + j, used, e * SLICE_USED + (used_at(s["used"], b) + j + 1), more)
                    act.wait_ge(gu_ready, e * GBLOCKS + (s["gu"] + b + 1))
                    act.activation(SG[:, b % 2, :], G[b % 2][:, 0:GB], ACT.Silu).then_inc(silu_done, 1)
                    ahead(e, i0 + GU_PIECES - 1, gu_ready, e * GBLOCKS + (s["gu"] + b + 1), more)

                def gathered_high(count, k0):
                    for q in range(KD // 4):
                        act.wait_ge(tp_ready, count + (q + 1))
                        act.activation(XTH[:, 4 * q:4 * q + 4, 0:SLOTS], TP[(k0 + q) % 2][:, :].rearrange("p (c n) -> p c n", c=4),
                                       ACT.Copy).then_inc(tp_high, 1)

                def expert(e, more):
                    for name, i, tp, _ in expert_steps(more)[0]:
                        count = e * TP_MORE + (s["tp"] + tp)
                        k0 = s["tp"] + tp
                        if name == "gu":
                            gate_up(e, i, more)
                        elif name == "t":
                            c0, c1 = T_AFTER[i]
                            act.wait_ge(tp_ready, count + 1)
                            act.activation(HTH[:, c0:c1, 0:SLOTS], TP[k0 % 2][:, 0:(c1 - c0) * P].rearrange("p (c n) -> p c n", n=P),
                                           ACT.Copy).then_inc(tp_high, 1)
                        elif name == "gather":
                            gathered_high(count, k0)
                        elif name == "dn":
                            i0 = GBLOCKS * GU_PIECES + i * DN_PIECES
                            for j in range(DN_PIECES - 1):
                                ahead(e, i0 + j, used, e * SLICE_USED
                                      + (s["used"] + GBLOCKS * (GU_PIECES - 1) + i * (DN_PIECES - 1) + j + 1), more)
                            act.wait_ge(dn_ready, e * DBLOCKS + (s["dn"] + i + 1))
                            act.activation(YH[i % 2], DN[i % 2][:, :].rearrange("p (c n) -> p c n", n=P), ACT.Copy).then_inc(y_high, 1)
                            ahead(e, i0 + DN_PIECES - 1, dn_ready, e * DBLOCKS + (s["dn"] + i + 1), more)

                if n_pass:
                    for i in range(RING):
                        high_ahead(i, WIDTHS[i], s["piece"] + i)
                gathered_high(s["tp0"], s["tp0"])
                gate_up(0, 0)
                with act.Fori(0, N_EXP - 1) as e:
                    expert(e, True)
                expert(N_EXP - 1, False)

            moe_pass(0)
            act.wait_ge(flag_done, 1)
            with act.If(act.value_load(FLAG[0:1, 0:1], min_val=0, max_val=1) > 0):
                moe_pass(1)

        @block.vector
        def _(dve):
            n_link = [0]

            def link(ins):
                n_link[0] += 1
                ins.then_inc(dve_chain, 1)
                dve.wait_ge(dve_chain, n_link[0])

            def low(i, width, piece, shift=None):
                dve.wait_ge(high_done, piece + 1 if shift is None else shift + (piece + 1))
                dve.tensor_tensor(WL[:, i % RING, 0:width], RAWS[:, i % RAW, 0:width], WH[:, i % RING, 0:width],
                                  ALU.subtract).then_inc(low_done, 1)

            def inverse_roots(dst, sums, count, n):
                dve.tensor_scalar(dst, sums, 1.0 / count, EPS, ALU.mult, ALU.add).then_inc(ms_done, 1)
                dve.wait_ge(root_done, n + 1)
                link(dve.reciprocal(dst, dst))

            def normalise(norm):
                dve.wait_ge(sq_done, TILES * (norm + 1))
                dve.wait_ge(gain_in, 16 * (norm + 1))
                inverse_roots(RSTD, SS, D, 4 * (norm // 2) + 3 * (norm % 2))
                for t in range(TILES):
                    dve.scalar_tensor_tensor(out=XN[:, t, :], in0=X[:, t, :], scalar=RSTD[:, t:t + 1], in1=GAIN,
                                             op0=ALU.mult, op1=ALU.mult).then_inc(xn_done, 1)

            def x_low(k, t, q):
                dve.wait_ge(tp_high, k + 1)
                dst = (slice(None), slice(4 * q, 4 * q + 4), slice(t * P, (t + 1) * P))
                dve.tensor_tensor(XTL[dst], TP[k % 2][:, :].rearrange("p (c n) -> p c n", c=4), XTH[dst],
                                  ALU.subtract).then_inc(tp_free, 1)

            normalise(0)
            dve.wait_ge(small_in, 32)
            link(dve.tensor_copy(POS, POS_I))
            for t in range(TILES):
                link(dve.tensor_scalar(ANG[:, t, :], INV, POS[:, t:t + 1], None, ALU.mult))
            link(dve.tensor_scalar(TURN, ANG, 1.0 / (2.0 * np.pi), ROUND, ALU.mult, ALU.add))
            link(dve.tensor_scalar(TURN, TURN, -ROUND, None, ALU.add))
            link(dve.scalar_tensor_tensor(out=RED, in0=TURN, scalar=-TWO_PI_PARTS[0], in1=ANG, op0=ALU.mult, op1=ALU.add))
            link(dve.scalar_tensor_tensor(out=RED, in0=TURN, scalar=-TWO_PI_PARTS[1], in1=RED, op0=ALU.mult, op1=ALU.add))
            link(dve.scalar_tensor_tensor(out=RED, in0=TURN, scalar=-TWO_PI_PARTS[2], in1=RED, op0=ALU.mult, op1=ALU.add))
            link(dve.tensor_scalar(RED, RED, 3.1415925, -3.1415925, ALU.min, ALU.max))
            link(dve.scalar_tensor_tensor(out=TURN, in0=RED, scalar=-1.0, in1=RED, op0=ALU.mult, op1=ALU.max))
            dve.sem_inc(rope_red, 1)
            dve.tensor_scalar(TURN, TURN, -1.0, np.pi / 2, ALU.mult, ALU.add).then_inc(rope_red, 1)
            dve.wait_ge(const_done, 1)
            link(dve.tensor_copy(IOTA[:, :], IOTA_I))
            link(dve.tensor_copy(DF, DIST))
            link(dve.tensor_scalar(CNT[:, :], DF, 128.5, None, ALU.is_lt))
            for dil in (4, 16):
                link(dve.tensor_scalar(DMOD, DIST, dil - 1, None, ALU.bitwise_and))
                link(dve.tensor_scalar(C1, DMOD, 0, None, ALU.is_equal))
                link(dve.tensor_tensor(CNT[:, :], CNT[:, :], C1, ALU.add))
            link(dve.scalar_tensor_tensor(out=CNT[:, :], in0=DF, scalar=-0.5, in1=CNT[:, :], op0=ALU.is_gt, op1=ALU.mult))
            dve.tensor_scalar(NEGU[:, :], CNT[:, :], 0.5, -BIG, ALU.is_lt, ALU.mult).then_inc(masks_done, 1)
            dve.wait_ge(tables_done, 2)

            for layer in range(LAYERS):
                m, f = MIX[layer], FFN[layer]
                for k in range(8):
                    x_low(m["tp_x"] + k, k // 4, k % 4)
                    if layer == 0:
                        low(k, NB_W, k)
                with dve.Fori(0, IN_BLOCKS) as c:
                    for j in range(IN_PIECES):
                        low(j, NB_W, m["p_in"] + j + RING, c * IN_PIECES)
                dve.wait_ge(gu_free, 2 + m["gu"] + IN_BLOCKS * TILES)
                dve.wait_ge(dilg_in, 32 * (layer + 1))
                for qk in range(2):
                    for t in range(TILES):
                        lo, hi = slice(0, DH // 2), slice(DH // 2, DH)
                        g = DIL_G[:, qk, :]
                        dve.tensor_tensor(ROPE_C[:, t, qk, lo], g[:, lo], COS[:, t, :], ALU.mult)
                        dve.tensor_tensor(ROPE_C[:, t, qk, hi], g[:, hi], COS[:, t, :], ALU.mult)
                        dve.scalar_tensor_tensor(out=ROPE_S[:, t, qk, lo], in0=g[:, hi], scalar=-1.0, in1=SIN[:, t, :],
                                                 op0=ALU.mult, op1=ALU.mult)
                        link(dve.tensor_tensor(ROPE_S[:, t, qk, hi], g[:, lo], SIN[:, t, :], ALU.mult))
                dve.wait_ge(sbg_in, 32 * (layer + 1))
                dve.tensor_scalar(SB_GAIN[:, 0:1], SB_GAIN[:, 0:1], SCALE, None, ALU.mult).then_inc(sbg_done, 1)
                for kind in range(2):
                    c0 = 3 * HEADS * DH * kind
                    qk_cols = QKV[:, :, c0:c0 + 2 * HEADS * DH]
                    link(dve.tensor_tensor(SQ, qk_cols, qk_cols, ALU.mult))
                    link(dve.tensor_reduce(HSS[:, 16 * kind:16 * kind + 16], SQ.rearrange("p t (h d) -> p (t h) d", d=DH),
                                           AX.X, ALU.add))
                inverse_roots(HSSR[:, :], HSS, DH, 4 * layer + 1)
                for kind in range(2):
                    c0 = 3 * HEADS * DH * kind
                    rs = HSSR[:, 16 * kind:16 * kind + 16]
                    for t in range(TILES):
                        v = QKV[:, t, c0:c0 + 2 * HEADS * DH].rearrange("p (h d) -> p h d", d=DH)
                        link(dve.tensor_tensor(v, v, rs[:, 8 * t:8 * t + 8].unsqueeze(2).to_broadcast([P, 8, DH]), ALU.mult))
                for t in range(TILES):
                    for qk in range(2):
                        c0 = 3 * HEADS * DH + qk * HEADS * DH
                        v = QKV[:, t, c0:c0 + HEADS * DH].rearrange("p (h d) -> p h d", d=DH)
                        t1 = RT1.rearrange("p (h d) -> p h d", d=DH)
                        t2 = RT2.rearrange("p (h d) -> p h d", d=DH)
                        half = DH // 2
                        bc = [P, HEADS, half]
                        dve.tensor_tensor(t1, v, ROPE_C[:, t, qk, :].unsqueeze(1).to_broadcast([P, HEADS, DH]), ALU.mult)
                        dve.tensor_tensor(t2[:, :, 0:half], v[:, :, half:DH],
                                          ROPE_S[:, t, qk, 0:half].unsqueeze(1).to_broadcast(bc), ALU.mult)
                        link(dve.tensor_tensor(t2[:, :, half:DH], v[:, :, 0:half],
                                               ROPE_S[:, t, qk, half:DH].unsqueeze(1).to_broadcast(bc), ALU.mult))
                        link(dve.tensor_tensor(v, t1, t2, ALU.add))
                dve.sem_inc(rope_done, 1)
                for h in range(HEADS):
                    n = HEADS * layer + h
                    b = h % 2
                    dve.wait_ge(s_ready, n + 1)
                    link(dve.tensor_tensor(WD[b], U[0][:, 0:3 * P], NEGU[:, :], ALU.add))
                    dve.tensor_reduce(MX[:, 2 * b:2 * b + 1], WD[b][:, 0:P], AX.X, ALU.max)
                    link(dve.tensor_reduce(MX[:, 2 * b + 1:2 * b + 2], WD[b][:, P:3 * P], AX.X, ALU.max))
                    dve.tensor_scalar(NMX[:, 2 * b:2 * b + 2], MX[:, 2 * b:2 * b + 2], -SCALE, None, ALU.mult).then_inc(s_max, 1)
                    dve.wait_ge(spl_done, n + 1)
                    link(dve.scalar_tensor_tensor(out=SP[b], in0=ZS[b], scalar=0.0, in1=SPL[b], op0=ALU.max, op1=ALU.add))
                    link(dve.tensor_scalar(AZ[b], ZS[b], EXP_OVERFLOW, BIG, ALU.is_gt, ALU.mult))
                    link(dve.tensor_tensor(SP[b], SP[b], AZ[b], ALU.add))
                    dve.tensor_tensor(SP[b][:, 0:P], SP[b][:, 0:P], KEEPZ[:, :], ALU.mult)
                    dve.tensor_tensor(SP[b][:, 2 * P:3 * P], SP[b][:, 2 * P:3 * P], KEEPZ[:, :], ALU.mult).then_inc(sp_done, 1)
                    dve.wait_ge(e_done, n + 1)
                    dve.tensor_tensor(WD[b][:, 0:3 * P], WD[b][:, 0:3 * P], CNT[:, :], ALU.mult).then_inc(w_done, 1)
                    dve.wait_ge(w_done, n + 1)
                    dve.tensor_reduce(DEN[:, 2 * b:2 * b + 1], WD[b][:, 0:P], AX.X, ALU.add)
                    link(dve.tensor_reduce(DEN[:, 2 * b + 1:2 * b + 2], WD[b][:, P:3 * P], AX.X, ALU.add))
                    link(dve.reciprocal(RDEN[:, 2 * b:2 * b + 2], DEN[:, 2 * b:2 * b + 2]))
                    dve.wait_ge(r_ready, n + 1)
                    link(dve.tensor_tensor(AZ[b], ZS[b], G[1][:, 0:3 * P], ALU.subtract))
                    dve.tensor_tensor(AZ[b][:, 0:P], AZ[b][:, 0:P], NEGZ[:, :], ALU.add)
                    dve.tensor_tensor(AZ[b][:, 2 * P:3 * P], AZ[b][:, 2 * P:3 * P], NEGZ[:, :], ALU.add).then_inc(az_done, 1)
                dve.wait_ge(osq_done, 2 * TILES * (layer + 1))
                dve.wait_ge(gout_in, 32 * (layer + 1))
                inverse_roots(O_RSTD, O_SS, HEADS * DH, 4 * layer + 2)
                for t in range(TILES):
                    for kind in range(2):
                        o = QKV[:, t, 3 * HEADS * DH * kind:3 * HEADS * DH * kind + HEADS * DH]
                        dve.scalar_tensor_tensor(out=o, in0=o, scalar=O_RSTD[:, 2 * t + kind:2 * t + kind + 1],
                                                 in1=GOUT[:, kind * HEADS * DH:(kind + 1) * HEADS * DH],
                                                 op0=ALU.mult, op1=ALU.mult).then_inc(on_done, 1)
                for t in range(TILES):
                    for kind in range(2):
                        k = m["tp_o"] + 2 * t + kind
                        dve.wait_ge(tp_high, k + 1)
                        dst = (slice(None), slice(HEADS * kind, HEADS * (kind + 1)), slice(t * P, (t + 1) * P))
                        dve.tensor_tensor(HTL[dst], TP[k % 2][:, :].rearrange("p (c n) -> p c n", c=4), HTH[dst],
                                          ALU.subtract).then_inc(tp_free, 1)

                def add_down(d, t, k):
                    dve.wait_ge(dn_ready, k + 1)
                    xs = X[:, t, d * NB:(d + 1) * NB]
                    dve.tensor_tensor(xs, DN[t][:, :], xs, ALU.add).then_inc(dn_free, 1)

                for d in range(OUT_BLOCKS):
                    add_down(d, 0, m["dn"] + TILES * d)
                    for j in range(OUT_PIECES):
                        i = d * OUT_PIECES + j
                        low(i, NB_W if i + RING < OUT_BLOCKS * OUT_PIECES else GU_W, m["p_out"] + i + RING)
                    add_down(d, 1, m["dn"] + TILES * d + 1)
                normalise(2 * layer + 1)
                if layer == 1:
                    dve.wait_ge(wr_high, 1)
                    dve.tensor_tensor(WRL[:, :, :], GAIN[:, 0:KD * N_EXP].rearrange("p (k e) -> p k e", k=KD), WRH[:, :, :],
                                      ALU.subtract).then_inc(wr_done, 1)
                for k in range(8):
                    x_low(f["tp_x"] + k, k // 4, k % 4)
                if layer == 1:
                    dve.wait_ge(lg_ready, 1)
                    dve.tensor_copy(LG[:, :, :], DN[0][:, 0:TILES * N_EXP].rearrange("p (t e) -> p t e", t=TILES)).then_inc(lg_done, 1)
                    dve.wait_ge(lg_done, 1)
                    sel, rank = R1[:, 3, :, :], R1[:, 2, :, :]
                    link(dve.tensor_reduce(MX[:, 0:TILES], LG[:, :, :], AX.X, ALU.max))
                    for t in range(TILES):
                        ins = dve.tensor_scalar(R1[:, 1, t, :], LG[:, t, :], MX[:, t:t + 1], None, ALU.subtract)
                    ins.then_inc(lg_done, 1)
                    for t in range(TILES):
                        mine = LG[:, t, :].unsqueeze(2).to_broadcast([P, N_EXP, N_EXP])
                        other = LG[:, t, :].unsqueeze(1).to_broadcast([P, N_EXP, N_EXP])
                        dve.tensor_tensor(RK[:, 0], mine, other, ALU.is_lt)
                        link(dve.tensor_tensor(RK[:, 1], mine, other, ALU.is_equal))
                        link(dve.tensor_tensor(RK[:, 1], RK[:, 1], BEFORE[:, :, :], ALU.mult))
                        link(dve.tensor_tensor(RK[:, 0], RK[:, 0], RK[:, 1], ALU.add))
                        link(dve.tensor_reduce(rank[:, t, :], RK[:, 0], AX.X, ALU.add))
                    dve.tensor_scalar(CHOSEN[:, :, :], rank, 1.5, None, ALU.is_lt).then_inc(chosen_done, 1)
                    dve.wait_ge(chosen_done, 1)
                    dve.wait_ge(pexp_done, 1)
                    link(dve.tensor_tensor(sel, CHOSEN[:, :, :], R1[:, 0, :, :], ALU.mult))
                    link(dve.tensor_reduce(MX[:, 0:TILES], sel, AX.X, ALU.add))
                    link(dve.reciprocal(MX[:, 0:TILES], MX[:, 0:TILES]))
                    for t in range(TILES):
                        link(dve.tensor_scalar(COMB[:, t, :], sel[:, t, :], MX[:, t:t + 1], None, ALU.mult))
                    dve.wait_ge(pos_ready, 1)
                    pos = DN[1][:, 0:TILES * N_EXP].rearrange("p (t e) -> p t e", t=TILES)
                    link(dve.scalar_tensor_tensor(out=SLOT[:, :, :], in0=pos, scalar=1.0, in1=CHOSEN[:, :, :],
                                                  op0=ALU.add, op1=ALU.mult))
                    link(dve.tensor_scalar(SLOT[:, :, :], SLOT[:, :, :], -1.0, None, ALU.add))
                    link(dve.tensor_reduce(MX[:, 0:1], DN[1][:, 2 * N_EXP:3 * N_EXP], AX.X, ALU.max))
                    dve.sem_inc(slot_done, 1)
                    dve.tensor_scalar(FLAG[:, :], MX[:, 0:1], SLOTS + 0.5, None, ALU.is_gt).then_inc(flag_done, 1)

                def ffn_slice(e):
                    def ahead(i):
                        low(i, WIDTHS[(i + RING) % SLICE_PIECES], f["piece"] + i + RING, e * SLICE_PIECES)

                    def gate_up(b, t):
                        if t == TILES - 1:
                            for j in range(GU_PIECES - 1):
                                ahead(b * GU_PIECES + j)
                        dve.wait_ge(silu_done, e * (GBLOCKS * TILES) + (b * TILES + t + 1))
                        dve.tensor_tensor(H[:, t, b * GB:(b + 1) * GB], U[t][:, 0:GB], SG[:, t, :], ALU.mult).then_inc(gu_free, 1)
                        if t == TILES - 1:
                            ahead(b * GU_PIECES + GU_PIECES - 1)

                    def h_low(b, t):
                        k = b * TILES + t
                        c0, c1 = T_AFTER[b]
                        dve.wait_ge(tp_high, e * (GBLOCKS * TILES) + (f["tp"] + k + 1))
                        dst = (slice(None), slice(c0, c1), slice(t * P, (t + 1) * P))
                        dve.tensor_tensor(HTL[dst], TP[(f["tp"] + k) % 2][:, 0:(c1 - c0) * P].rearrange("p (c n) -> p c n", n=P),
                                          HTH[dst], ALU.subtract).then_inc(tp_free, 1)

                    for b in range(GBLOCKS):
                        gate_up(b, 0)
                        if b:
                            h_low(b - 1, 1)
                        gate_up(b, 1)
                        h_low(b, 0)
                    for d in range(DBLOCKS):
                        for t in range(TILES):
                            if d == 0 and t == 0:
                                h_low(GBLOCKS - 1, 1)
                            if t == TILES - 1:
                                for j in range(DN_PIECES):
                                    ahead(GBLOCKS * GU_PIECES + d * DN_PIECES + j)
                            add_down(d, t, e * (DBLOCKS * TILES) + (f["dn"] + d * TILES + t))

                if layer == 0:
                    with dve.Fori(0, DENSE_SLICES) as e:
                        ffn_slice(e)
                    normalise(2)

            def moe_pass(n_pass):
                s = PASS[n_pass]

                def ahead(e, i, more):
                    if i + RING < SLICE_PIECES or more:
                        low(i, WIDTHS[(i + RING) % SLICE_PIECES], s["piece"] + i + RING, e * SLICE_PIECES)

                def gate_up(e, b, more=True):
                    i0 = piece_at(0, b)
                    for j in range(GU_PIECES - 1):
                        ahead(e, i0 + j, more)
                    c = b % GBLOCKS
                    dve.wait_ge(silu_done, e * GBLOCKS + (s["silu"] + b + 1))
                    dve.tensor_tensor(HM[:, c * GB:(c + 1) * GB], U[b % 2][:, 0:GB], SG[:, b % 2, :], ALU.mult).then_inc(gu_free, 1)
                    ahead(e, i0 + GU_PIECES - 1, more)

                def select(expert_index):
                    for t in range(TILES):
                        ins = dve.tensor_scalar(SEL[:, t, :], IOTA[:, :], SLOT[:, t, expert_index], None, ALU.is_equal)
                    ins.then_inc(sel_done, 1)

                def gathered_low(high, k0):
                    for q in range(KD // 4):
                        dve.wait_ge(tp_high, high + (q + 1))
                        dst = (slice(None), slice(4 * q, 4 * q + 4), slice(0, SLOTS))
                        dve.tensor_tensor(XTL[dst], TP[(k0 + q) % 2][:, :].rearrange("p (c n) -> p c n", c=4), XTH[dst],
                                          ALU.subtract).then_inc(tp_free, 1)

                def selection_transposed(count, k0):
                    for t in range(TILES):
                        dve.wait_ge(tp_ready, count + (t + 1))
                        dve.tensor_copy(SELT[:, t * P:(t + 1) * P], TP[(k0 + t) % 2][:, 0:P]).then_inc(tp_free, 1)

                def expert(e, more):
                    if more:
                        select(bass.ds(e + 1, 1))
                    for name, i, tp, high in expert_steps(more)[0]:
                        count = e * TP_MORE + (s["tp"] + tp)
                        high_count = e * HIGH_MORE + (s["high"] + high)
                        k0 = s["tp"] + tp
                        if name == "gu":
                            gate_up(e, i, more)
                        elif name == "t":
                            c0, c1 = T_AFTER[i]
                            dve.wait_ge(tp_high, high_count + 1)
                            dst = (slice(None), slice(c0, c1), slice(0, SLOTS))
                            dve.tensor_tensor(HTL[dst], TP[k0 % 2][:, 0:(c1 - c0) * P].rearrange("p (c n) -> p c n", n=P),
                                              HTH[dst], ALU.subtract).then_inc(tp_free, 1)
                        elif name == "gather":
                            gathered_low(high_count, k0)
                        elif name == "dn":
                            i0 = GBLOCKS * GU_PIECES + i * DN_PIECES
                            for j in range(DN_PIECES - 1):
                                ahead(e, i0 + j, more)
                            dve.wait_ge(y_high, e * DBLOCKS + (N_EXP * DBLOCKS * n_pass + i + 1))
                            dve.tensor_tensor(YL[i % 2], DN[i % 2][:, :].rearrange("p (c n) -> p c n", n=P), YH[i % 2],
                                              ALU.subtract).then_inc(dn_free, 1)
                            ahead(e, i0 + DN_PIECES - 1, more)
                        elif name == "sc":
                            for t in range(TILES):
                                dve.wait_ge(tp_ready, count + (t + 1))
                                gate = COMB[:, t, bass.ds(e, 1)] if more else COMB[:, t, e:e + 1]
                                xs = X[:, t, i * NB:(i + 1) * NB]
                                dve.scalar_tensor_tensor(out=xs, in0=TP[(k0 + t) % 2][:, :], scalar=gate, in1=xs,
                                                         op0=ALU.mult, op1=ALU.add).then_inc(tp_free, 1)
                        else:
                            selection_transposed(count, k0)

                if n_pass:
                    link(dve.tensor_scalar(SLOT[:, :, :], SLOT[:, :, :], -float(SLOTS), None, ALU.add))
                select(slice(0, 1))
                if n_pass:
                    for i in range(RING):
                        low(i, WIDTHS[i], s["piece"] + i)
                gathered_low(s["high0"], s["tp0"])
                gate_up(0, 0)
                selection_transposed(s["tp0"] + KD // 4, s["tp0"] + KD // 4)
                with dve.Fori(0, N_EXP - 1) as e:
                    expert(e, True)
                expert(N_EXP - 1, False)

            moe_pass(0)
            dve.wait_ge(flag_done, 1)
            with dve.If(dve.value_load(FLAG[0:1, 0:1], min_val=0, max_val=1) > 0):
                moe_pass(1)


def pieces_by_column_block(w, width):
    *lead, k, n = w.shape
    w = w.reshape(*lead, k // (2 * P), 2, P, n // width, width)
    a = len(lead)
    w = w.transpose(*range(a), a + 3, a, a + 2, a + 1, a + 4)
    return np.ascontiguousarray(w.reshape(*lead, n // width, k // (2 * P), P, 2 * width))


def gate_up_pieces(gate, up):
    s = gate.shape[0]
    w = np.stack([gate, up], 1).reshape(s, 2, KD // 2, 2, P, GBLOCKS, GB)
    return np.ascontiguousarray(w.transpose(0, 5, 2, 4, 3, 1, 6).reshape(s, GBLOCKS, KD // 2, P, GU_W))


def down_pieces(down):
    s = down.shape[0]
    w = down.reshape(s, FC, P, DBLOCKS, NB).transpose(0, 3, 2, 1, 4)
    return np.ascontiguousarray(w.reshape(s, DBLOCKS, P, FC * NB))


def kernel(**inputs):
    import concourse.bacc as _bacc
    from concourse.bass_utils import run_bass_kernel_spmd as _run

    a = {k: np.asarray(v) for k, v in inputs.items()}
    by_slice = lambda w: w[0].reshape(D, DENSE_SLICES, FE).transpose(1, 0, 2)
    laid = {
        "x": a["x"][0],
        "positions": a["positions"].reshape(TILES, P).T,
        "norm_mix": a["norm_mix"],
        "w_in": pieces_by_column_block(a["w_in"], NB),
        "q_norm_sb": a["q_norm_sb"], "k_norm_sb": a["k_norm_sb"],
        "q_norm_dil": a["q_norm_dil"], "k_norm_dil": a["k_norm_dil"],
        "out_norm_sb": a["out_norm_sb"], "out_norm_dil": a["out_norm_dil"],
        "w_out": pieces_by_column_block(a["w_out"], NB),
        "norm_ffn": a["norm_ffn"],
        "gu_dense": gate_up_pieces(by_slice(a["w_gate_dense"]), by_slice(a["w_up_dense"])),
        "down_dense": down_pieces(a["w_down_dense"][0].reshape(DENSE_SLICES, FE, D)),
        "w_router": a["w_router"][0].reshape(KD, P, N_EXP).transpose(1, 0, 2).reshape(P, KD * N_EXP),
        "gu_moe": gate_up_pieces(a["w_gate_moe"][0], a["w_up_moe"][0]),
        "down_moe": down_pieces(a["w_down_moe"][0]),
        "inv_freq": (ROPE_THETA ** (-np.arange(0, DH, 2, dtype=np.float32) / np.float32(DH))).astype(np.float32),
    }
    nc = _bacc.Bacc("TRN2", target_bir_lowering=False, num_devices=1, dynamic_dma_scratch_size=4096)
    arrays, args = {}, {}
    for name, v in laid.items():
        v = np.ascontiguousarray(v)
        arrays[f"in_{name}"] = v
        args[name] = nc.dram_tensor(f"in_{name}", v.shape, mybir.dt.from_np(v.dtype), kind="ExternalInput").ap()
    args["out"] = nc.dram_tensor("out_x", (SEQ, D), F32, kind="ExternalOutput").ap()
    trunk(nc, **args)
    r = _run(nc, [arrays], core_ids=[0])
    return r.results[0]["out_x"].reshape(1, SEQ, D)
```

```python
from contextlib import ExitStack

import numpy as np
import concourse.bass as bass
from concourse import mybir

F32 = mybir.dt.float32
F32R = mybir.dt.float32r
I32 = mybir.dt.int32
ALU = mybir.AluOpType
ACT = mybir.ActivationFunctionType
AX = mybir.AxisListType

P = 128
SEQ = 256
TILES = SEQ // P
D = 2048
KD = D // P
HEADS = 4
DH = 128
D_MIX = 2 * HEADS * DH
D_IN = 3 * D_MIX
LAYERS = 2
N_EXP = 8
FE = 1408
FC = FE // P
DENSE_SLICES = 4
EPS = 1e-6
BIG = 1e30
EXP_OVERFLOW = 88.72283
SCALE = DH ** -0.5
ROPE_THETA = 10000.0

GB = 352
GBLOCKS = FE // GB
NB = 512
GU_W = 2 * 2 * GB
NB_W = 2 * NB
DN_PIECES = (FC + 1) // 2
RAW = 4
LATER = 3
RING = 8

IN_BLOCKS, OUT_BLOCKS, DBLOCKS = D_IN // NB, D // NB, D // NB
IN_PIECES, OUT_PIECES, GU_PIECES = KD // 2, D_MIX // P // 2, KD // 2
QK_BLOCKS = (0, 1, 3, 4)
X_BLOCKS = TILES * (D // NB)
ROOTS = 7
SLICE_PIECES = GBLOCKS * GU_PIECES + DBLOCKS * DN_PIECES
SLICE_USED = GBLOCKS * (GU_PIECES - 1) + DBLOCKS * (DN_PIECES - 1)
T_AFTER = [(0, 2), (2, 5), (5, 8), (8, 11)]

SLOTS = P
PASSES = SEQ // SLOTS

TWO_PI_PARTS = (6.28125, 0.0019350051879882812, 3.019916e-07)
ROUND = 12582912.0


BETWEEN = {
    ("gu", 1, 5): [("t", 0, 0)], ("gu", 2, 5): [("t", 1, 0)], ("gu", 3, 5): [("t", 2, 0)],
    ("dn", 0, 1): [("t", 3, 0)], ("dn", 0, 4): [("gather", 0, 0)], ("dn", 1, 0): [("gather", 1, 0)],
    ("dn", 1, 2): [("gather", 2, 0)], ("dn", 1, 4): [("gather", 3, 0)],
    ("dn", 2, 0): [("sc", 0, 0)], ("dn", 2, 2): [("sc", 0, 1)], ("dn", 3, 0): [("sc", 1, 0)], ("dn", 3, 1): [("sc", 1, 1)],
    ("dn", 3, 4): [("sc", 2, 0)], ("dn", 3, 5): [("sc", 2, 1)],
    ("gu", GBLOCKS, 3): [("sc", 3, 0)], ("gu", GBLOCKS, 5): [("sc", 3, 1)],
    ("gu", GBLOCKS, 6): [("st", 0, 0)], ("gu", GBLOCKS, 7): [("st", 1, 0)],
}


def expert_steps(more):
    order = []
    for kind, b, j in ([("gu", b, j) for b in range(1, GBLOCKS) for j in range(GU_PIECES)]
                       + [("dn", d, j) for d in range(DBLOCKS) for j in range(DN_PIECES)]
                       + [("gu", GBLOCKS, j) for j in range(GU_PIECES)]):
        order += [(kind, b, j)] + BETWEEN.get((kind, b, j), [])
    tp = high = 0
    steps = []
    for kind, b, j in order:
        if not more and (kind in ("gather", "st") or (kind, b) == ("gu", GBLOCKS)):
            continue
        steps.append((kind, b, j, tp, high))
        tp += kind in ("t", "gather", "sc", "st")
        high += kind in ("t", "gather")
    return steps, tp, high


def down_width(j):
    return min(2, FC - 2 * j) * NB


def trunk(nc, x, positions, norm_mix, w_in, q_norm_sb, k_norm_sb, q_norm_dil, k_norm_dil, out_norm_sb,
          out_norm_dil, w_out, norm_ffn, gu_dense, down_dense, w_router, gu_moe, down_moe, inv_freq, out):
    FFN = [dict(), dict()]
    n_piece = n_gu = n_dn = n_tp = n_used = 0
    MIX = []
    for layer in range(LAYERS):
        MIX.append(dict(p_in=n_piece, p_out=n_piece + IN_BLOCKS * IN_PIECES, gu=n_gu, dn=n_dn,
                        tp_x=n_tp, tp_o=n_tp + 8, used_in=n_used, used_out=n_used + IN_BLOCKS * (IN_PIECES - 1)))
        n_used += IN_BLOCKS * (IN_PIECES - 1) + OUT_BLOCKS * (OUT_PIECES - 1)
        n_piece += IN_BLOCKS * IN_PIECES + OUT_BLOCKS * OUT_PIECES
        n_gu += IN_BLOCKS * TILES
        n_dn += OUT_BLOCKS * TILES
        n_tp += 12
        f = FFN[layer]
        f.update(piece=n_piece, gu=n_gu, dn=n_dn, tp_x=n_tp, tp=n_tp + 8, used=n_used)
        if layer == 0:
            n_piece += DENSE_SLICES * SLICE_PIECES
            n_used += DENSE_SLICES * SLICE_USED
            n_gu += DENSE_SLICES * GBLOCKS * TILES
            n_dn += DENSE_SLICES * DBLOCKS * TILES
            n_tp += 8 + DENSE_SLICES * GBLOCKS * TILES
    TP_MORE, HIGH_MORE = expert_steps(True)[1:]
    TP_LAST, HIGH_LAST = expert_steps(False)[1:]
    n_tp += 8
    n_high, n_silu = n_tp, DENSE_SLICES * GBLOCKS * TILES
    PASS = []
    for _ in range(PASSES):
        PASS.append(dict(piece=n_piece, used=n_used, gu=n_gu, dn=n_dn, tp0=n_tp, tp=n_tp + KD // 4 + TILES,
                         high0=n_high, high=n_high + KD // 4, silu=n_silu))
        n_piece += N_EXP * SLICE_PIECES
        n_used += N_EXP * SLICE_USED
        n_gu += N_EXP * GBLOCKS
        n_dn += N_EXP * DBLOCKS
        n_silu += N_EXP * GBLOCKS
        n_tp += KD // 4 + TILES + (N_EXP - 1) * TP_MORE + TP_LAST
        n_high += KD // 4 + (N_EXP - 1) * HIGH_MORE + HIGH_LAST

    with ExitStack() as ctx:
        def sb(name, shape, dt=F32, where=ctx):
            return where.enter_context(nc.sbuf_tensor(name, shape, dt))

        def sem(name):
            return ctx.enter_context(nc.semaphore(name))

        RAWS = sb("raw_pieces", [P, RAW, GU_W])
        WH = sb("w_high", [P, RING, GU_W], F32R)
        WL = sb("w_low", [P, RING, GU_W], F32R)
        X = sb("x_resid", [P, TILES, D])
        TOK = sb("token_major", [P, TILES * D_IN])
        with ExitStack() as scratch:
            PRE = sb("heads_scratch", [P, 2 * FC * SEQ], F32, scratch)
        HTH = sb("hT_high", [P, FC, SEQ], F32R)
        HTL = sb("hT_low", [P, FC, SEQ], F32R)
        SG = sb("silu_gate", [P, TILES, GB])
        IDN = sb("identity", [P, P])
        INCL = sb("incl", [P, P])
        ONES = sb("ones", [P, P])
        NEGZ = sb("neg_not_strict", [P, P])
        KEEPZ = sb("keep_strict", [P, P])
        CNT = sb("branch_count", [P, 3 * P])
        NEGU = sb("neg_union", [P, 3 * P])
        COS = sb("rope_cos", [P, TILES, DH // 2])
        SIN = sb("rope_sin", [P, TILES, DH // 2])
        WRH = sb("router_high", [P, KD, N_EXP], F32R)
        WRL = sb("router_low", [P, KD, N_EXP], F32R)
        COMB = sb("expert_gates", [P, TILES, N_EXP])
        SMALL = sb("small", [P, 64])
        XN = TOK[:, 0:TILES * D].rearrange("p (t n) -> p t n", t=TILES)
        GAIN = TOK[:, TILES * D:TILES * D + D]
        QKV = TOK[:, :].rearrange("p (t n) -> p t n", t=TILES)
        H = TOK[:, 0:TILES * FE].rearrange("p (t n) -> p t n", t=TILES)
        HM = GAIN[:, 0:FE]
        with ExitStack() as scratch:
            ATT = sb("mixer_scratch", [P, 2 * KD * SEQ], F32, scratch)
        XTH = sb("xT_high", [P, KD, SEQ], F32R)
        XTL = sb("xT_low", [P, KD, SEQ], F32R)

        at = [0]

        def part(n, where=ATT):
            at[0] += n
            return where[:, at[0] - n:at[0]]

        GOUT = part(D_MIX)
        heads_at = at[0]
        QKT = [[part(4 * P) for _ in range(2)] for _ in range(2)]
        ZS, SPL, SP, AZ, WD, WDT = ([part(3 * P) for _ in range(2)] for _ in range(6))
        at[0] = 0
        ROPE_C, ROPE_S = (part(2 * TILES * DH, PRE).rearrange("p (t q d) -> p t q d", t=TILES, q=2) for _ in range(2))
        DIL_G = part(2 * DH, PRE).rearrange("p (q d) -> p q d", q=2)
        SQ = part(TILES * NB, PRE).rearrange("p (t n) -> p t n", t=TILES)
        RT1, RT2 = part(HEADS * DH, PRE), part(HEADS * DH, PRE)
        SETUP = PRE[:, at[0]:]
        ANG, TURN, RED = (SETUP[:, i * P:(i + 1) * P].rearrange("p (t d) -> p t d", t=TILES) for i in range(3))
        INV = SETUP[:, 3 * P:3 * P + DH // 2]
        POS_I = SETUP[:, 4 * P:4 * P + TILES].bitcast(I32)
        POS = SETUP[:, 4 * P + 4:4 * P + 4 + TILES]
        DIST = SETUP[:, 5 * P:8 * P].bitcast(I32)
        IOTA_I = SETUP[:, 17 * P:18 * P].bitcast(I32)
        DMOD = SETUP[:, 8 * P:11 * P].bitcast(I32)
        DF, C1 = SETUP[:, 11 * P:14 * P], SETUP[:, 14 * P:17 * P]
        SS, RSTD = SMALL[:, 0:2], SMALL[:, 2:4]
        SSP = sb("block_square_sums", [P, TILES * DBLOCKS])
        JUNK = SG[:, :, :].rearrange("p t n -> p (t n)")[:, 0:NB]
        SB_GAIN = SMALL[:, 4:6]
        O_SS, O_RSTD = SMALL[:, 6:10], SMALL[:, 10:14]
        HSS = SMALL[:, 14:46]
        MX, NMX, DEN, RDEN = (SMALL[:, 46 + 4 * i:50 + 4 * i] for i in range(4))
        HSSR = sb("head_rstd", [P, 32])
        LG = sb("logits", [P, TILES, N_EXP])
        RK = sb("rank_terms", [P, 2, N_EXP, N_EXP])
        BEFORE = sb("earlier_expert", [P, N_EXP, N_EXP])
        R1 = sb("router_rows", [P, 4, TILES, N_EXP])
        CHOSEN = sb("chosen", [P, TILES, N_EXP])
        SLOT = sb("slot", [P, TILES, N_EXP])
        IOTA = sb("iota_slots", [P, SLOTS])
        SEL = sb("selection", [P, TILES, SLOTS])
        LGT = SEL[:, :, :].rearrange("p t s -> p (t s)")[0:N_EXP, :]
        SELT = sb("selection_T", [P, SEQ], F32R)
        FLAG = sb("another_pass", [P, 1], I32)
        YH = [HTH[:, 4 * i:4 * i + 4, P:2 * P] for i in range(2)]
        YL = [HTL[:, 4 * i:4 * i + 4, P:2 * P] for i in range(2)]

        def bank(name):
            return ctx.enter_context(nc.psum_tensor(name, [P, 512], F32))
        G = [bank("gate0"), bank("gate1")]
        U = [bank("up0"), bank("up1")]
        DN = [bank("down0"), bank("down1")]
        TP = [bank("transpose0"), bank("transpose1")]

        raw_full = [sem(f"raw_full{i}") for i in range(RAW)]
        high_done = sem("high_done")
        low_done = sem("low_done")
        used = sem("piece_used")
        gu_ready = sem("gu_ready")
        gu_free = sem("gu_free")
        silu_done = sem("silu_done")
        dn_ready = sem("dn_ready")
        dn_free = sem("dn_free")
        tp_ready = sem("tp_ready")
        tp_high = sem("tp_high")
        tp_free = sem("tp_free")
        x_in = [sem(f"x_in{t}") for t in range(TILES)]
        small_in = sem("small_in")
        gain_in = sem("gain_in")
        gain_used = sem("gain_used")
        router_in = sem("router_in")
        const_done = sem("const_done")
        tables_done = sem("tables_done")
        masks_done = sem("masks_done")
        pool_chain = sem("pool_chain")
        dve_chain = sem("dve_chain")
        act_chain = sem("act_chain")
        rope_red = sem("rope_reduced")
        sq_done = sem("sq_done")
        xg_done = sem("xg_done")
        ms_done = sem("mean_square_done")
        root_done = sem("root_done")
        xn_done = sem("xn_done")
        dilg_in, gout_in, sbg_in = sem("dilg_in"), sem("gout_in"), sem("sbg_in")
        rope_done = sem("rope_done")
        sbg_done = sem("sbg_done")
        qk_t = sem("qk_transposed")
        qk_ev = sem("qk_evacuated")
        z_ready, z_copied, spl_done = sem("z_ready"), sem("z_copied"), sem("spl_done")
        sp_done, r_ready, az_done, a_done = sem("sp_done"), sem("r_ready"), sem("az_done"), sem("a_done")
        osb_ready, osb_done = sem("osb_ready"), sem("osb_done")
        s_ready, s_max, e_done = sem("s_ready"), sem("s_max"), sem("e_done")
        w_done, wt_ready, wt_done = sem("w_done"), sem("wt_ready"), sem("wt_done")
        odil_ready, odil_done = sem("odil_ready"), sem("odil_done")
        osq_done, on_done = sem("osq_done"), sem("on_done")
        wr_high, wr_done = sem("wr_high"), sem("wr_done")
        lgt_ready, lgt_done = sem("lgt_ready"), sem("lgt_done")
        lg_ready, lg_done, pexp_done, comb_done = sem("lg_ready"), sem("lg_done"), sem("pexp_done"), sem("comb_done")
        chosen_done, pos_ready, slot_done = sem("chosen_done"), sem("pos_ready"), sem("slot_done")
        flag_done = sem("flag_done")
        sel_done = sem("sel_done")
        y_high = sem("y_high")
        stored = sem("stored")

        block = ctx.enter_context(nc.Block())

        def slice_pieces():
            return ([("gu", b, j, GU_W) for b in range(GBLOCKS) for j in range(GU_PIECES)]
                    + [("dn", d, j, down_width(j)) for d in range(DBLOCKS) for j in range(DN_PIECES)])

        def piece_at(piece0, b):
            return piece0 + (b * GU_PIECES if b < GBLOCKS else SLICE_PIECES)

        def used_at(used0, b):
            return used0 + (b * (GU_PIECES - 1) if b < GBLOCKS else SLICE_USED)

        WIDTHS = [w for _, _, _, w in slice_pieces()]

        @block.sync
        def _(sp):
            def load(slot, width, src, piece):
                if isinstance(piece, int):
                    if piece >= RAW:
                        sp.wait_ge(low_done, piece - RAW + 1)
                else:
                    sp.wait_ge(low_done, piece - (RAW - 1))
                sp.dma_start(RAWS[:, slot, 0:width], src).then_inc(raw_full[slot], 16)

            def stream_slice(gu, down, e, piece0):
                for i, (kind, b, j, width) in enumerate(slice_pieces()):
                    if kind == "gu":
                        src = gu[bass.ds(e, 1), b, j].rearrange("o p n -> (o p) n")
                    else:
                        src = down[bass.ds(e, 1), b, :, j * NB_W:j * NB_W + width].rearrange("o p n -> (o p) n")
                    load(i % RAW, width, src, e * SLICE_PIECES + (piece0 + i))

            for t in range(TILES):
                sp.dma_start(X[:, t, :], x[t * P:(t + 1) * P, :]).then_inc(x_in[t], 16)
            for layer in range(LAYERS):
                m, f = MIX[layer], FFN[layer]
                for c in range(IN_BLOCKS):
                    for j in range(IN_PIECES):
                        n = m["p_in"] + c * IN_PIECES + j
                        load(n % RAW, NB_W, w_in[layer, c, j], n)
                for d in range(OUT_BLOCKS):
                    for j in range(OUT_PIECES):
                        n = m["p_out"] + d * OUT_PIECES + j
                        load(n % RAW, NB_W, w_out[layer, d, j], n)
                if layer == 0:
                    with sp.Fori(0, DENSE_SLICES) as e:
                        stream_slice(gu_dense, down_dense, e, f["piece"])
            with sp.Fori(0, N_EXP) as e:
                stream_slice(gu_moe, down_moe, e, PASS[0]["piece"])
            sp.wait_ge(flag_done, 1)
            with sp.If(sp.value_load(FLAG[0:1, 0:1], min_val=0, max_val=1) > 0):
                with sp.Fori(0, N_EXP) as e:
                    stream_slice(gu_moe, down_moe, e, PASS[1]["piece"])
                sp.wait_ge(tp_free, n_tp)
            last = PASS[0]["tp"] + (N_EXP - 1) * TP_MORE
            for kind, d, t, tp, _ in expert_steps(False)[0]:
                if kind == "sc":
                    sp.wait_ge(tp_free, last + tp + 1)
                    sp.dma_start(out[t * P:(t + 1) * P, d * NB:(d + 1) * NB],
                                 X[:, t, d * NB:(d + 1) * NB]).then_inc(stored, 16)
            sp.wait_ge(stored, 16 * DBLOCKS * TILES)

        @block.gpsimd
        def _(pool):
            n = [0]

            def link(ins):
                n[0] += 1
                ins.then_inc(pool_chain, 1)
                pool.wait_ge(pool_chain, n[0])

            pool.dma_start(GAIN, norm_mix[0].partition_broadcast(P)).then_inc(gain_in, 16)
            pool.dma_start(INV, inv_freq.partition_broadcast(P)).then_inc(small_in, 16)
            pool.dma_start(POS_I, positions).then_inc(small_in, 16)
            link(pool.memset(IDN[:, :], 0.0))
            link(pool.affine_select(out=IDN[:, :], in_=IDN[:, :], compare_op=ALU.not_equal, fill=1.0, base=0,
                                    pattern=[[-1, P]], channel_multiplier=1))
            link(pool.memset(ONES[:, :], 1.0))
            link(pool.affine_select(out=INCL[:, :], in_=ONES[:, :], compare_op=ALU.is_ge, fill=0.0, base=0,
                                    pattern=[[-1, P]], channel_multiplier=1))
            link(pool.affine_select(out=KEEPZ[:, :], in_=ONES[:, :], compare_op=ALU.is_gt, fill=0.0, base=0,
                                    pattern=[[1, P]], channel_multiplier=-1))
            link(pool.memset(NEGZ[:, :], 0.0))
            link(pool.affine_select(out=NEGZ[:, :], in_=NEGZ[:, :], compare_op=ALU.is_gt, fill=-BIG, base=0,
                                    pattern=[[1, P]], channel_multiplier=-1))
            link(pool.iota(DIST[:, 0:P], [[-1, P]], base=0, channel_multiplier=1))
            link(pool.iota(DIST[:, P:3 * P], [[-1, 2 * P]], base=P, channel_multiplier=1))
            link(pool.iota(IOTA_I, [[1, SLOTS]], base=0, channel_multiplier=0))
            link(pool.memset(BEFORE[:, :, :], 1.0))
            pool.affine_select(out=BEFORE[:, :, :], in_=BEFORE[:, :, :], compare_op=ALU.is_gt, fill=0.0, base=0,
                               pattern=[[1, N_EXP], [-1, N_EXP]], channel_multiplier=0).then_inc(const_done, 1)
            for layer in range(LAYERS):
                m = MIX[layer]
                if layer:
                    pool.wait_ge(dn_ready, m["dn"])
                pool.dma_start(DIL_G[:, 0, :], q_norm_dil[layer].partition_broadcast(P)).then_inc(dilg_in, 16)
                pool.dma_start(DIL_G[:, 1, :], k_norm_dil[layer].partition_broadcast(P)).then_inc(dilg_in, 16)
                if layer:
                    pool.wait_ge(qk_ev, 2 * HEADS * layer)
                pool.dma_start(SB_GAIN[:, 0:1], q_norm_sb[layer].rearrange("(p o) -> p o", o=1)).then_inc(sbg_in, 16)
                pool.dma_start(SB_GAIN[:, 1:2], k_norm_sb[layer].rearrange("(p o) -> p o", o=1)).then_inc(sbg_in, 16)
                pool.wait_ge(gu_ready, m["gu"] + IN_BLOCKS * TILES)
                pool.dma_start(GOUT[:, 0:HEADS * DH], out_norm_sb[layer].partition_broadcast(P)).then_inc(gout_in, 16)
                pool.dma_start(GOUT[:, HEADS * DH:], out_norm_dil[layer].partition_broadcast(P)).then_inc(gout_in, 16)
                pool.wait_ge(tp_ready, m["tp_o"] + 4)
                pool.dma_start(GAIN, norm_ffn[layer].partition_broadcast(P)).then_inc(gain_in, 16)
                if layer + 1 < LAYERS:
                    pool.wait_ge(xg_done, X_BLOCKS * (2 * layer + 2))
                    pool.dma_start(GAIN, norm_mix[layer + 1].partition_broadcast(P)).then_inc(gain_in, 16)
            pool.wait_ge(xg_done, X_BLOCKS * 2 * LAYERS)
            pool.dma_start(GAIN[:, 0:KD * N_EXP], w_router).then_inc(router_in, 16)
            for s, v in ((gain_in, 16 * 2 * LAYERS), (small_in, 32), (router_in, 16)):
                pool.wait_ge(s, v)

        @block.tensor
        def _(pe):
            def three(out_ap, left, ls, right, rs, first, last):
                (lh, ll), (rh, rl) = left, right
                pe.matmul(out_ap, lh[ls], rh[rs], start=first, stop=False)
                pe.matmul(out_ap, lh[ls], rl[rs], start=False, stop=False)
                return pe.matmul(out_ap, ll[ls], rh[rs], start=False, stop=last)

            def transposes(k, src, chunks):
                for i, c in enumerate(chunks):
                    ins = pe.transpose(TP[k % 2][:, i * P:(i + 1) * P], src[:, c * P:(c + 1) * P], IDN[:, :])
                ins.then_inc(tp_ready, 1)

            def x_transposes(norm, tp):
                for t in range(TILES):
                    for q in range(4):
                        pe.wait_ge(xn_done, X_BLOCKS * norm + 4 * t + q + 1)
                        k = tp + 4 * t + q
                        if k >= 2:
                            pe.wait_ge(tp_free, k - 1)
                        transposes(k, XN[:, t, :], range(4 * q, 4 * q + 4))

            def project(t, slot0, pieces, chunks, piece0, banks, act, last_tile, shift=0):
                for j in range(pieces):
                    slot = (slot0 + j) % RING
                    if t == 0:
                        pe.wait_ge(low_done, piece0 + (j + 1))
                    k2 = min(2, chunks - 2 * j)
                    for i in range(k2):
                        k = 2 * j + i
                        first, last = k == 0, k == chunks - 1
                        left = [a[:, k, t * P:(t + 1) * P] for a in act]
                        for half in range(2):
                            for n, (b, lo, hi) in enumerate(banks):
                                right = [w[:, slot, i * (GU_W // 2 if len(banks) == 2 else NB) + lo:
                                           i * (GU_W // 2 if len(banks) == 2 else NB) + hi] for w in (WH, WL)]
                                if half == 0:
                                    pe.matmul(b, left[0], right[0], start=first, stop=False)
                                    ins = pe.matmul(b, left[0], right[1], start=False, stop=False)
                                else:
                                    ins = pe.matmul(b, left[1], right[0], start=False, stop=last)
                    if last_tile and j < pieces - 1:
                        ins.then_inc(used, 1)
                return ins

            pe.wait_ge(const_done, 1)
            for layer in range(LAYERS):
                m, f = MIX[layer], FFN[layer]
                x_transposes(2 * layer, m["tp_x"])
                pe.wait_ge(tp_free, m["tp_x"] + 8)
                with pe.Fori(0, IN_BLOCKS) as c:
                    for t in range(TILES):
                        pe.wait_ge(gu_free, c * TILES + (m["gu"] + t + 1))
                        ins = project(t, 0, IN_PIECES, KD, c * IN_PIECES + m["p_in"], [(G[t][:, :], 0, NB)],
                                      (XTH, XTL), t == TILES - 1)
                        ins.then_inc(gu_ready, 1)
                pe.wait_ge(rope_done, layer + 1)

                def turned(h):
                    n = HEADS * layer + h
                    for kind in range(2):
                        col = 3 * HEADS * DH * kind + h * DH
                        if n:
                            pe.wait_ge(qk_ev, 2 * (n - 1) + kind + 1)
                        for qk in range(2):
                            for t in range(TILES):
                                ins = pe.transpose(TP[kind][:, (2 * qk + t) * P:(2 * qk + t + 1) * P],
                                                   QKV[:, t, col + qk * HEADS * DH:col + qk * HEADS * DH + DH], IDN[:, :])
                        ins.then_inc(qk_t, 1)

                def scores(h):
                    n, b = HEADS * layer + h, h % 2
                    qs, ks = QKT[0][b][:, 0:2 * P], QKT[0][b][:, 2 * P:4 * P]
                    qd, kd = QKT[1][b][:, 0:2 * P], QKT[1][b][:, 2 * P:4 * P]
                    pe.wait_ge(qk_ev, 2 * n + 1)
                    if n:
                        pe.wait_ge(z_copied, n)
                    pe.matmul(G[0][:, 0:2 * P], ks[:, 0:P], qs, start=True, stop=True)
                    pe.matmul(G[0][:, 2 * P:3 * P], ks[:, P:2 * P], qs[:, P:2 * P], start=True, stop=True).then_inc(z_ready, 1)
                    pe.wait_ge(qk_ev, 2 * n + 2)
                    if n:
                        pe.wait_ge(s_max, n)
                    pe.matmul(U[0][:, 0:P], qd[:, 0:P], kd[:, 0:P], start=True, stop=True)
                    pe.matmul(U[0][:, P:3 * P], qd[:, P:2 * P], kd, start=True, stop=True).then_inc(s_ready, 1)

                def suffix_sums(h):
                    n, b = HEADS * layer + h, h % 2
                    pe.wait_ge(sp_done, n + 1)
                    if n:
                        pe.wait_ge(az_done, n)
                    sp_b = SP[b]
                    pe.matmul(G[1][:, 0:2 * P], INCL[:, :], sp_b[:, 0:2 * P], start=True, stop=False)
                    pe.matmul(G[1][:, P:2 * P], ONES[:, :], sp_b[:, 2 * P:3 * P], start=False, stop=True)
                    pe.matmul(G[1][:, 2 * P:3 * P], INCL[:, :], sp_b[:, 2 * P:3 * P], start=True, stop=True).then_inc(r_ready, 1)

                def weights_transposed(h):
                    n, b = HEADS * layer + h, h % 2
                    pe.wait_ge(w_done, n + 1)
                    if n:
                        pe.wait_ge(wt_done, n)
                    for i in range(3):
                        ins = pe.transpose(U[1][:, i * P:(i + 1) * P], WD[b][:, i * P:(i + 1) * P], IDN[:, :])
                    ins.then_inc(wt_ready, 1)

                def values(h):
                    n, b = HEADS * layer + h, h % 2
                    for w, bnk, done, free, ready, kind in ((AZ[b], DN[0], a_done, osb_done, osb_ready, 0),
                                                            (WDT[b], DN[1], wt_done, odil_done, odil_ready, 1)):
                        v = 3 * HEADS * DH * kind + 2 * HEADS * DH + h * DH
                        pe.wait_ge(done, n + 1)
                        if n:
                            pe.wait_ge(free, n)
                        pe.matmul(bnk[:, 0:P], w[:, 0:P], QKV[:, 0, v:v + DH], start=True, stop=True)
                        pe.matmul(bnk[:, P:2 * P], w[:, P:2 * P], QKV[:, 0, v:v + DH], start=True, stop=False)
                        pe.matmul(bnk[:, P:2 * P], w[:, 2 * P:3 * P], QKV[:, 1, v:v + DH], start=False, stop=True).then_inc(ready, 1)

                turned(0)
                scores(0)
                for h in range(HEADS):
                    if h + 1 < HEADS:
                        turned(h + 1)
                    suffix_sums(h)
                    weights_transposed(h)
                    if h + 1 < HEADS:
                        scores(h + 1)
                    values(h)
                for t in range(TILES):
                    for kind in range(2):
                        k = m["tp_o"] + 2 * t + kind
                        pe.wait_ge(on_done, 2 * TILES * layer + 2 * t + kind + 1)
                        pe.wait_ge(tp_free, k - 1)
                        transposes(k, QKV[:, t, 3 * HEADS * DH * kind:], range(HEADS))
                pe.wait_ge(tp_free, m["tp_o"] + 4)
                for d in range(OUT_BLOCKS):
                    for t in range(TILES):
                        n = m["dn"] + TILES * d + t
                        pe.wait_ge(dn_free, n + 1)
                        ins = project(t, d * OUT_PIECES, OUT_PIECES, D_MIX // P, m["p_out"] + d * OUT_PIECES,
                                      [(DN[t][:, :], 0, NB)], (HTH, HTL), t == TILES - 1)
                        ins.then_inc(dn_ready, 1)
                x_transposes(2 * layer + 1, f["tp_x"])
                pe.wait_ge(tp_free, f["tp_x"] + 8)
                if layer == 1:
                    pe.wait_ge(wr_done, 1)
                    for k in range(KD):
                        ks = (slice(None), k, slice(None))
                        ins = three(DN[0][0:N_EXP, 0:SEQ], (WRH, WRL), ks, (XTH, XTL), ks, k == 0, k == KD - 1)
                    ins.then_inc(lgt_ready, 1)
                    pe.wait_ge(lgt_done, 1)
                    for t in range(TILES):
                        ins = pe.transpose(DN[1][:, t * N_EXP:(t + 1) * N_EXP], LGT[:, t * P:(t + 1) * P],
                                           IDN[0:N_EXP, 0:N_EXP])
                    ins.then_inc(lg_ready, 1)
                    pe.wait_ge(lg_done, 1)

                def ffn_slice(e):
                    def gate_up(b, t):
                        pe.wait_ge(gu_free, e * (GBLOCKS * TILES) + (f["gu"] + b * TILES + t + 1))
                        ins = project(t, b * GU_PIECES, GU_PIECES, KD, e * SLICE_PIECES + (f["piece"] + b * GU_PIECES),
                                      [(G[t][:, 0:GB], 0, GB), (U[t][:, 0:GB], GB, 2 * GB)], (XTH, XTL), t == TILES - 1)
                        ins.then_inc(gu_ready, 1)

                    def h_transposes(b, t):
                        k = b * TILES + t
                        pe.wait_ge(gu_free, e * (GBLOCKS * TILES) + (f["gu"] + k + 3))
                        pe.wait_ge(tp_free, e * (GBLOCKS * TILES) + (f["tp"] + k - 1))
                        transposes(f["tp"] + k, H[:, t, :], range(*T_AFTER[b]))

                    def down(d, t):
                        k = e * (DBLOCKS * TILES) + (f["dn"] + d * TILES + t)
                        pe.wait_ge(dn_free, k + 1)
                        if d == 0:
                            pe.wait_ge(tp_free, e * (GBLOCKS * TILES) + (f["tp"] + (GBLOCKS - 1) * TILES + t + 1))
                        ins = project(t, GBLOCKS * GU_PIECES + d * DN_PIECES, DN_PIECES, FC,
                                      e * SLICE_PIECES + (f["piece"] + GBLOCKS * GU_PIECES + d * DN_PIECES),
                                      [(DN[t][:, :], 0, NB)], (HTH, HTL), t == TILES - 1)
                        ins.then_inc(dn_ready, 1)

                    for b in range(GBLOCKS):
                        gate_up(b, 0)
                        if b:
                            h_transposes(b - 1, 1)
                        gate_up(b, 1)
                        h_transposes(b, 0)
                    down(0, 0)
                    h_transposes(GBLOCKS - 1, 1)
                    for d in range(DBLOCKS):
                        if d:
                            down(d, 0)
                        down(d, 1)

                if layer == 0:
                    with pe.Fori(0, DENSE_SLICES) as e:
                        ffn_slice(e)

            pe.wait_ge(chosen_done, 1)
            pe.matmul(DN[1][:, 0:N_EXP], KEEPZ[:, :], CHOSEN[:, 0, :], start=True, stop=True)
            pe.matmul(DN[1][:, N_EXP:2 * N_EXP], ONES[:, :], CHOSEN[:, 0, :], start=True, stop=False)
            pe.matmul(DN[1][:, N_EXP:2 * N_EXP], KEEPZ[:, :], CHOSEN[:, 1, :], start=False, stop=True)
            pe.matmul(DN[1][:, 2 * N_EXP:3 * N_EXP], ONES[:, :], CHOSEN[:, 0, :], start=True, stop=False)
            pe.matmul(DN[1][:, 2 * N_EXP:3 * N_EXP], ONES[:, :], CHOSEN[:, 1, :], start=False, stop=True).then_inc(pos_ready, 1)
            pe.wait_ge(slot_done, 1)

            def moe_pass(n_pass):
                s = PASS[n_pass]

                def gate_up(e, b, j):
                    if j == 0:
                        pe.wait_ge(gu_free, e * GBLOCKS + (s["gu"] + b + 1))
                    n, slot = b % 2, j % RING
                    pe.wait_ge(low_done, e * SLICE_PIECES + (piece_at(s["piece"], b) + j + 1))
                    for i in range(2):
                        k = 2 * j + i
                        for bnk, lo in ((G[n], 0), (U[n], GB)):
                            wh, wl = (w[:, slot, i * 2 * GB + lo:i * 2 * GB + lo + GB] for w in (WH, WL))
                            pe.matmul(bnk[:, 0:GB], XTH[:, k, 0:SLOTS], wh, start=k == 0, stop=False)
                            pe.matmul(bnk[:, 0:GB], XTH[:, k, 0:SLOTS], wl, start=False, stop=False)
                            ins = pe.matmul(bnk[:, 0:GB], XTL[:, k, 0:SLOTS], wh, start=False, stop=k == KD - 1)
                    ins.then_inc(used if j < GU_PIECES - 1 else gu_ready, 1)

                def down(e, d, j):
                    if j == 0:
                        pe.wait_ge(dn_free, e * DBLOCKS + (s["dn"] + d + 1))
                    i_piece = GBLOCKS * GU_PIECES + d * DN_PIECES + j
                    slot = i_piece % RING
                    pe.wait_ge(low_done, e * SLICE_PIECES + (s["piece"] + i_piece + 1))
                    for i in range(min(2, FC - 2 * j)):
                        k = 2 * j + i
                        wh, wl = (w[:, slot, i * NB:(i + 1) * NB] for w in (WH, WL))
                        pe.matmul(DN[d % 2][:, :], HTH[:, k, 0:SLOTS], wh, start=k == 0, stop=False)
                        pe.matmul(DN[d % 2][:, :], HTH[:, k, 0:SLOTS], wl, start=False, stop=False)
                        ins = pe.matmul(DN[d % 2][:, :], HTL[:, k, 0:SLOTS], wh, start=False, stop=k == FC - 1)
                    ins.then_inc(used if j < DN_PIECES - 1 else dn_ready, 1)

                def gather(count, k, q):
                    pe.wait_ge(tp_free, count - 1)
                    for i in range(4):
                        c = 4 * q + i
                        for t in range(TILES):
                            ins = pe.matmul(TP[k % 2][:, i * P:(i + 1) * P], XN[:, t, c * P:(c + 1) * P],
                                            SEL[:, t, :], start=t == 0, stop=t == TILES - 1)
                    ins.then_inc(tp_ready, 1)

                def selection_transposed(count, k, t):
                    pe.wait_ge(tp_free, count - 1)
                    pe.transpose(TP[k % 2][:, 0:P], SEL[:, t, :], IDN[:, :]).then_inc(tp_ready, 1)

                def expert(e, more):
                    steps = expert_steps(more)[0]
                    t_at = {b: tp for kind, b, _, tp, _ in steps if kind == "t"}
                    gather_at = {q: tp for kind, q, _, tp, _ in steps if kind == "gather"}
                    for kind, b, j, tp, _ in steps:
                        count, k = e * TP_MORE + (s["tp"] + tp), s["tp"] + tp
                        if kind == "gu":
                            if b == GBLOCKS and j % 2 == 0:
                                pe.wait_ge(tp_free, e * TP_MORE + (s["tp"] + gather_at[j // 2] + 1))
                            gate_up(e, b, j)
                        elif kind == "t":
                            pe.wait_ge(gu_free, e * GBLOCKS + (s["gu"] + b + 3))
                            pe.wait_ge(tp_free, count - 1)
                            transposes(k, HM, range(*T_AFTER[b]))
                        elif kind == "gather":
                            if b == 0:
                                pe.wait_ge(sel_done, e + (N_EXP * n_pass + 2))
                            gather(count, k, b)
                        elif kind == "dn":
                            if b == 0 and j in (0, T_AFTER[-1][0] // 2):
                                pe.wait_ge(tp_free, e * TP_MORE + (s["tp"] + t_at[GBLOCKS - (2 if j == 0 else 1)] + 1))
                            down(e, b, j)
                        elif kind == "sc":
                            pe.wait_ge(dn_free, e * DBLOCKS + (s["dn"] + b + 3))
                            pe.wait_ge(tp_free, count - 1)
                            rows, bnk = SELT[:, j * P:(j + 1) * P], TP[k % 2][:, :]
                            pe.matmul(bnk, rows, YH[b % 2], start=True, stop=False)
                            pe.matmul(bnk, rows, YL[b % 2], start=False, stop=True).then_inc(tp_ready, 1)
                        else:
                            selection_transposed(count, k, b)

                pe.wait_ge(sel_done, N_EXP * n_pass + 1)
                for q in range(KD // 4):
                    gather(s["tp0"] + q, s["tp0"] + q, q)
                for j in range(GU_PIECES):
                    if j % 2 == 0:
                        pe.wait_ge(tp_free, s["tp0"] + j // 2 + 1)
                    gate_up(0, 0, j)
                for t in range(TILES):
                    selection_transposed(s["tp0"] + KD // 4 + t, s["tp0"] + KD // 4 + t, t)
                with pe.Fori(0, N_EXP - 1) as e:
                    expert(e, True)
                expert(N_EXP - 1, False)

            moe_pass(0)
            pe.wait_ge(flag_done, 1)
            with pe.If(pe.value_load(FLAG[0:1, 0:1], min_val=0, max_val=1) > 0):
                moe_pass(1)

        @block.scalar
        def _(act):
            n_link = [0]

            def link(ins):
                n_link[0] += 1
                ins.then_inc(act_chain, 1)
                act.wait_ge(act_chain, n_link[0])

            def high_ahead(i, width, piece, shift=0):
                act.wait_ge(raw_full[i % RAW], shift * (16 // RAW) + 16 * (piece // RAW + 1))
                act.activation(WH[:, i % RING, 0:width], RAWS[:, i % RAW, 0:width], ACT.Copy).then_inc(high_done, 1)

            n_square = [0]

            def squares(d, t):
                act.wait_ge(sq_done, n_square[0]) if n_square[0] else None
                n_square[0] += 1
                act.activation(JUNK, X[:, t, d * NB:(d + 1) * NB], ACT.Square,
                               accum_out=SSP[:, DBLOCKS * t + d:DBLOCKS * t + d + 1]).then_inc(sq_done, 1)

            def squares_added(d, dn):
                for t in range(TILES):
                    act.wait_ge(dn_free, 2 + dn + TILES * d + t + 1)
                    squares(d, t)

            def x_high(k, t, q):
                act.wait_ge(tp_ready, k + 1)
                act.activation(XTH[:, 4 * q:4 * q + 4, t * P:(t + 1) * P], TP[k % 2][:, :].rearrange("p (c n) -> p c n", c=4),
                               ACT.Copy).then_inc(tp_high, 1)

            def roots(which, n):
                act.wait_ge(ms_done, n + 1)
                act.activation(which, which, ACT.Sqrt).then_inc(root_done, 1)

            act.sem_inc(gu_free, 2)
            act.sem_inc(dn_free, 2)
            for t in range(TILES):
                act.wait_ge(x_in[t], 16)
                for d in range(DBLOCKS):
                    squares(d, t)
            roots(RSTD, 0)
            for layer in range(LAYERS):
                m, f = MIX[layer], FFN[layer]
                for k in range(8):
                    x_high(m["tp_x"] + k, k // 4, k % 4)
                    if layer == 0:
                        high_ahead(k, NB_W, k)
                if layer == 0:
                    act.wait_ge(rope_red, 1)
                    act.activation(SIN[:, :, :], RED, ACT.Sin).then_inc(tables_done, 1)
                    act.wait_ge(rope_red, 2)
                    act.activation(COS[:, :, :], TURN, ACT.Sin).then_inc(tables_done, 1)
                for c in range(IN_BLOCKS):
                    for t in range(TILES):
                        if t == TILES - 1:
                            for j in range(IN_PIECES - 1):
                                act.wait_ge(used, c * (IN_PIECES - 1) + m["used_in"] + j + 1)
                                high_ahead(j, NB_W, m["p_in"] + c * IN_PIECES + j + RING)
                        act.wait_ge(gu_ready, c * TILES + m["gu"] + t + 1)
                        act.activation(QKV[:, t, c * NB:(c + 1) * NB], G[t][:, :], ACT.Copy).then_inc(gu_free, 1)
                        if t == TILES - 1:
                            high_ahead(IN_PIECES - 1, NB_W, m["p_in"] + (c + 1) * IN_PIECES - 1 + RING)
                    if c in QK_BLOCKS:
                        n = QK_BLOCKS.index(c)
                        roots(HSSR[:, 8 * n:8 * n + 8], ROOTS * layer + 1 + n)
                act.wait_ge(sbg_done, layer + 1)

                def turned(h):
                    n, b = HEADS * layer + h, h % 2
                    act.wait_ge(qk_t, 2 * n + 1)
                    if h >= 2:
                        act.wait_ge(z_ready, n - 1)
                        act.wait_ge(s_ready, n - 1)
                    act.activation(QKT[0][b][:, 0:2 * P], TP[0][:, 0:2 * P], ACT.Copy, scale=SB_GAIN[:, 0:1])
                    act.activation(QKT[0][b][:, 2 * P:4 * P], TP[0][:, 2 * P:4 * P], ACT.Copy,
                                   scale=SB_GAIN[:, 1:2]).then_inc(qk_ev, 1)
                    act.wait_ge(qk_t, 2 * n + 2)
                    act.activation(QKT[1][b], TP[1][:, :], ACT.Copy).then_inc(qk_ev, 1)

                def scores(h):
                    n, b = HEADS * layer + h, h % 2
                    act.wait_ge(z_ready, n + 1)
                    if h >= 2:
                        act.wait_ge(az_done, n - 1)
                    act.activation(ZS[b], G[0][:, 0:3 * P], ACT.Copy)
                    act.activation(SPL[b], G[0][:, 0:3 * P], ACT.Abs).then_inc(z_copied, 1)
                    act.wait_ge(z_copied, n + 1)
                    link(act.activation(SPL[b], SPL[b], ACT.Exp, scale=-1.0))
                    act.activation(SPL[b], SPL[b], ACT.Ln, bias=1.0).then_inc(spl_done, 1)
                    act.wait_ge(s_max, n + 1)
                    act.activation(WD[b][:, 0:P], WD[b][:, 0:P], ACT.Exp, bias=NMX[:, 2 * b:2 * b + 1], scale=SCALE)
                    act.activation(WD[b][:, P:3 * P], WD[b][:, P:3 * P], ACT.Exp, bias=NMX[:, 2 * b + 1:2 * b + 2],
                                   scale=SCALE).then_inc(e_done, 1)

                def weights(h):
                    n, b = HEADS * layer + h, h % 2
                    act.wait_ge(az_done, n + 1)
                    act.activation(AZ[b], AZ[b], ACT.Exp).then_inc(a_done, 1)
                    act.wait_ge(wt_ready, n + 1)
                    if h >= 2:
                        act.wait_ge(odil_ready, n - 1)
                    act.activation(WDT[b], U[1][:, 0:3 * P], ACT.Copy).then_inc(wt_done, 1)

                def outputs(h):
                    n, b = HEADS * layer + h, h % 2
                    act.wait_ge(osb_ready, n + 1)
                    act.activation(QKV[:, :, h * DH:(h + 1) * DH], DN[0][:, 0:2 * P].rearrange("p (t d) -> p t d", t=TILES),
                                   ACT.Copy).then_inc(osb_done, 1)
                    act.wait_ge(odil_ready, n + 1)
                    for t in range(TILES):
                        ins = act.activation(QKV[:, t, 3 * HEADS * DH + h * DH:3 * HEADS * DH + (h + 1) * DH],
                                             DN[1][:, t * P:(t + 1) * P], ACT.Copy, scale=RDEN[:, 2 * b + t:2 * b + t + 1])
                    ins.then_inc(odil_done, 1)

                turned(0)
                scores(0)
                for h in range(HEADS):
                    if h + 1 < HEADS:
                        turned(h + 1)
                    weights(h)
                    if h + 1 < HEADS:
                        scores(h + 1)
                    outputs(h)
                act.wait_ge(odil_done, HEADS * (layer + 1))
                act.wait_ge(osb_done, HEADS * (layer + 1))
                for t in range(TILES):
                    for kind in range(2):
                        act.activation(ATT[:, heads_at:heads_at + HEADS * DH], QKV[:, t, 3 * HEADS * DH * kind:3 * HEADS * DH * kind + HEADS * DH],
                                       ACT.Square, accum_out=O_SS[:, 2 * t + kind:2 * t + kind + 1]).then_inc(osq_done, 1)
                        act.wait_ge(osq_done, 2 * TILES * layer + 2 * t + kind + 1)
                roots(O_RSTD, ROOTS * layer + 5)
                for t in range(TILES):
                    for kind in range(2):
                        k = m["tp_o"] + 2 * t + kind
                        act.wait_ge(tp_ready, k + 1)
                        act.activation(HTH[:, HEADS * kind:HEADS * (kind + 1), t * P:(t + 1) * P],
                                       TP[k % 2][:, :].rearrange("p (c n) -> p c n", c=4), ACT.Copy).then_inc(tp_high, 1)
                for d in range(OUT_BLOCKS):
                    for j in range(OUT_PIECES):
                        i = d * OUT_PIECES + j
                        if j < OUT_PIECES - 1:
                            act.wait_ge(used, m["used_out"] + d * (OUT_PIECES - 1) + j + 1)
                        else:
                            act.wait_ge(dn_ready, m["dn"] + TILES * (d + 1))
                        high_ahead(i, NB_W if i + RING < OUT_BLOCKS * OUT_PIECES else GU_W, m["p_out"] + i + RING)
                        if j == 0 and d:
                            squares_added(d - 1, m["dn"])
                squares_added(OUT_BLOCKS - 1, m["dn"])
                roots(RSTD, ROOTS * layer + 6)
                for k in range(8):
                    x_high(f["tp_x"] + k, k // 4, k % 4)
                if layer == 1:
                    act.wait_ge(router_in, 16)
                    act.activation(WRH[:, :, :], GAIN[:, 0:KD * N_EXP].rearrange("p (k e) -> p k e", k=KD), ACT.Copy).then_inc(wr_high, 1)
                if layer == 1:
                    act.wait_ge(lg_done, 2)
                    for t in range(TILES):
                        ins = act.activation(R1[:, 0, t, :], R1[:, 1, t, :], ACT.Exp)
                    ins.then_inc(pexp_done, 1)

                def ffn_slice(e, last=False):
                    dn = f["dn"] + (DENSE_SLICES - 1) * DBLOCKS * TILES
                    def ahead(i, semaphore, count):
                        act.wait_ge(semaphore, count)
                        high_ahead(i, WIDTHS[(i + RING) % SLICE_PIECES], f["piece"] + i + RING, e * SLICE_PIECES)

                    def gate_up(b, t):
                        if t == TILES - 1:
                            for j in range(GU_PIECES - 1):
                                ahead(b * GU_PIECES + j, used, e * SLICE_USED + (f["used"] + b * (GU_PIECES - 1) + j + 1))
                        act.wait_ge(gu_ready, e * (GBLOCKS * TILES) + (f["gu"] + b * TILES + t + 1))
                        act.activation(SG[:, t, :], G[t][:, 0:GB], ACT.Silu).then_inc(silu_done, 1)
                        if t == TILES - 1:
                            ahead(b * GU_PIECES + GU_PIECES - 1, gu_ready,
                                  e * (GBLOCKS * TILES) + (f["gu"] + b * TILES + t + 1))

                    def h_high(b, t):
                        k = b * TILES + t
                        c0, c1 = T_AFTER[b]
                        act.wait_ge(tp_ready, e * (GBLOCKS * TILES) + (f["tp"] + k + 1))
                        act.activation(HTH[:, c0:c1, t * P:(t + 1) * P],
                                       TP[(f["tp"] + k) % 2][:, 0:(c1 - c0) * P].rearrange("p (c n) -> p c n", n=P),
                                       ACT.Copy).then_inc(tp_high, 1)

                    for b in range(GBLOCKS):
                        gate_up(b, 0)
                        if b:
                            h_high(b - 1, 1)
                        gate_up(b, 1)
                        h_high(b, 0)
                    h_high(GBLOCKS - 1, 1)
                    for d in range(DBLOCKS):
                        for j in range(DN_PIECES - 1):
                            ahead(GBLOCKS * GU_PIECES + d * DN_PIECES + j, used,
                                  e * SLICE_USED + (f["used"] + GBLOCKS * (GU_PIECES - 1) + d * (DN_PIECES - 1) + j + 1))
                            if last and j == 0 and d:
                                squares_added(d - 1, dn)
                        ahead(GBLOCKS * GU_PIECES + (d + 1) * DN_PIECES - 1, dn_ready,
                              e * (DBLOCKS * TILES) + (f["dn"] + TILES * (d + 1)))
                    if last:
                        squares_added(DBLOCKS - 1, dn)

                if layer == 0:
                    with act.Fori(0, DENSE_SLICES - 1) as e:
                        ffn_slice(e)
                    ffn_slice(DENSE_SLICES - 1, last=True)
                    roots(RSTD, ROOTS)

            def moe_pass(n_pass):
                s = PASS[n_pass]

                def ahead(e, i, more):
                    if i < 0 or i + RING >= SLICE_PIECES and not more:
                        return
                    gu_pieces = GBLOCKS * GU_PIECES
                    if i < gu_pieces or i >= SLICE_PIECES:
                        b, j = (i // GU_PIECES, i % GU_PIECES) if i < gu_pieces else (GBLOCKS, i - SLICE_PIECES)
                        if j < GU_PIECES - 1:
                            act.wait_ge(used, e * SLICE_USED + (used_at(s["used"], b) + j + 1))
                        else:
                            act.wait_ge(gu_ready, e * GBLOCKS + (s["gu"] + b + 1))
                    else:
                        d, j = (i - gu_pieces) // DN_PIECES, (i - gu_pieces) % DN_PIECES
                        if j < DN_PIECES - 1:
                            act.wait_ge(used, e * SLICE_USED
                                        + (s["used"] + GBLOCKS * (GU_PIECES - 1) + d * (DN_PIECES - 1) + j + 1))
                        else:
                            act.wait_ge(dn_ready, e * DBLOCKS + (s["dn"] + d + 1))
                    high_ahead(i, WIDTHS[(i + RING) % SLICE_PIECES], s["piece"] + i + RING, e * SLICE_PIECES)

                def gate_up(e, b, j, more=True):
                    if j == GU_PIECES - 1:
                        act.wait_ge(gu_ready, e * GBLOCKS + (s["gu"] + b + 1))
                        act.activation(SG[:, b % 2, :], G[b % 2][:, 0:GB], ACT.Silu).then_inc(silu_done, 1)
                    ahead(e, piece_at(0, b) + j - LATER, more)

                def down(e, d, j, more):
                    if j == DN_PIECES - 1:
                        act.wait_ge(dn_ready, e * DBLOCKS + (s["dn"] + d + 1))
                        act.activation(YH[d % 2], DN[d % 2][:, :].rearrange("p (c n) -> p c n", n=P), ACT.Copy).then_inc(y_high, 1)
                    ahead(e, GBLOCKS * GU_PIECES + d * DN_PIECES + j - LATER, more)

                def gathered_high(count, k, q):
                    act.wait_ge(tp_ready, count + 1)
                    act.activation(XTH[:, 4 * q:4 * q + 4, 0:SLOTS], TP[k % 2][:, :].rearrange("p (c n) -> p c n", c=4),
                                   ACT.Copy).then_inc(tp_high, 1)

                def expert(e, more):
                    for kind, b, j, tp, _ in expert_steps(more)[0]:
                        count, k = e * TP_MORE + (s["tp"] + tp), s["tp"] + tp
                        if kind == "gu":
                            gate_up(e, b, j, more)
                        elif kind == "dn":
                            down(e, b, j, more)
                        elif kind == "t":
                            c0, c1 = T_AFTER[b]
                            act.wait_ge(tp_ready, count + 1)
                            act.activation(HTH[:, c0:c1, 0:SLOTS], TP[k % 2][:, 0:(c1 - c0) * P].rearrange("p (c n) -> p c n", n=P),
                                           ACT.Copy).then_inc(tp_high, 1)
                        elif kind == "gather":
                            gathered_high(count, k, b)

                if n_pass:
                    for i in range(RING):
                        high_ahead(i, WIDTHS[i], s["piece"] + i)
                for q in range(KD // 4):
                    gathered_high(s["tp0"] + q, s["tp0"] + q, q)
                for j in range(GU_PIECES):
                    gate_up(0, 0, j)
                with act.Fori(0, N_EXP - 1) as e:
                    expert(e, True)
                expert(N_EXP - 1, False)

            moe_pass(0)
            act.wait_ge(flag_done, 1)
            with act.If(act.value_load(FLAG[0:1, 0:1], min_val=0, max_val=1) > 0):
                moe_pass(1)

        @block.vector
        def _(dve):
            n_link = [0]

            def link(ins):
                n_link[0] += 1
                ins.then_inc(dve_chain, 1)
                dve.wait_ge(dve_chain, n_link[0])

            def low(i, width, piece, shift=None):
                dve.wait_ge(high_done, piece + 1 if shift is None else shift + (piece + 1))
                dve.tensor_tensor(WL[:, i % RING, 0:width], RAWS[:, i % RAW, 0:width], WH[:, i % RING, 0:width],
                                  ALU.subtract).then_inc(low_done, 1)

            def inverse_roots(dst, sums, count, n):
                dve.tensor_scalar(dst, sums, 1.0 / count, EPS, ALU.mult, ALU.add).then_inc(ms_done, 1)
                dve.wait_ge(root_done, n + 1)
                link(dve.reciprocal(dst, dst))

            def normalise(norm):
                dve.wait_ge(sq_done, X_BLOCKS * (norm + 1))
                link(dve.tensor_reduce(SS, SSP[:, :].rearrange("p (t d) -> p t d", t=TILES), AX.X, ALU.add))
                inverse_roots(RSTD, SS, D, ROOTS * (norm // 2) + (ROOTS - 1) * (norm % 2))
                dve.wait_ge(xg_done, X_BLOCKS * (norm + 1))

            def times_gain(d, t):
                cols = slice(d * NB, (d + 1) * NB)
                dve.tensor_tensor(XN[:, t, cols], X[:, t, cols], GAIN[:, cols], ALU.mult).then_inc(xg_done, 1)

            def scaled(k):
                t, q = k // 4, k % 4
                v = XN[:, t, q * NB:(q + 1) * NB]
                dve.tensor_scalar(v, v, RSTD[:, t:t + 1], None, ALU.mult).then_inc(xn_done, 1)

            def x_turned(tp, first_pieces):
                scaled(0)
                scaled(1)
                for k in range(X_BLOCKS):
                    if k + 2 < X_BLOCKS:
                        scaled(k + 2)
                    x_low(tp + k, k // 4, k % 4)
                    if first_pieces:
                        low(k, NB_W, k)

            def x_low(k, t, q):
                dve.wait_ge(tp_high, k + 1)
                dst = (slice(None), slice(4 * q, 4 * q + 4), slice(t * P, (t + 1) * P))
                dve.tensor_tensor(XTL[dst], TP[k % 2][:, :].rearrange("p (c n) -> p c n", c=4), XTH[dst],
                                  ALU.subtract).then_inc(tp_free, 1)

            dve.wait_ge(gain_in, 16)
            for t in range(TILES):
                dve.wait_ge(x_in[t], 16)
                for d in range(DBLOCKS):
                    times_gain(d, t)
            normalise(0)
            x_turned(MIX[0]["tp_x"], True)
            dve.wait_ge(small_in, 32)
            link(dve.tensor_copy(POS, POS_I))
            for t in range(TILES):
                link(dve.tensor_scalar(ANG[:, t, :], INV, POS[:, t:t + 1], None, ALU.mult))
            link(dve.tensor_scalar(TURN, ANG, 1.0 / (2.0 * np.pi), ROUND, ALU.mult, ALU.add))
            link(dve.tensor_scalar(TURN, TURN, -ROUND, None, ALU.add))
            link(dve.scalar_tensor_tensor(out=RED, in0=TURN, scalar=-TWO_PI_PARTS[0], in1=ANG, op0=ALU.mult, op1=ALU.add))
            link(dve.scalar_tensor_tensor(out=RED, in0=TURN, scalar=-TWO_PI_PARTS[1], in1=RED, op0=ALU.mult, op1=ALU.add))
            link(dve.scalar_tensor_tensor(out=RED, in0=TURN, scalar=-TWO_PI_PARTS[2], in1=RED, op0=ALU.mult, op1=ALU.add))
            link(dve.tensor_scalar(RED, RED, 3.1415925, -3.1415925, ALU.min, ALU.max))
            link(dve.scalar_tensor_tensor(out=TURN, in0=RED, scalar=-1.0, in1=RED, op0=ALU.mult, op1=ALU.max))
            dve.sem_inc(rope_red, 1)
            dve.tensor_scalar(TURN, TURN, -1.0, np.pi / 2, ALU.mult, ALU.add).then_inc(rope_red, 1)
            dve.wait_ge(const_done, 1)
            link(dve.tensor_copy(IOTA[:, :], IOTA_I))
            link(dve.tensor_copy(DF, DIST))
            link(dve.tensor_scalar(CNT[:, :], DF, 128.5, None, ALU.is_lt))
            for dil in (4, 16):
                link(dve.tensor_scalar(DMOD, DIST, dil - 1, None, ALU.bitwise_and))
                link(dve.tensor_scalar(C1, DMOD, 0, None, ALU.is_equal))
                link(dve.tensor_tensor(CNT[:, :], CNT[:, :], C1, ALU.add))
            link(dve.scalar_tensor_tensor(out=CNT[:, :], in0=DF, scalar=-0.5, in1=CNT[:, :], op0=ALU.is_gt, op1=ALU.mult))
            dve.tensor_scalar(NEGU[:, :], CNT[:, :], 0.5, -BIG, ALU.is_lt, ALU.mult).then_inc(masks_done, 1)
            dve.wait_ge(masks_done, 1)
            dve.wait_ge(tables_done, 2)

            for layer in range(LAYERS):
                m, f = MIX[layer], FFN[layer]
                if layer:
                    x_turned(m["tp_x"], False)
                dve.wait_ge(dilg_in, 32 * (layer + 1))
                for qk in range(2):
                    for t in range(TILES):
                        lo, hi = slice(0, DH // 2), slice(DH // 2, DH)
                        g = DIL_G[:, qk, :]
                        dve.tensor_tensor(ROPE_C[:, t, qk, lo], g[:, lo], COS[:, t, :], ALU.mult)
                        dve.tensor_tensor(ROPE_C[:, t, qk, hi], g[:, hi], COS[:, t, :], ALU.mult)
                        dve.scalar_tensor_tensor(out=ROPE_S[:, t, qk, lo], in0=g[:, hi], scalar=-1.0, in1=SIN[:, t, :],
                                                 op0=ALU.mult, op1=ALU.mult)
                        link(dve.tensor_tensor(ROPE_S[:, t, qk, hi], g[:, lo], SIN[:, t, :], ALU.mult))
                dve.wait_ge(sbg_in, 32 * (layer + 1))
                dve.tensor_scalar(SB_GAIN[:, 0:1], SB_GAIN[:, 0:1], SCALE, None, ALU.mult).then_inc(sbg_done, 1)

                def heads_normalised(c):
                    n = QK_BLOCKS.index(c)
                    sums, rs = HSS[:, 8 * n:8 * n + 8], HSSR[:, 8 * n:8 * n + 8]
                    cols = QKV[:, :, c * NB:(c + 1) * NB]
                    dve.wait_ge(gu_free, 2 + m["gu"] + (c + 1) * TILES)
                    link(dve.tensor_tensor(SQ, cols, cols, ALU.mult))
                    link(dve.tensor_reduce(sums, SQ.rearrange("p t (h d) -> p (t h) d", d=DH), AX.X, ALU.add))
                    inverse_roots(rs, sums, DH, ROOTS * layer + 1 + n)
                    for t in range(TILES):
                        v = QKV[:, t, c * NB:(c + 1) * NB].rearrange("p (h d) -> p h d", d=DH)
                        link(dve.tensor_tensor(v, v, rs[:, HEADS * t:HEADS * (t + 1)].unsqueeze(2).to_broadcast([P, HEADS, DH]),
                                               ALU.mult))
                        if c < IN_BLOCKS // 2:
                            continue
                        qk = c - IN_BLOCKS // 2
                        t1 = RT1.rearrange("p (h d) -> p h d", d=DH)
                        t2 = RT2.rearrange("p (h d) -> p h d", d=DH)
                        half = DH // 2
                        bc = [P, HEADS, half]
                        dve.tensor_tensor(t1, v, ROPE_C[:, t, qk, :].unsqueeze(1).to_broadcast([P, HEADS, DH]), ALU.mult)
                        dve.tensor_tensor(t2[:, :, 0:half], v[:, :, half:DH],
                                          ROPE_S[:, t, qk, 0:half].unsqueeze(1).to_broadcast(bc), ALU.mult)
                        link(dve.tensor_tensor(t2[:, :, half:DH], v[:, :, 0:half],
                                               ROPE_S[:, t, qk, half:DH].unsqueeze(1).to_broadcast(bc), ALU.mult))
                        link(dve.tensor_tensor(v, t1, t2, ALU.add))

                for c in range(IN_BLOCKS):
                    for j in range(IN_PIECES):
                        low(j, NB_W, m["p_in"] + c * IN_PIECES + j + RING)
                    if c in QK_BLOCKS:
                        heads_normalised(c)
                dve.sem_inc(rope_done, 1)

                def scores(h):
                    n, b = HEADS * layer + h, h % 2
                    dve.wait_ge(s_ready, n + 1)
                    link(dve.tensor_tensor(WD[b], U[0][:, 0:3 * P], NEGU[:, :], ALU.add))
                    dve.tensor_reduce(MX[:, 2 * b:2 * b + 1], WD[b][:, 0:P], AX.X, ALU.max)
                    link(dve.tensor_reduce(MX[:, 2 * b + 1:2 * b + 2], WD[b][:, P:3 * P], AX.X, ALU.max))
                    dve.tensor_scalar(NMX[:, 2 * b:2 * b + 2], MX[:, 2 * b:2 * b + 2], -SCALE, None, ALU.mult).then_inc(s_max, 1)
                    dve.wait_ge(spl_done, n + 1)
                    link(dve.scalar_tensor_tensor(out=SP[b], in0=ZS[b], scalar=0.0, in1=SPL[b], op0=ALU.max, op1=ALU.add))
                    link(dve.tensor_scalar(AZ[b], ZS[b], EXP_OVERFLOW, BIG, ALU.is_gt, ALU.mult))
                    link(dve.tensor_tensor(SP[b], SP[b], AZ[b], ALU.add))
                    dve.tensor_tensor(SP[b][:, 0:P], SP[b][:, 0:P], KEEPZ[:, :], ALU.mult)
                    dve.tensor_tensor(SP[b][:, 2 * P:3 * P], SP[b][:, 2 * P:3 * P], KEEPZ[:, :], ALU.mult).then_inc(sp_done, 1)
                    dve.wait_ge(e_done, n + 1)
                    dve.tensor_tensor(WD[b][:, 0:3 * P], WD[b][:, 0:3 * P], CNT[:, :], ALU.mult).then_inc(w_done, 1)
                    dve.wait_ge(w_done, n + 1)
                    dve.tensor_reduce(DEN[:, 2 * b:2 * b + 1], WD[b][:, 0:P], AX.X, ALU.add)
                    link(dve.tensor_reduce(DEN[:, 2 * b + 1:2 * b + 2], WD[b][:, P:3 * P], AX.X, ALU.add))
                    link(dve.reciprocal(RDEN[:, 2 * b:2 * b + 2], DEN[:, 2 * b:2 * b + 2]))

                def weights(h):
                    n, b = HEADS * layer + h, h % 2
                    dve.wait_ge(r_ready, n + 1)
                    link(dve.tensor_tensor(AZ[b], ZS[b], G[1][:, 0:3 * P], ALU.subtract))
                    dve.tensor_tensor(AZ[b][:, 0:P], AZ[b][:, 0:P], NEGZ[:, :], ALU.add)
                    dve.tensor_tensor(AZ[b][:, 2 * P:3 * P], AZ[b][:, 2 * P:3 * P], NEGZ[:, :], ALU.add).then_inc(az_done, 1)

                scores(0)
                for h in range(HEADS):
                    weights(h)
                    if h + 1 < HEADS:
                        scores(h + 1)
                dve.wait_ge(osq_done, 2 * TILES * (layer + 1))
                dve.wait_ge(gout_in, 32 * (layer + 1))
                inverse_roots(O_RSTD, O_SS, HEADS * DH, ROOTS * layer + 5)
                for t in range(TILES):
                    for kind in range(2):
                        o = QKV[:, t, 3 * HEADS * DH * kind:3 * HEADS * DH * kind + HEADS * DH]
                        dve.scalar_tensor_tensor(out=o, in0=o, scalar=O_RSTD[:, 2 * t + kind:2 * t + kind + 1],
                                                 in1=GOUT[:, kind * HEADS * DH:(kind + 1) * HEADS * DH],
                                                 op0=ALU.mult, op1=ALU.mult).then_inc(on_done, 1)
                for t in range(TILES):
                    for kind in range(2):
                        k = m["tp_o"] + 2 * t + kind
                        dve.wait_ge(tp_high, k + 1)
                        dst = (slice(None), slice(HEADS * kind, HEADS * (kind + 1)), slice(t * P, (t + 1) * P))
                        dve.tensor_tensor(HTL[dst], TP[k % 2][:, :].rearrange("p (c n) -> p c n", c=4), HTH[dst],
                                          ALU.subtract).then_inc(tp_free, 1)

                def add_down(d, t, k, complete):
                    dve.wait_ge(dn_ready, k + 1)
                    xs = X[:, t, d * NB:(d + 1) * NB]
                    dve.tensor_tensor(xs, DN[t][:, :], xs, ALU.add).then_inc(dn_free, 1)
                    if complete:
                        dve.wait_ge(dn_free, 2 + k + 1)
                        times_gain(d, t)

                dve.wait_ge(gain_in, 16 * (2 * layer + 2))
                for d in range(OUT_BLOCKS):
                    add_down(d, 0, m["dn"] + TILES * d, True)
                    for j in range(OUT_PIECES):
                        i = d * OUT_PIECES + j
                        low(i, NB_W if i + RING < OUT_BLOCKS * OUT_PIECES else GU_W, m["p_out"] + i + RING)
                    add_down(d, 1, m["dn"] + TILES * d + 1, True)
                normalise(2 * layer + 1)
                x_turned(f["tp_x"], False)
                if layer == 1:
                    dve.wait_ge(wr_high, 1)
                    dve.tensor_tensor(WRL[:, :, :], GAIN[:, 0:KD * N_EXP].rearrange("p (k e) -> p k e", k=KD), WRH[:, :, :],
                                      ALU.subtract).then_inc(wr_done, 1)
                if layer == 1:
                    dve.wait_ge(lgt_ready, 1)
                    dve.tensor_copy(LGT, DN[0][0:N_EXP, 0:SEQ]).then_inc(lgt_done, 1)
                    dve.wait_ge(lg_ready, 1)
                    dve.tensor_copy(LG[:, :, :], DN[1][:, 0:TILES * N_EXP].rearrange("p (t e) -> p t e", t=TILES)).then_inc(lg_done, 1)
                    dve.wait_ge(lg_done, 1)
                    sel, rank = R1[:, 3, :, :], R1[:, 2, :, :]
                    link(dve.tensor_reduce(MX[:, 0:TILES], LG[:, :, :], AX.X, ALU.max))
                    for t in range(TILES):
                        ins = dve.tensor_scalar(R1[:, 1, t, :], LG[:, t, :], MX[:, t:t + 1], None, ALU.subtract)
                    ins.then_inc(lg_done, 1)
                    for t in range(TILES):
                        mine = LG[:, t, :].unsqueeze(2).to_broadcast([P, N_EXP, N_EXP])
                        other = LG[:, t, :].unsqueeze(1).to_broadcast([P, N_EXP, N_EXP])
                        dve.tensor_tensor(RK[:, 0], mine, other, ALU.is_lt)
                        link(dve.tensor_tensor(RK[:, 1], mine, other, ALU.is_equal))
                        link(dve.tensor_tensor(RK[:, 1], RK[:, 1], BEFORE[:, :, :], ALU.mult))
                        link(dve.tensor_tensor(RK[:, 0], RK[:, 0], RK[:, 1], ALU.add))
                        link(dve.tensor_reduce(rank[:, t, :], RK[:, 0], AX.X, ALU.add))
                    dve.tensor_scalar(CHOSEN[:, :, :], rank, 1.5, None, ALU.is_lt).then_inc(chosen_done, 1)
                    dve.wait_ge(chosen_done, 1)
                    dve.wait_ge(pexp_done, 1)
                    link(dve.tensor_tensor(sel, CHOSEN[:, :, :], R1[:, 0, :, :], ALU.mult))
                    link(dve.tensor_reduce(MX[:, 0:TILES], sel, AX.X, ALU.add))
                    link(dve.reciprocal(MX[:, 0:TILES], MX[:, 0:TILES]))
                    for t in range(TILES):
                        link(dve.tensor_scalar(COMB[:, t, :], sel[:, t, :], MX[:, t:t + 1], None, ALU.mult))
                    dve.wait_ge(pos_ready, 1)
                    pos = DN[1][:, 0:TILES * N_EXP].rearrange("p (t e) -> p t e", t=TILES)
                    link(dve.scalar_tensor_tensor(out=SLOT[:, :, :], in0=pos, scalar=1.0, in1=CHOSEN[:, :, :],
                                                  op0=ALU.add, op1=ALU.mult))
                    link(dve.tensor_scalar(SLOT[:, :, :], SLOT[:, :, :], -1.0, None, ALU.add))
                    link(dve.tensor_reduce(MX[:, 0:1], DN[1][:, 2 * N_EXP:3 * N_EXP], AX.X, ALU.max))
                    dve.sem_inc(slot_done, 1)
                    dve.tensor_scalar(FLAG[:, :], MX[:, 0:1], SLOTS + 0.5, None, ALU.is_gt).then_inc(flag_done, 1)

                def ffn_slice(e, last=False):
                    if last:
                        dve.wait_ge(gain_in, 16 * 3)
                    def ahead(i):
                        low(i, WIDTHS[(i + RING) % SLICE_PIECES], f["piece"] + i + RING, e * SLICE_PIECES)

                    def gate_up(b, t):
                        if t == TILES - 1:
                            for j in range(GU_PIECES - 1):
                                ahead(b * GU_PIECES + j)
                        dve.wait_ge(silu_done, e * (GBLOCKS * TILES) + (b * TILES + t + 1))
                        dve.tensor_tensor(H[:, t, b * GB:(b + 1) * GB], U[t][:, 0:GB], SG[:, t, :], ALU.mult).then_inc(gu_free, 1)
                        if t == TILES - 1:
                            ahead(b * GU_PIECES + GU_PIECES - 1)

                    def h_low(b, t):
                        k = b * TILES + t
                        c0, c1 = T_AFTER[b]
                        dve.wait_ge(tp_high, e * (GBLOCKS * TILES) + (f["tp"] + k + 1))
                        dst = (slice(None), slice(c0, c1), slice(t * P, (t + 1) * P))
                        dve.tensor_tensor(HTL[dst], TP[(f["tp"] + k) % 2][:, 0:(c1 - c0) * P].rearrange("p (c n) -> p c n", n=P),
                                          HTH[dst], ALU.subtract).then_inc(tp_free, 1)

                    for b in range(GBLOCKS):
                        gate_up(b, 0)
                        if b:
                            h_low(b - 1, 1)
                        gate_up(b, 1)
                        h_low(b, 0)
                    for d in range(DBLOCKS):
                        for t in range(TILES):
                            if d == 0 and t == 0:
                                h_low(GBLOCKS - 1, 1)
                            if t == TILES - 1:
                                for j in range(DN_PIECES):
                                    ahead(GBLOCKS * GU_PIECES + d * DN_PIECES + j)
                            add_down(d, t, e * (DBLOCKS * TILES) + (f["dn"] + d * TILES + t), last)

                if layer == 0:
                    with dve.Fori(0, DENSE_SLICES - 1) as e:
                        ffn_slice(e)
                    ffn_slice(DENSE_SLICES - 1, last=True)
                    normalise(2)

            def moe_pass(n_pass):
                s = PASS[n_pass]

                def ahead(e, i, more):
                    if i >= 0 and (i + RING < SLICE_PIECES or more):
                        low(i, WIDTHS[(i + RING) % SLICE_PIECES], s["piece"] + i + RING, e * SLICE_PIECES)

                def gate_up(e, b, j, more=True):
                    c = b % GBLOCKS
                    if j == GU_PIECES - 1:
                        dve.wait_ge(silu_done, e * GBLOCKS + (s["silu"] + b + 1))
                        dve.tensor_tensor(HM[:, c * GB:(c + 1) * GB], U[b % 2][:, 0:GB], SG[:, b % 2, :], ALU.mult).then_inc(gu_free, 1)
                    ahead(e, piece_at(0, b) + j - LATER, more)

                def down(e, d, j, more):
                    if j == DN_PIECES - 1:
                        dve.wait_ge(y_high, e * DBLOCKS + (N_EXP * DBLOCKS * n_pass + d + 1))
                        dve.tensor_tensor(YL[d % 2], DN[d % 2][:, :].rearrange("p (c n) -> p c n", n=P), YH[d % 2],
                                          ALU.subtract).then_inc(dn_free, 1)
                    ahead(e, GBLOCKS * GU_PIECES + d * DN_PIECES + j - LATER, more)

                def select(expert_index):
                    for t in range(TILES):
                        ins = dve.tensor_scalar(SEL[:, t, :], IOTA[:, :], SLOT[:, t, expert_index], None, ALU.is_equal)
                    ins.then_inc(sel_done, 1)

                def gathered_low(high, k, q):
                    dve.wait_ge(tp_high, high + 1)
                    dst = (slice(None), slice(4 * q, 4 * q + 4), slice(0, SLOTS))
                    dve.tensor_tensor(XTL[dst], TP[k % 2][:, :].rearrange("p (c n) -> p c n", c=4), XTH[dst],
                                      ALU.subtract).then_inc(tp_free, 1)

                def selection_transposed(count, k, t):
                    dve.wait_ge(tp_ready, count + 1)
                    dve.tensor_copy(SELT[:, t * P:(t + 1) * P], TP[k % 2][:, 0:P]).then_inc(tp_free, 1)

                def expert(e, more):
                    if more:
                        select(bass.ds(e + 1, 1))
                    for kind, b, j, tp, high in expert_steps(more)[0]:
                        count, k = e * TP_MORE + (s["tp"] + tp), s["tp"] + tp
                        high_count = e * HIGH_MORE + (s["high"] + high)
                        if kind == "gu":
                            gate_up(e, b, j, more)
                        elif kind == "dn":
                            down(e, b, j, more)
                        elif kind == "t":
                            c0, c1 = T_AFTER[b]
                            dve.wait_ge(tp_high, high_count + 1)
                            dst = (slice(None), slice(c0, c1), slice(0, SLOTS))
                            dve.tensor_tensor(HTL[dst], TP[k % 2][:, 0:(c1 - c0) * P].rearrange("p (c n) -> p c n", n=P),
                                              HTH[dst], ALU.subtract).then_inc(tp_free, 1)
                        elif kind == "gather":
                            gathered_low(high_count, k, b)
                        elif kind == "sc":
                            dve.wait_ge(tp_ready, count + 1)
                            gate = COMB[:, j, bass.ds(e, 1)] if more else COMB[:, j, e:e + 1]
                            xs = X[:, j, b * NB:(b + 1) * NB]
                            dve.scalar_tensor_tensor(out=xs, in0=TP[k % 2][:, :], scalar=gate, in1=xs,
                                                     op0=ALU.mult, op1=ALU.add).then_inc(tp_free, 1)
                        else:
                            selection_transposed(count, k, b)

                if n_pass:
                    link(dve.tensor_scalar(SLOT[:, :, :], SLOT[:, :, :], -float(SLOTS), None, ALU.add))
                select(slice(0, 1))
                if n_pass:
                    for i in range(RING):
                        low(i, WIDTHS[i], s["piece"] + i)
                for q in range(KD // 4):
                    gathered_low(s["high0"] + q, s["tp0"] + q, q)
                for j in range(GU_PIECES):
                    gate_up(0, 0, j)
                for t in range(TILES):
                    selection_transposed(s["tp0"] + KD // 4 + t, s["tp0"] + KD // 4 + t, t)
                with dve.Fori(0, N_EXP - 1) as e:
                    expert(e, True)
                expert(N_EXP - 1, False)

            moe_pass(0)
            dve.wait_ge(flag_done, 1)
            with dve.If(dve.value_load(FLAG[0:1, 0:1], min_val=0, max_val=1) > 0):
                moe_pass(1)


def pieces_by_column_block(w, width):
    *lead, k, n = w.shape
    w = w.reshape(*lead, k // (2 * P), 2, P, n // width, width)
    a = len(lead)
    w = w.transpose(*range(a), a + 3, a, a + 2, a + 1, a + 4)
    return np.ascontiguousarray(w.reshape(*lead, n // width, k // (2 * P), P, 2 * width))


def gate_up_pieces(gate, up):
    s = gate.shape[0]
    w = np.stack([gate, up], 1).reshape(s, 2, KD // 2, 2, P, GBLOCKS, GB)
    return np.ascontiguousarray(w.transpose(0, 5, 2, 4, 3, 1, 6).reshape(s, GBLOCKS, KD // 2, P, GU_W))


def down_pieces(down):
    s = down.shape[0]
    w = down.reshape(s, FC, P, DBLOCKS, NB).transpose(0, 3, 2, 1, 4)
    return np.ascontiguousarray(w.reshape(s, DBLOCKS, P, FC * NB))


def kernel(**inputs):
    import concourse.bacc as _bacc
    from concourse.bass_utils import run_bass_kernel_spmd as _run

    a = {k: np.asarray(v) for k, v in inputs.items()}
    by_slice = lambda w: w[0].reshape(D, DENSE_SLICES, FE).transpose(1, 0, 2)
    laid = {
        "x": a["x"][0],
        "positions": a["positions"].reshape(TILES, P).T,
        "norm_mix": a["norm_mix"],
        "w_in": pieces_by_column_block(a["w_in"], NB),
        "q_norm_sb": a["q_norm_sb"], "k_norm_sb": a["k_norm_sb"],
        "q_norm_dil": a["q_norm_dil"], "k_norm_dil": a["k_norm_dil"],
        "out_norm_sb": a["out_norm_sb"], "out_norm_dil": a["out_norm_dil"],
        "w_out": pieces_by_column_block(a["w_out"], NB),
        "norm_ffn": a["norm_ffn"],
        "gu_dense": gate_up_pieces(by_slice(a["w_gate_dense"]), by_slice(a["w_up_dense"])),
        "down_dense": down_pieces(a["w_down_dense"][0].reshape(DENSE_SLICES, FE, D)),
        "w_router": a["w_router"][0].reshape(KD, P, N_EXP).transpose(1, 0, 2).reshape(P, KD * N_EXP),
        "gu_moe": gate_up_pieces(a["w_gate_moe"][0], a["w_up_moe"][0]),
        "down_moe": down_pieces(a["w_down_moe"][0]),
        "inv_freq": (ROPE_THETA ** (-np.arange(0, DH, 2, dtype=np.float32) / np.float32(DH))).astype(np.float32),
    }
    nc = _bacc.Bacc("TRN2", target_bir_lowering=False, num_devices=1, dynamic_dma_scratch_size=4096)
    arrays, args = {}, {}
    for name, v in laid.items():
        v = np.ascontiguousarray(v)
        arrays[f"in_{name}"] = v
        args[name] = nc.dram_tensor(f"in_{name}", v.shape, mybir.dt.from_np(v.dtype), kind="ExternalInput").ap()
    args["out"] = nc.dram_tensor("out_x", (SEQ, D), F32, kind="ExternalOutput").ap()
    trunk(nc, **args)
    r = _run(nc, [arrays], core_ids=[0])
    return r.results[0]["out_x"].reshape(1, SEQ, D)
```
